# Optimizing a Trainium2 kernel written in Bass

```python
import math
import jax, jax.numpy as jnp
from jax import lax
import numpy as np

D_MODEL = 1024
BATCH = 1
SEQ = 256
DEPTH = 2

ATT_HEADS = 8
ATT_HEAD_DIM = 64
ATT_W = ATT_HEADS * ATT_HEAD_DIM
Q_BLOCK = 128
SSM_GROUP = 16
SSM_GROUPS = 16
SSM_W = SSM_GROUP * SSM_GROUPS
SSM_STATE = 64
DT_MIN = 1e-3
DT_MAX = 1e-1
CONV_W = 256
CONV_K = 31
N_BRANCH = 3
D_FF = 2816
N_EXPERTS = 8
TOP_K = 2
D_FF_EXPERT = 3584
N_DENSE = (DEPTH + 1) // 2
N_MOE = DEPTH // 2
EPS = 1e-6

Q_END = ATT_W
K_END = 2 * ATT_W
V_END = 3 * ATT_W
F_END = V_END + ATT_HEADS
U_END = F_END + SSM_W
C_END = U_END + 2 * CONV_W
N_IN = C_END + N_BRANCH * D_MODEL
SPLITS = [Q_END, K_END, V_END, F_END, U_END, C_END]

kernel_name = "gated_parallel_fox_s5_conformer_moe_trunk"

def rmsnorm(x, g):
    xf = x.astype(jnp.float32)
    y = xf * lax.rsqrt(jnp.mean(xf * xf, axis=-1, keepdims=True) + EPS) * g.astype(jnp.float32)
    return y.astype(x.dtype)

def fox_attention(q, k, v, logf):
    B, L, H, dh = q.shape
    nb = L // Q_BLOCK
    Fh = jnp.cumsum(logf, axis=1).transpose(0, 2, 1)
    qb = q.astype(jnp.float32).reshape(B, nb, Q_BLOCK, H, dh).transpose(1, 0, 2, 3, 4)
    Fb = Fh.reshape(B, H, nb, Q_BLOCK).transpose(2, 0, 1, 3)
    kf = k.astype(jnp.float32)
    vf = v.astype(jnp.float32)
    kpos = jnp.arange(L)
    scale = dh ** -0.5

    def block(args):
        i, qi, Fi = args
        qpos = i * Q_BLOCK + jnp.arange(Q_BLOCK)
        s = jnp.einsum('bqhd,bkhd->bhqk', qi, kf) * scale
        s = s + Fi[..., None] - Fh[:, :, None, :]
        s = jnp.where(kpos[None, :] <= qpos[:, None], s, -jnp.inf)
        p = jax.nn.softmax(s, axis=-1)
        return jnp.einsum('bhqk,bkhd->bqhd', p, vf)

    out = lax.map(block, (jnp.arange(nb), qb, Fb))
    return out.transpose(1, 0, 2, 3, 4).reshape(B, L, H * dh)

def s5_ssm(u, a_re, a_im, log_dt, b_re, b_im, c_re, c_im, d_skip, w_glu):
    B, L, _ = u.shape
    uf = u.astype(jnp.float32).reshape(B, L, SSM_GROUPS, SSM_GROUP)
    lam = lax.complex(a_re.astype(jnp.float32), a_im.astype(jnp.float32))
    dt = jnp.exp(log_dt.astype(jnp.float32))[:, None]
    a_bar = jnp.exp(lam * dt)
    b = lax.complex(b_re.astype(jnp.float32), b_im.astype(jnp.float32))
    b_bar = ((a_bar - 1.0) / lam)[..., None] * b
    bu = jnp.einsum('blgh,gph->blgp', uf.astype(jnp.complex64), b_bar)
    a_seq = jnp.broadcast_to(a_bar[None, None], (1, L) + a_bar.shape)

    def combine(e1, e2):
        a1, x1 = e1
        a2, x2 = e2
        return a1 * a2, a2 * x1 + x2

    _, xs = lax.associative_scan(combine, (a_seq, bu), axis=1)
    c = lax.complex(c_re.astype(jnp.float32), c_im.astype(jnp.float32))
    y = jnp.real(jnp.einsum('blgp,ghp->blgh', xs, c)) + d_skip.astype(jnp.float32) * uf
    y = jax.nn.gelu(y.reshape(B, L, SSM_W))
    val, gate = jnp.split(y @ w_glu.astype(jnp.float32), 2, axis=-1)
    return val * jax.nn.sigmoid(gate)

def conformer_conv(z, conv_w, conv_b, ln_g, ln_b):
    a, g = jnp.split(z.astype(jnp.float32), 2, axis=-1)
    h = a * jax.nn.sigmoid(g)
    hp = jnp.pad(h, ((0, 0), (CONV_K - 1, 0), (0, 0)))
    y = lax.conv_general_dilated(hp, conv_w.astype(jnp.float32)[:, None, :], window_strides=(1,),
                                 padding='VALID', dimension_numbers=('NWC', 'WIO', 'NWC'),
                                 feature_group_count=CONV_W) + conv_b.astype(jnp.float32)
    mu = jnp.mean(y, axis=-1, keepdims=True)
    var = jnp.mean(jnp.square(y - mu), axis=-1, keepdims=True)
    y = (y - mu) * lax.rsqrt(var + EPS) * ln_g.astype(jnp.float32) + ln_b.astype(jnp.float32)
    return jax.nn.silu(y)

def swiglu(h, w_gate, w_up, w_down):
    return (jax.nn.silu(h @ w_gate) * (h @ w_up)) @ w_down

def moe_swiglu(h, w_router, b_router, w_gate, w_up, w_down):
    B, L, D = h.shape
    t = h.reshape(-1, D)
    logits = (t @ w_router).astype(jnp.float32) + b_router.astype(jnp.float32)
    top_val, top_idx = lax.top_k(logits, TOP_K)
    probs = jax.nn.softmax(top_val, axis=-1)
    weights = jnp.sum(jax.nn.one_hot(top_idx, N_EXPERTS, dtype=jnp.float32) * probs[..., None], axis=1)
    weights = weights.astype(t.dtype)
    out = jnp.zeros_like(t)
    for e in range(N_EXPERTS):
        out = out + weights[:, e:e + 1] * swiglu(t, w_gate[e], w_up[e], w_down[e])
    return out.reshape(B, L, D)

def setup_inputs(seed: int = 0) -> dict:
    key = jax.random.key(seed)
    ks = jax.random.split(key, 32)
    f32 = jnp.float32
    nrm = lambda k, shape, scale: jax.random.normal(k, shape, f32) * scale
    x = jax.random.normal(ks[0], (BATCH, SEQ, D_MODEL), f32)
    g_mix = 1.0 + nrm(ks[1], (DEPTH, D_MODEL), 0.02)
    w_in = nrm(ks[2], (DEPTH, D_MODEL, N_IN), D_MODEL ** -0.5)
    b_in = nrm(ks[3], (DEPTH, N_IN), 0.02)
    b_in = b_in.at[:, V_END:F_END].add(jnp.linspace(1.0, 6.0, ATT_HEADS, dtype=f32))
    n = jnp.arange(SSM_STATE, dtype=f32)
    ssm_a_re = -0.5 + nrm(ks[4], (DEPTH, SSM_GROUPS, SSM_STATE), 0.01)
    ssm_a_im = math.pi * n + nrm(ks[5], (DEPTH, SSM_GROUPS, SSM_STATE), 0.01)
    ssm_log_dt = jax.random.uniform(ks[6], (DEPTH, SSM_GROUPS), f32, math.log(DT_MIN), math.log(DT_MAX))
    bs = (2.0 * SSM_GROUP) ** -0.5
    ssm_b_re = nrm(ks[7], (DEPTH, SSM_GROUPS, SSM_STATE, SSM_GROUP), bs)
    ssm_b_im = nrm(ks[8], (DEPTH, SSM_GROUPS, SSM_STATE, SSM_GROUP), bs)
    cs = (2.0 * SSM_STATE) ** -0.5
    ssm_c_re = nrm(ks[9], (DEPTH, SSM_GROUPS, SSM_GROUP, SSM_STATE), cs)
    ssm_c_im = nrm(ks[10], (DEPTH, SSM_GROUPS, SSM_GROUP, SSM_STATE), cs)
    ssm_d = nrm(ks[11], (DEPTH, SSM_GROUPS, SSM_GROUP), 0.5)
    ssm_w_glu = nrm(ks[12], (DEPTH, SSM_W, 2 * SSM_W), SSM_W ** -0.5)
    conv_w = nrm(ks[13], (DEPTH, CONV_K, CONV_W), CONV_K ** -0.5)
    conv_b = nrm(ks[14], (DEPTH, CONV_W), 0.02)
    conv_ln_g = 1.0 + nrm(ks[15], (DEPTH, CONV_W), 0.02)
    conv_ln_b = nrm(ks[16], (DEPTH, CONV_W), 0.02)
    w_att_out = nrm(ks[17], (DEPTH, ATT_W, D_MODEL), ATT_W ** -0.5)
    w_ssm_out = nrm(ks[18], (DEPTH, SSM_W, D_MODEL), SSM_W ** -0.5)
    w_conv_out = nrm(ks[19], (DEPTH, CONV_W, D_MODEL), CONV_W ** -0.5)
    w_o = nrm(ks[20], (DEPTH, D_MODEL, D_MODEL), D_MODEL ** -0.5)
    g_ffn = 1.0 + nrm(ks[21], (DEPTH, D_MODEL), 0.02)
    ffn_w_gate = nrm(ks[22], (N_DENSE, D_MODEL, D_FF), D_MODEL ** -0.5)
    ffn_w_up = nrm(ks[23], (N_DENSE, D_MODEL, D_FF), D_MODEL ** -0.5)
    ffn_w_down = nrm(ks[24], (N_DENSE, D_FF, D_MODEL), D_FF ** -0.5)
    moe_w_router = nrm(ks[25], (N_MOE, D_MODEL, N_EXPERTS), D_MODEL ** -0.5)
    moe_b_router = nrm(ks[26], (N_MOE, N_EXPERTS), 0.01)
    moe_w_gate = nrm(ks[27], (N_MOE, N_EXPERTS, D_MODEL, D_FF_EXPERT), D_MODEL ** -0.5)
    moe_w_up = nrm(ks[28], (N_MOE, N_EXPERTS, D_MODEL, D_FF_EXPERT), D_MODEL ** -0.5)
    moe_w_down = nrm(ks[29], (N_MOE, N_EXPERTS, D_FF_EXPERT, D_MODEL), D_FF_EXPERT ** -0.5)
    g_final = 1.0 + nrm(ks[30], (D_MODEL,), 0.02)
    return {"x": x, "g_mix": g_mix, "w_in": w_in, "b_in": b_in,
            "ssm_a_re": ssm_a_re, "ssm_a_im": ssm_a_im, "ssm_log_dt": ssm_log_dt,
            "ssm_b_re": ssm_b_re, "ssm_b_im": ssm_b_im, "ssm_c_re": ssm_c_re, "ssm_c_im": ssm_c_im,
            "ssm_d": ssm_d, "ssm_w_glu": ssm_w_glu,
            "conv_w": conv_w, "conv_b": conv_b, "conv_ln_g": conv_ln_g, "conv_ln_b": conv_ln_b,
            "w_att_out": w_att_out, "w_ssm_out": w_ssm_out, "w_conv_out": w_conv_out, "w_o": w_o,
            "g_ffn": g_ffn, "ffn_w_gate": ffn_w_gate, "ffn_w_up": ffn_w_up, "ffn_w_down": ffn_w_down,
            "moe_w_router": moe_w_router, "moe_b_router": moe_b_router,
            "moe_w_gate": moe_w_gate, "moe_w_up": moe_w_up, "moe_w_down": moe_w_down,
            "g_final": g_final}

def reference(x, g_mix, w_in, b_in, ssm_a_re, ssm_a_im, ssm_log_dt, ssm_b_re, ssm_b_im,
              ssm_c_re, ssm_c_im, ssm_d, ssm_w_glu, conv_w, conv_b, conv_ln_g, conv_ln_b,
              w_att_out, w_ssm_out, w_conv_out, w_o, g_ffn, ffn_w_gate, ffn_w_up, ffn_w_down,
              moe_w_router, moe_b_router, moe_w_gate, moe_w_up, moe_w_down, g_final):
    B, L, D = x.shape
    dt = x.dtype
    for l in range(DEPTH):
        h = rmsnorm(x, g_mix[l])
        proj = h @ w_in[l] + b_in[l]
        q, k, v, fz, u, cz, gz = jnp.split(proj, SPLITS, axis=-1)
        hs = (B, L, ATT_HEADS, ATT_HEAD_DIM)
        logf = jax.nn.log_sigmoid(fz.astype(jnp.float32))
        att = fox_attention(q.reshape(hs), k.reshape(hs), v.reshape(hs), logf).astype(dt)
        ssm = s5_ssm(u, ssm_a_re[l], ssm_a_im[l], ssm_log_dt[l], ssm_b_re[l], ssm_b_im[l],
                     ssm_c_re[l], ssm_c_im[l], ssm_d[l], ssm_w_glu[l]).astype(dt)
        conv = conformer_conv(cz, conv_w[l], conv_b[l], conv_ln_g[l], conv_ln_b[l]).astype(dt)
        gates = jax.nn.sigmoid(gz).reshape(B, L, N_BRANCH, D)
        merged = (gates[:, :, 0] * (att @ w_att_out[l])
                  + gates[:, :, 1] * (ssm @ w_ssm_out[l])
                  + gates[:, :, 2] * (conv @ w_conv_out[l]))
        x = x + merged @ w_o[l]
        h = rmsnorm(x, g_ffn[l])
        if l % 2 == 0:
            i = l // 2
            f = swiglu(h, ffn_w_gate[i], ffn_w_up[i], ffn_w_down[i])
        else:
            i = l // 2
            f = moe_swiglu(h, moe_w_router[i], moe_b_router[i], moe_w_gate[i], moe_w_up[i], moe_w_down[i])
        x = x + f.astype(dt)
    return rmsnorm(x, g_final)


_drawn_inputs = setup_inputs


def setup_inputs(seed=0):
    import zlib

    import numpy as np

    out = dict(_drawn_inputs(seed))
    spreads = {}
    factors = {'ssm_a_re': 64.0,
     'ssm_log_dt': 23.496,
     'ssm_b_im': 21.8,
     'ssm_c_re': 26.136,
     'conv_ln_g': 3.321,
     'conv_ln_b': 3.425,
     'moe_b_router': 5.199,
     'g_final': 7.648,
     'ssm_a_im': 8.0,
     'ssm_b_re': 8.0,
     'ssm_c_im': 8.0}
    for name, (base, spread) in spreads.items():
        noise = np.random.default_rng([zlib.crc32(name.encode()), seed]).standard_normal(out[name].shape)
        drawn = base * np.exp(spread * noise) if base else spread * noise
        out[name] = __import__('jax').numpy.asarray(drawn.astype(out[name].dtype))
    for name, factor in factors.items():
        out[name] = (out[name] * factor).astype(out[name].dtype)
    return out
```

```python
from contextlib import ExitStack

import concourse.bass as bass
from concourse import mybir

P = 128
F32 = mybir.dt.float32
U32 = mybir.dt.uint32
ALU = mybir.AluOpType
ACT = mybir.ActivationFunctionType
AX_X = mybir.AxisListType.X

EPS = 1e-6
MASKED = -1e30
TWO_PI = 6.283185307179586
TWO_PI_A = 6.28125
TWO_PI_B = 0.0019340515136718750
TWO_PI_C = TWO_PI - TWO_PI_A - TWO_PI_B
ROUND_MAGIC = 12582912.0

RING = 4
EXPERT_RING = 7
SLOT = 4096
MIX_LOADS = 16


def hybrid_trunk(nc, t, out):
    DEPTH, D, N_IN = t["w_in"].shape
    T = t["x"].shape[1]
    KT, TT = D // P, T // P
    G, S, GH = t["ssm_b_re"].shape[1:]
    H = (N_IN - 3 * D - G * GH - 2 * t["conv_w"].shape[2]) // (3 * 64 + 1)
    DH = 64
    AW = H * DH
    V_AT, F_AT = 2 * AW, 3 * AW
    U_AT = F_AT + H
    C_AT = U_AT + G * GH
    CK, CW = t["conv_w"].shape[1:]
    G_AT = C_AT + 2 * CW
    DFF = t["ffn_w_gate"].shape[2]
    NE, _, DFE = t["moe_w_gate"].shape[1:]
    NJ = G * S // P
    HJ = NJ // 2
    PAD = CK - 1
    assert (D, T, AW, G * GH, CW, NJ) == (1024, 256, 512, 256, 256, 8) and DEPTH == 2

    ctx = ExitStack()
    with ctx:
        def sb(name, shape, dt=F32):
            return ctx.enter_context(nc.sbuf_tensor(name, shape, dt))

        arena = sb("arena", [P, EXPERT_RING * SLOT])
        at = RING * SLOT
        gates = arena[:, at:at + 24 * T].rearrange("p (n t) -> p n t", t=T)
        at += 24 * T
        phase = arena[:, at:at + 2 * HJ * T].rearrange("p (c j t) -> p c j t", c=2, t=T)
        at += 2 * HJ * T
        state = arena[:, at:at + 2 * HJ * T].rearrange("p (c j t) -> p c j t", c=2, t=T)
        at += 2 * HJ * T
        rot_tmp = arena[:, at:at + 1024].rearrange("p (c j t) -> p c j t", c=2, t=T)
        at += 1024
        back_flat = arena[:, at:at + 1024]
        back_tmp = back_flat.rearrange("p (c j t) -> p c j t", c=2, t=T)
        at += 1024
        assert at <= EXPERT_RING * SLOT

        def slot(s, k, n, first=0):
            return arena[:, s * SLOT + first:s * SLOT + first + k * n].rearrange("p (k n) -> p k n", n=n)

        x_sb = sb("x_sb", [P, TT, D])
        hn = sb("hn", [P, TT, D])
        merged = hn[:].rearrange("p a (b t) -> p (a b) t", t=T)
        mat_src = hn[:].rearrange("p a (b n) -> p (a b) n", n=512)
        hT = sb("hT", [P, KT, T])
        qT = sb("qT", [P, AW // P, T])
        k_pad = sb("k_pad", [P, H, T])
        v_sb = sb("v_sb", [P, TT, AW])
        f_left = sb("f_left", [P, T])
        f_right = sb("f_right", [P, 4, T])
        f_sum = sb("f_sum", [64, T])
        probs = sb("probs", [P, 4, 384])
        probsT = sb("probsT", [P, 4, 384])
        attT = sb("attT", [P, AW // P, T])
        uT = sb("uT", [P, 2, T])
        conv_in = sb("conv_in", [P, 2, PAD + T])
        conv_acc = sb("conv_acc", [P, 2, T])
        conv_sig = sb("conv_sig", [P, 2, T])
        ssm_z = uT
        ssm_g = sb("ssm_g", [P, 2, T])
        ssm_sig = ssm_g
        b_mat = sb("b_mat", [P, 2, HJ, P])
        c_mat = sb("c_mat", [P, 2, HJ, P])
        silu_g = probs[:].rearrange("p a b -> p (a b)")[:, 0:2 * T].rearrange("p (r t) -> p r t", t=T)
        hidden = probsT[:].rearrange("p a b -> p (a b)")[:, 0:4 * T].rearrange("p (r t) -> p r t", t=T)

        ident = sb("ident", [P, P])
        causal = sb("causal", [P, P])
        mean_mat = sb("mean_mat", [P, P])
        ones_row = sb("ones_row", [1, P])
        b_mask = sb("b_mask", [P, HJ * 8])
        c_mask = sb("c_mask", [P, 2, 8])
        f_scale = sb("f_scale", [64, H + 1])
        f_shift = sb("f_shift", [64, H + 1])

        NROW = 30 + 12 + 8 + 8 + 8 + CK * CW // P
        rows = back_flat[:, 512:512 + DEPTH * P].rearrange("p (l n) -> p l n", l=DEPTH)
        cols = sb("cols", [P, DEPTH, NROW])
        srow = sb("srow", [32, P])
        ldt_row = sb("ldt_row", [16, P])
        ones_col = sb("ones_col", [64, 1])
        ldt = sb("ldt", [16, 2])
        scol = sb("scol", [P, 48])
        b_raw = sb("b_raw", [P, 2, DEPTH, NJ, GH])
        b_bar = sb("b_bar", [P, 2, NJ, GH])
        b_tmp = back_flat[:, 0:2 * NJ * GH].rearrange("p (c j h) -> p c j h", c=2, j=NJ)
        c_raw = sb("c_raw", [P, 2, DEPTH, 2, S])
        wf = sb("wf", [P, KT, 64])
        bf = sb("bf", [64, DEPTH])
        w_router = sb("w_router", [P, KT, NE])
        b_router = sb("b_router", [1, NE])
        g_final = qT[:].rearrange("p a t -> p (a t)")
        fz = rot_tmp[0:64, 0]
        SC = DEPTH * NJ
        sm = sb("sm", [P, 14, SC])
        rot_pow = sb("rot_pow", [P, 2, 8, SC])
        st = sb("st", [P, 5, 3, TT])
        att_max = sb("att_max", [P, 2, 4])
        att_sum = sb("att_sum", [P, 2, 4])
        att_rs = sb("att_rs", [P, 2, 4])
        ln_r = rot_tmp[:, 0, 0]
        logits = sb("logits", [P, TT, NE])
        top = sb("top", [P, TT, 8])
        top_at = sb("top_at", [P, TT, 8], U32)
        top_f = sb("top_f", [P, TT, 8])
        rt = sb("rt", [P, TT, 4])
        e_iota = sb("e_iota", [P, NE])
        w_exp = sb("w_exp", [P, TT, NE])
        w_tmp = sb("w_tmp", [P, TT, NE])

        bank = [ctx.enter_context(nc.psum_tensor(f"bank{i}", [P, 512], F32)) for i in range(8)]

        def halves(b):
            return bank[b][:, :].rearrange("p (a t) -> p a t", a=2)

        BI = 0
        QK = 30
        GM, GF = 42, 50
        SD, CB, LG, LB = 58, 60, 62, 64
        CWC = 66

        def sems(names):
            return {n: ctx.enter_context(nc.semaphore(n)) for n in names.split()}

        slot_full = [ctx.enter_context(nc.semaphore(f"slot_full{i}")) for i in range(RING)]
        expert_full = [ctx.enter_context(nc.semaphore(f"expert_full{i}")) for i in range(EXPERT_RING)]
        g = sems("x_in rows_in states_in mats_in side_in gain_in final_in out_done "
                 "gate_used pe_params act_params "
                 "pool_const pool_order dve_const dve_order act_order dve_theta act_trig dve_states "
                 "ffn_up_done ffn_act_silu ffn_hidden ffn_down_done acc_read "
                 "pe_router router_read act_top")
        PER = dict(pe_proj=10, act_qk=12, dve_v=2, dve_fz=2, act_f=2, dve_f=9, dve_u=2, act_cg=2, dve_cv=2,
                   pool_mats=8, pe_mats=8, act_mats=8, pool_phase=2, pe_bu=4, dve_bu=4, dve_scan=4, pool_back=4,
                   pe_y=2, dve_z=2, act_gelu=1, pe_glu=2, act_glu=1, dve_glu=1, pe_gate=12, act_gate=24,
                   pe_s=8, dve_max=2, act_exp=16, dve_p=4, pe_pt=8, act_pt=8, pe_att=4, dve_att=8,
                   dve_conv=2, pe_ln=2, dve_ln=4, act_ln=1, act_conv=2, pe_out=12, dve_merge=4, pe_wo=2, dve_wo=4,
                   act_ss=2, dve_rv=1, act_sd=1, dve_hn=1, act_hn=1, pe_tr=4, dve_ht=4, act_ht=4)
        S_ = sems(" ".join(PER))

        loads, used_at = [], []

        def k_tiles(w):
            return w.rearrange("(k p) n -> p k n", p=P)

        def load(used, *parts):
            s = len(loads) % RING
            loads.append([(slot(s, src.shape[1], src.shape[2], first), src) for src, first in parts])
            used_at.append(used)

        FF_CH = [(c, min(512, DFF - c)) for c in range(0, DFF, 512)]
        mix_at, ffn_at = [], None
        for l in range(DEPTH):
            mix_at.append(len(loads))
            w = t["w_in"][l]

            def used(name, v):
                return S_[name], l * PER[name] + v

            for n, (a, b) in enumerate(((0, AW), (AW, V_AT), (V_AT, F_AT), (U_AT, C_AT), (C_AT, G_AT))):
                load(used("pe_proj", (2, 4, 6, 8, 10)[n]), (k_tiles(w[:, a:b]), 0))
            for n, c in enumerate(range(G_AT, N_IN, 512)):
                load(used("pe_gate", 2 * n + 2), (k_tiles(w[:, c:c + 512]), 0))
            load(used("pe_glu", 2), (k_tiles(t["ssm_w_glu"][l]), 0))
            load(used("pe_out", 12), (k_tiles(t["w_att_out"][l]), 0))
            load(used("pe_out", 12), (k_tiles(t["w_ssm_out"][l]), 0), (k_tiles(t["w_conv_out"][l]), 2 * D))
            load(used("pe_wo", 1), (k_tiles(t["w_o"][l, 0:512]), 0))
            load(used("pe_wo", 2), (k_tiles(t["w_o"][l, 512:D]), 0))
            assert len(loads) == mix_at[l] + MIX_LOADS
            if l == 0:
                ffn_at = len(loads)
                for n, (c, w_) in enumerate(FF_CH):
                    tiles = (c + w_) // P
                    load((g["gate_used"], n + 1), (k_tiles(t["ffn_w_gate"][0][:, c:c + w_]), 0))
                    load((g["ffn_up_done"], tiles), (k_tiles(t["ffn_w_up"][0][:, c:c + w_]), 0))
                    load((g["ffn_down_done"], tiles), (k_tiles(t["ffn_w_down"][0][c:c + w_, :]), 0))
        N_LOADS = len(loads)
        full_at, count = [], [0] * RING
        for n, parts in enumerate(loads):
            count[n % RING] += 16 * len(parts)
            full_at.append(count[n % RING])
        last_in_slot = [max(n for n in range(N_LOADS) if n % RING == s) for s in range(RING)]

        E_CH = DFE // 512
        E_LOADS = 3 * E_CH
        assert E_LOADS % EXPERT_RING == 0 and DFE % 512 == 0
        E_TURNS = E_LOADS // EXPERT_RING
        N_FF = DFF // P
        N_FE = DFE // P

        block = ctx.enter_context(nc.Block())

        @block.sync
        def _(sp):
            sp.dma_start(x_sb[:], t["x"][0].rearrange("(a p) d -> p a d", p=P)).then_inc(g["x_in"], 16)
            for n, parts in enumerate(loads):
                if n >= RING:
                    sp.wait_ge(*used_at[n - RING])
                for dst, src in parts:
                    sp.dma_start(dst, src).then_inc(slot_full[n % RING], 16)
            with sp.Fori(0, NE) as e:
                for j in range(E_LOADS):
                    s, c = j % EXPERT_RING, j // 3
                    if j < RING:
                        sp.wait_ge(*used_at[last_in_slot[s]])
                    elif j < EXPERT_RING:
                        sp.wait_ge(S_["dve_merge"], DEPTH * PER["dve_merge"])
                    e_, j_ = (e, j - EXPERT_RING) if j >= EXPERT_RING else (e - 1, j - EXPERT_RING + E_LOADS)
                    if j_ % 3 == 0:
                        sp.wait_ge(g["gate_used"], e_ * E_CH + (len(FF_CH) + j_ // 3 + 1))
                    else:
                        sp.wait_ge(g["ffn_up_done" if j_ % 3 == 1 else "ffn_down_done"],
                                   e_ * N_FE + (N_FF + 4 * (j_ // 3) + 4))
                    name = ("moe_w_gate", "moe_w_up", "moe_w_down")[j % 3]
                    w = t[name][0, bass.ds(e, 1)]
                    if j % 3 < 2:
                        src = w[:, :, c * 512:(c + 1) * 512].rearrange("o (k p) n -> p (o k) n", p=P)
                        dst = slot(s, KT, 512)
                    else:
                        src = w[:, c * 512:(c + 1) * 512, :].rearrange("o (k p) n -> p (o k) n", p=P)
                        dst = slot(s, 4, D)
                    sp.dma_start(dst, src).then_inc(expert_full[s], 16)
            sp.wait_ge(g["final_in"], 1)
            sp.dma_start(out[0].rearrange("(a p) d -> p a d", p=P), hn[:]).then_inc(g["out_done"], 16)
            sp.wait_ge(g["out_done"], 16)

        @block.gpsimd
        def _(pool):
            done = [0]

            def link(ins):
                done[0] += 1
                ins.then_inc(g["pool_order"], 1)
                pool.wait_ge(g["pool_order"], done[0])

            def const(ins):
                ins.then_inc(g["pool_const"], 1)

            link(pool.memset(ident[:], 0.0))
            const(pool.affine_select(out=ident[:], in_=ident[:], compare_op=ALU.not_equal, fill=1.0, base=0,
                                     pattern=[[-1, P]], channel_multiplier=1))
            link(pool.memset(causal[:], 0.0))
            const(pool.affine_select(out=causal[:], in_=causal[:], compare_op=ALU.is_ge, fill=MASKED, base=0,
                                     pattern=[[-1, P]], channel_multiplier=1))
            link(pool.memset(c_mask[:, 0, :], 1.0))
            link(pool.affine_select(out=c_mask[:, 0, :], in_=c_mask[:, 0, :], compare_op=ALU.is_ge, fill=0.0, base=0,
                                    pattern=[[-GH, 8]], channel_multiplier=1))
            link(pool.affine_select(out=c_mask[:, 0, :], in_=c_mask[:, 0, :], compare_op=ALU.is_ge, fill=0.0,
                                    base=GH - 1, pattern=[[GH, 8]], channel_multiplier=-1))
            link(pool.tensor_scalar(c_mask[:, 1, :], c_mask[:, 0, :], -1.0, None, ALU.mult))
            link(pool.memset(b_mask[:], 0.0))
            link(pool.memset(b_mask[0:64, 0:3 * 10 + 1:10], 1.0))
            link(pool.memset(b_mask[64:P, 1:3 * 10 + 2:10], 1.0))
            link(pool.memset(f_scale[:], 0.0))
            link(pool.memset(f_shift[:], 0.0))
            link(pool.memset(f_scale[0:H, H:H + 1], 8.0))
            link(pool.memset(f_shift[32:32 + H, H:H + 1], 1.0))
            link(pool.affine_select(out=f_scale[:, 0:H], in_=f_scale[:, 0:H], compare_op=ALU.not_equal, fill=-8.0,
                                    base=-32, pattern=[[-1, H]], channel_multiplier=1))
            const(pool.affine_select(out=f_shift[:, 0:H], in_=f_shift[:, 0:H], compare_op=ALU.not_equal, fill=1.0,
                                     base=0, pattern=[[-1, H]], channel_multiplier=1))
            link(pool.memset(k_pad[:], 0.0))
            link(pool.memset(conv_in[:], 0.0))
            const(pool.iota(e_iota[:], [[1, NE]], base=0, channel_multiplier=0,
                            allow_small_or_imprecise_dtypes=True))

            pool.wait_ge(g["dve_const"], 2)
            def forget_weights(l):
                for at_ in (0, 32):
                    pool.dma_start(wf[:, :, at_:at_ + H], k_tiles(t["w_in"][l][:, F_AT:U_AT])).then_inc(g["side_in"], 16)
                    pool.dma_start(bf[at_:at_ + H, l:l + 1],
                                   t["b_in"][l, F_AT:U_AT].rearrange("(n o) -> n o", o=1)).then_inc(g["side_in"], 16)

            forget_weights(0)
            pool.dma_start(w_router[:], k_tiles(t["moe_w_router"][0])).then_inc(g["side_in"], 16)
            pool.dma_start(b_router[:], t["moe_b_router"][0:1]).then_inc(g["side_in"], 16)

            for l in range(DEPTH):
                if l:
                    pool.wait_ge(S_["pe_proj"], (l - 1) * PER["pe_proj"] + 7)
                    forget_weights(l)
                pool.wait_ge(g["dve_states"], 1)
                pool.wait_ge(g["mats_in"], 128)
                j0 = l * NJ
                f_re, f_im = (sm[:, k, j0:j0 + NJ].rearrange("p (j o) -> p j o", o=1).to_broadcast([P, NJ, GH])
                              for k in (10, 11))
                link(pool.tensor_tensor(b_bar[:, 0], b_raw[:, 0, l], f_re, ALU.mult))
                link(pool.tensor_tensor(b_tmp[:, 0], b_raw[:, 1, l], f_im, ALU.mult))
                link(pool.tensor_tensor(b_bar[:, 1], b_raw[:, 1, l], f_re, ALU.mult))
                link(pool.tensor_tensor(b_tmp[:, 1], b_raw[:, 0, l], f_im, ALU.mult))
                link(pool.tensor_tensor(b_bar[:, 0], b_bar[:, 0], b_tmp[:, 0], ALU.subtract))
                link(pool.tensor_tensor(b_bar[:, 1], b_bar[:, 1], b_tmp[:, 1], ALU.add))
                pool.wait_ge(S_["pe_tr"], 2 * l * PER["pe_tr"] + 4)
                for half in range(2):
                    if half:
                        pool.wait_ge(S_["pe_mats"], l * PER["pe_mats"] + 4)
                    for c in range(2):
                        o = mat_src[:, c].rearrange("p (j g h) -> p j g h", j=HJ, g=8)
                        src = b_bar[:, c, half * HJ:(half + 1) * HJ]
                        pool.tensor_tensor(
                            o, src.rearrange("p j (o h) -> p j o h", o=1).to_broadcast([P, HJ, 8, GH]),
                            b_mask[:].rearrange("p (j g o) -> p j g o", g=8, o=1).to_broadcast([P, HJ, 8, GH]),
                            ALU.mult).then_inc(S_["pool_mats"], 1)
                    for c in range(2):
                        o = mat_src[:, 2 + c].rearrange("p (g s) -> p g s", g=8)
                        pool.tensor_tensor(
                            o, c_raw[:, c, l, half:half + 1].to_broadcast([P, 8, S]),
                            c_mask[:, c].rearrange("p (g o) -> p g o", o=1).to_broadcast([P, 8, S]),
                            ALU.mult).then_inc(S_["pool_mats"], 1)
                    if l and half == 0:
                        pool.wait_ge(S_["dve_bu"], l * PER["dve_bu"])
                    if half:
                        pool.wait_ge(S_["dve_bu"], l * PER["dve_bu"] + 2)
                        pool.wait_ge(S_["pool_back"], l * PER["pool_back"] + 2)
                    cs, sn = phase[:, 0], phase[:, 1]
                    link(pool.memset(cs[:, :, 0:1], 1.0))
                    link(pool.memset(sn[:, :, 0:1], 0.0))
                    w, n = 1, 0
                    while w < T:
                        zj = j0 + half * HJ
                        z_re, z_im = (rot_pow[:, c, n, zj:zj + HJ].rearrange("p (j o) -> p j o", o=1)
                                      .to_broadcast([P, HJ, w]) for c in range(2))
                        tmp = [back_tmp.rearrange("p c j t -> p (c j t)")[:, a * HJ * w:(a + 1) * HJ * w]
                               .rearrange("p (j t) -> p j t", t=w) for a in range(2)]
                        link(pool.tensor_tensor(tmp[0], cs[:, :, 0:w], z_re, ALU.mult))
                        link(pool.tensor_tensor(tmp[1], sn[:, :, 0:w], z_im, ALU.mult))
                        link(pool.tensor_tensor(cs[:, :, w:2 * w], tmp[0], tmp[1], ALU.subtract))
                        link(pool.tensor_tensor(tmp[0], cs[:, :, 0:w], z_im, ALU.mult))
                        link(pool.tensor_tensor(tmp[1], sn[:, :, 0:w], z_re, ALU.mult))
                        last = pool.tensor_tensor(sn[:, :, w:2 * w], tmp[0], tmp[1], ALU.add)
                        w, n = 2 * w, n + 1
                        if w < T:
                            link(last)
                        else:
                            last.then_inc(S_["pool_phase"], 1)
                            pool.wait_ge(S_["pool_phase"], l * PER["pool_phase"] + half + 1)
                    for q in range(2):
                        pair = 2 * half + q
                        pool.wait_ge(S_["dve_scan"], l * PER["dve_scan"] + pair + 1)
                        y_re, y_im = (state[:, c, 2 * q:2 * q + 2] for c in range(2))
                        c_, s_ = (phase[:, c, 2 * q:2 * q + 2] for c in range(2))
                        ta, tb = back_tmp[:, 0], back_tmp[:, 1]
                        link(pool.tensor_tensor(ta, y_im, s_, ALU.mult))
                        link(pool.tensor_tensor(tb, y_re, s_, ALU.mult))
                        link(pool.tensor_tensor(y_re, y_re, c_, ALU.mult))
                        link(pool.tensor_tensor(y_im, y_im, c_, ALU.mult))
                        link(pool.tensor_tensor(y_re, y_re, ta, ALU.subtract))
                        pool.tensor_tensor(y_im, y_im, tb, ALU.add).then_inc(S_["pool_back"], 1)
                        pool.wait_ge(S_["pool_back"], l * PER["pool_back"] + pair + 1)
            pool.wait_ge(S_["dve_merge"], DEPTH * 4)
            pool.dma_start(g_final, t["g_final"].rearrange("(o d) -> o d", o=1).to_broadcast([P, D])).then_inc(g["gain_in"], 16)

        @block.scalar
        def _(act):
            for l in range(DEPTH):
                def row_load(at, src):
                    act.dma_start(rows[at:at + src.shape[0], l, :], src).then_inc(g["rows_in"], 16)

                row_load(BI, t["b_in"][l, U_AT:N_IN].rearrange("(r n) -> r n", n=P))
                row_load(QK, t["b_in"][l, 0:F_AT].rearrange("(r n) -> r n", n=P))
                row_load(GM, t["g_mix"][l].rearrange("(r n) -> r n", n=P))
                row_load(GF, t["g_ffn"][l].rearrange("(r n) -> r n", n=P))
                row_load(SD, t["ssm_d"][l].rearrange("(r a) h -> r (a h)", r=2))
                row_load(CB, t["conv_b"][l].rearrange("(r n) -> r n", n=P))
                row_load(LG, t["conv_ln_g"][l].rearrange("(r n) -> r n", n=P))
                row_load(LB, t["conv_ln_b"][l].rearrange("(r n) -> r n", n=P))
                row_load(CWC, t["conv_w"][l].rearrange("k (r n) -> (k r) n", n=P))
            act.dma_start(srow[0:16, :], t["ssm_a_re"].rearrange("l (j a) s -> (l j) (a s)", a=2)).then_inc(g["states_in"], 16)
            act.dma_start(srow[16:32, :], t["ssm_a_im"].rearrange("l (j a) s -> (l j) (a s)", a=2)).then_inc(g["states_in"], 16)
            act.dma_start(ldt[:, :], t["ssm_log_dt"].rearrange("l (j a) -> (l j) a", a=2)).then_inc(g["states_in"], 16)
            for l in range(DEPTH):
                for c, (b, cc) in enumerate((("ssm_b_re", "ssm_c_re"), ("ssm_b_im", "ssm_c_im"))):
                    act.dma_start(b_raw[:, c, l], t[b][l].rearrange("(j a) s h -> (a s) j h", a=2)).then_inc(g["mats_in"], 16)
                    act.dma_start(c_raw[:, c, l], t[cc][l].rearrange("(i a) h s -> (a h) i s", i=2)).then_inc(g["mats_in"], 16)
            for l in range(DEPTH):
                act.wait_ge(g["pe_params"], l + 1)
                act.activation(cols[:, l], bank[7 - l][:, 0:NROW], ACT.Copy).then_inc(g["act_params"], 1)
            act.wait_ge(g["dve_theta"], 1)
            act.activation(sm[:, 0], sm[:, 0], ACT.Exp).then_inc(g["act_trig"], 1)
            act.wait_ge(g["dve_theta"], 2)
            act.activation(sm[:, 3], sm[:, 3], ACT.Exp).then_inc(g["act_trig"], 1)
            act.activation(sm[:, 4], sm[:, 4], ACT.Sin).then_inc(g["act_trig"], 1)
            act.activation(sm[:, 5], sm[:, 5], ACT.Sin).then_inc(g["act_trig"], 1)

            def norm(m, gain):
                if m == 0:
                    act.wait_ge(g["x_in"], 16)
                else:
                    act.wait_ge(g["acc_read"] if m % 2 == 0 else S_["dve_wo"], {1: 4, 2: 4, 3: 8, 4: 4 + 4 * NE}[m])
                for a in range(TT):
                    act.activation(hn[:, a], x_sb[:, a], ACT.Square, accum_out=st[:, m, 0, a:a + 1]).then_inc(S_["act_ss"], 1)
                act.wait_ge(S_["dve_rv"], m * PER["dve_rv"] + 1)
                act.activation(st[:, m, 2], st[:, m, 1], ACT.Sqrt).then_inc(S_["act_sd"], 1)
                act.wait_ge(S_["act_sd"], m * PER["act_sd"] + 1)
                act.activation(hn[:, 1], x_sb[:, 1], ACT.Copy, scale=st[:, m, 2, 1:2]).then_inc(S_["act_hn"], 1)
                if gain is None:
                    return
                act.wait_ge(g["act_params"], 2)
                for b in (2, 3):
                    act.wait_ge(S_["pe_tr"], m * PER["pe_tr"] + b + 1)
                    for a in range(2):
                        k = 2 * b + a
                        act.activation(hT[:, k], halves(b)[:, a], ACT.Copy,
                                       scale=cols[:, m // 2, gain + k:gain + k + 1]).then_inc(S_["act_ht"], 1)

            def gate_sigmoids(l, first, last):
                for n in range(first, last):
                    act.wait_ge(S_["pe_gate"], l * PER["pe_gate"] + n + 1)
                    for a in range(2):
                        i = 2 * n + a
                        act.activation(gates[:, i], halves(6 + n % 2)[:, a], ACT.Sigmoid,
                                       bias=cols[:, l, BI + 6 + i:BI + 7 + i]).then_inc(S_["act_gate"], 1)

            def mats(l, half):
                for n in range(4):
                    act.wait_ge(S_["pe_mats"], l * PER["pe_mats"] + 4 * half + n + 1)
                    if half and n < 2:
                        act.wait_ge(S_["pe_bu"], l * PER["pe_bu"] + 2)
                    if half and n >= 2:
                        act.wait_ge(S_["pe_y"], l * PER["pe_y"] + 1)
                    dst = (b_mat if n < 2 else c_mat)[:, n % 2].rearrange("p j n -> p (j n)")
                    act.activation(dst, bank[n][:, :], ACT.Copy).then_inc(S_["act_mats"], 1)

            def exps(l, grp):
                act.wait_ge(S_["dve_max"], l * PER["dve_max"] + grp + 1)
                if grp:
                    act.wait_ge(S_["pe_pt"], l * PER["pe_pt"] + 4)
                for h in range(4):
                    s = bank[h]
                    act.activation(probs[:, h, 0:P], s[:, 0:P], ACT.Exp, bias=att_max[:, 0, h:h + 1], scale=0.125,
                                   accum_out=att_sum[:, 0, h:h + 1]).then_inc(S_["act_exp"], 1)
                    act.activation(probs[:, h, P:384], s[:, P:384], ACT.Exp, bias=att_max[:, 1, h:h + 1], scale=0.125,
                                   accum_out=att_sum[:, 1, h:h + 1]).then_inc(S_["act_exp"], 1)

            def probs_out(l, grp):
                for h in range(4):
                    act.wait_ge(S_["pe_pt"], l * PER["pe_pt"] + 4 * grp + h + 1)
                    if grp:
                        act.wait_ge(S_["pe_att"], l * PER["pe_att"] + 2)
                    act.activation(probsT[:, h], bank[h][:, 0:384], ACT.Copy).then_inc(S_["act_pt"], 1)

            for l in range(DEPTH):
                norm(2 * l, GM)
                for b in range(4):
                    act.wait_ge(S_["pe_proj"], l * PER["pe_proj"] + b + 1)
                    for a in range(2):
                        j = 2 * (b % 2) + a
                        src = halves(4 + b)[:, a]
                        if b < 2:
                            act.activation(qT[:, j], src, ACT.Identity,
                                           bias=cols[:, l, QK + j:QK + j + 1]).then_inc(S_["act_qk"], 1)
                        else:
                            if b == 2 and a == 0:
                                act.wait_ge(g["pool_const"], 4)
                            for o in range(2):
                                r = slice(64 * o, 64 * o + 64)
                                act.activation(k_pad[r, 2 * j + o], src[r], ACT.Identity,
                                               bias=cols[r, l, QK + 4 + j:QK + 5 + j]).then_inc(S_["act_qk"], 1)
                act.wait_ge(S_["dve_fz"], l * PER["dve_fz"] + 2)
                act.activation(fz[:, 1], fz[:, 1], ACT.Exp, scale=-1.0).then_inc(S_["act_f"], 1)
                act.wait_ge(S_["act_f"], l * PER["act_f"] + 1)
                act.activation(fz[:, 1], fz[:, 1], ACT.Ln, bias=1.0).then_inc(S_["act_f"], 1)
                act.wait_ge(S_["pe_proj"], l * PER["pe_proj"] + 10)
                for a in range(2):
                    act.activation(conv_sig[:, a], halves(5)[:, a], ACT.Sigmoid,
                                   bias=cols[:, l, BI + 4 + a:BI + 5 + a]).then_inc(S_["act_cg"], 1)
                mats(l, 0)
                exps(l, 0)
                gate_sigmoids(l, 0, 4)
                probs_out(l, 0)
                gate_sigmoids(l, 4, 6)
                mats(l, 1)
                exps(l, 1)
                gate_sigmoids(l, 6, 10)
                probs_out(l, 1)
                gate_sigmoids(l, 10, 12)
                act.wait_ge(S_["dve_ln"], l * PER["dve_ln"] + 3)
                act.activation(ln_r[:], ln_r[:], ACT.Sqrt).then_inc(S_["act_ln"], 1)
                act.wait_ge(S_["dve_ln"], l * PER["dve_ln"] + 4)
                for a in range(2):
                    act.activation(conv_sig[:, a], conv_acc[:, a], ACT.Silu, scale=cols[:, l, LG + a:LG + a + 1],
                                   bias=cols[:, l, LB + a:LB + a + 1]).then_inc(S_["act_conv"], 1)
                act.wait_ge(S_["dve_z"], l * PER["dve_z"] + 2)
                act.activation(ssm_g[:], ssm_z[:], ACT.Gelu_apprx_tanh).then_inc(S_["act_gelu"], 1)
                act.wait_ge(S_["pe_glu"], l * PER["pe_glu"] + 2)
                act.activation(ssm_sig[:], halves(5)[:, :], ACT.Sigmoid).then_inc(S_["act_glu"], 1)

                norm(2 * l + 1, GF)
                if l == 0:
                    for f in range(N_FF):
                        act.wait_ge(g["ffn_up_done"], f + 1)
                        if f >= 2:
                            act.wait_ge(g["ffn_hidden"], f - 1)
                        act.activation(silu_g[:, f % 2], halves(4 + f % 4)[:, 0], ACT.Silu).then_inc(g["ffn_act_silu"], 1)
                else:
                    act.wait_ge(g["router_read"], 3)
                    act.activation(rt[:, :, 1:2], rt[:, :, 0:1], ACT.Exp).then_inc(g["act_top"], 1)
                    with act.Fori(0, NE) as e:
                        for f in range(N_FE):
                            act.wait_ge(g["ffn_up_done"], e * N_FE + (N_FF + f + 1))
                            act.wait_ge(g["ffn_hidden"], e * N_FE + (N_FF + f - 1))
                            act.activation(silu_g[:, f % 2], halves(4 + f % 4)[:, 0],
                                           ACT.Silu).then_inc(g["ffn_act_silu"], 1)
            norm(4, None)

        @block.vector
        def _(dve):
            counts = {}

            def step(ins, sem=g["dve_order"]):
                counts[id(sem)] = counts.get(id(sem), 0) + 1
                ins.then_inc(sem, 1)
                dve.wait_ge(sem, counts[id(sem)])

            step(dve.memset(wf[:], 0.0), g["dve_const"])
            step(dve.memset(bf[:], 0.0), g["dve_const"])
            step(dve.memset(mean_mat[:], 1.0 / CW), g["dve_const"])
            step(dve.memset(ones_row[:], 1.0), g["dve_const"])
            step(dve.memset(ones_col[:], 1.0))
            step(dve.memset(f_left[:], 0.0))
            step(dve.memset(f_right[:], 0.0))

            dve.wait_ge(g["states_in"], 48)
            step(dve.tensor_copy(ldt_row[:].rearrange("r (a s) -> r a s", a=2),
                                 ldt[:].rearrange("r (a o) -> r a o", o=1).to_broadcast([16, 2, S])), g["dve_const"])
            dve.wait_ge(g["pe_params"], 3)
            step(dve.tensor_copy(scol[:], bank[5][:, 0:48]))
            a_re, a_im = scol[:, 0:SC], scol[:, SC:2 * SC]
            step(dve.tensor_copy(sm[:, 0], scol[:, 2 * SC:3 * SC]), g["dve_theta"])
            dve.wait_ge(g["act_trig"], 1)
            step(dve.tensor_tensor(sm[:, 3], a_re, sm[:, 0], ALU.mult))
            step(dve.tensor_tensor(sm[:, 1], a_im, sm[:, 0], ALU.mult))
            step(dve.tensor_scalar(sm[:, 2], sm[:, 1], 1.0 / TWO_PI, ROUND_MAGIC, ALU.mult, ALU.add))
            step(dve.tensor_scalar(sm[:, 2], sm[:, 2], ROUND_MAGIC, None, ALU.subtract))
            for part in (TWO_PI_A, TWO_PI_B, TWO_PI_C):
                step(dve.scalar_tensor_tensor(sm[:, 1], sm[:, 2], -part, sm[:, 1], ALU.mult, ALU.add))
            step(dve.tensor_scalar(sm[:, 4], sm[:, 1], 3.1415925, -3.1415925, ALU.min, ALU.max))
            step(dve.scalar_tensor_tensor(sm[:, 5], sm[:, 4], -1.0, sm[:, 4], ALU.mult, ALU.max))
            step(dve.tensor_scalar(sm[:, 5], sm[:, 5], -1.0, TWO_PI / 4, ALU.mult, ALU.add), g["dve_theta"])
            dve.wait_ge(g["act_trig"], 4)
            step(dve.tensor_copy(rot_pow[:, 0, 0], sm[:, 5]))
            step(dve.tensor_copy(rot_pow[:, 1, 0], sm[:, 4]))
            step(dve.tensor_tensor(sm[:, 5], sm[:, 5], sm[:, 3], ALU.mult))
            step(dve.tensor_scalar(sm[:, 5], sm[:, 5], 1.0, None, ALU.subtract))
            step(dve.tensor_tensor(sm[:, 6], sm[:, 4], sm[:, 3], ALU.mult))
            step(dve.tensor_tensor(sm[:, 7], a_re, a_re, ALU.mult))
            step(dve.tensor_tensor(sm[:, 8], a_im, a_im, ALU.mult))
            step(dve.tensor_tensor(sm[:, 7], sm[:, 7], sm[:, 8], ALU.add))
            step(dve.reciprocal(sm[:, 7], sm[:, 7]))
            step(dve.tensor_tensor(sm[:, 8], sm[:, 5], a_re, ALU.mult))
            step(dve.tensor_tensor(sm[:, 9], sm[:, 6], a_im, ALU.mult))
            step(dve.tensor_tensor(sm[:, 8], sm[:, 8], sm[:, 9], ALU.add))
            step(dve.tensor_tensor(sm[:, 10], sm[:, 8], sm[:, 7], ALU.mult))
            step(dve.tensor_tensor(sm[:, 8], sm[:, 6], a_re, ALU.mult))
            step(dve.tensor_tensor(sm[:, 9], sm[:, 5], a_im, ALU.mult))
            step(dve.tensor_tensor(sm[:, 8], sm[:, 8], sm[:, 9], ALU.subtract))
            step(dve.tensor_tensor(sm[:, 11], sm[:, 8], sm[:, 7], ALU.mult))
            for n in range(7):
                zr, zi = rot_pow[:, 0, n], rot_pow[:, 1, n]
                step(dve.tensor_tensor(sm[:, 12], zr, zr, ALU.mult))
                step(dve.tensor_tensor(sm[:, 13], zi, zi, ALU.mult))
                step(dve.tensor_tensor(rot_pow[:, 0, n + 1], sm[:, 12], sm[:, 13], ALU.subtract))
                step(dve.scalar_tensor_tensor(rot_pow[:, 1, n + 1], zr, 2.0, zi, ALU.mult, ALU.mult),
                     g["dve_states"] if n == 6 else g["dve_order"])

            def norm(m, gain):
                dve.wait_ge(S_["act_ss"], m * PER["act_ss"] + 2)
                step(dve.tensor_scalar(st[:, m, 1], st[:, m, 0], 1.0 / D, EPS, ALU.mult, ALU.add))
                step(dve.reciprocal(st[:, m, 1], st[:, m, 1]), S_["dve_rv"])
                dve.wait_ge(S_["act_sd"], m * PER["act_sd"] + 1)
                step(dve.tensor_scalar(hn[:, 0], x_sb[:, 0], st[:, m, 2, 0:1], None, ALU.mult), S_["dve_hn"])
                if gain is None:
                    return
                dve.wait_ge(g["act_params"], 2)
                for b in (0, 1):
                    dve.wait_ge(S_["pe_tr"], m * PER["pe_tr"] + b + 1)
                    for a in range(2):
                        k = 2 * b + a
                        step(dve.tensor_scalar(hT[:, k], halves(b)[:, a], cols[:, m // 2, gain + k:gain + k + 1],
                                               None, ALU.mult), S_["dve_ht"])

            def rotate_scan(l, pair):
                half, q = pair // 2, pair % 2
                dve.wait_ge(S_["pool_phase"], l * PER["pool_phase"] + half + 1)
                dve.wait_ge(S_["pe_bu"], l * PER["pe_bu"] + pair + 1)
                if pair == 2:
                    dve.wait_ge(S_["pe_y"], l * PER["pe_y"] + 1)
                re, im = halves(4)[:, :], halves(5)[:, :]
                c_, s_ = (phase[:, c, 2 * q:2 * q + 2] for c in range(2))
                y_re, y_im = (state[:, c, 2 * q:2 * q + 2] for c in range(2))
                step(dve.tensor_tensor(rot_tmp[:, 0], re, c_, ALU.mult))
                step(dve.tensor_tensor(rot_tmp[:, 1], im, s_, ALU.mult))
                step(dve.tensor_tensor(y_re, rot_tmp[:, 0], rot_tmp[:, 1], ALU.add))
                step(dve.tensor_tensor(rot_tmp[:, 0], im, c_, ALU.mult))
                step(dve.tensor_tensor(rot_tmp[:, 1], re, s_, ALU.mult))
                step(dve.tensor_tensor(y_im, rot_tmp[:, 0], rot_tmp[:, 1], ALU.subtract), S_["dve_bu"])
                for c in range(2):
                    for a in range(2):
                        j = l * NJ + 2 * pair + a
                        y = state[:, c, 2 * q + a]
                        step(dve.tensor_tensor_scan(y, sm[:, 3, j:j + 1].to_broadcast([P, T]), y, 0.0,
                                                    ALU.mult, ALU.add),
                             S_["dve_scan"] if c and a else g["dve_order"])

            def softmax_max(l, grp):
                dve.wait_ge(S_["pe_s"], l * PER["pe_s"] + 4 * grp + 4)
                if grp:
                    dve.wait_ge(S_["act_exp"], l * PER["act_exp"] + 8)
                for h in range(4):
                    step(dve.reduce_max(att_max[:, 0, h:h + 1], bank[h][:, 0:P], AX_X))
                    step(dve.reduce_max(att_max[:, 1, h:h + 1], bank[h][:, P:384], AX_X))
                step(dve.tensor_scalar(att_max[:], att_max[:], -0.125, None, ALU.mult), S_["dve_max"])

            def forget_right(l, grp):
                for h in range(4):
                    hd = 4 * grp + h
                    step(dve.tensor_scalar(f_right[0:64, h], f_sum[:], f_scale[:, hd:hd + 1], f_shift[:, hd:hd + 1],
                                           ALU.mult, ALU.add), S_["dve_f"])

            def softmax_norm(l, grp):
                dve.wait_ge(S_["act_exp"], l * PER["act_exp"] + 8 * grp + 8)
                step(dve.reciprocal(att_rs[:], att_sum[:]))
                for o, (a, b) in enumerate(((0, P), (P, 384))):
                    step(dve.tensor_tensor(probs[:, :, a:b], probs[:, :, a:b],
                                           att_rs[:, o].rearrange("p (h o) -> p h o", o=1).to_broadcast([P, 4, b - a]),
                                           ALU.mult), S_["dve_p"])

            def attention_out(l, grp):
                for q in range(2):
                    dve.wait_ge(S_["pe_att"], l * PER["pe_att"] + 2 * grp + q + 1)
                    for o in range(2):
                        r = slice(64 * o, 64 * o + 64)
                        j = 2 * grp + q
                        step(dve.tensor_scalar(attT[r, j], halves(q)[r, o], cols[r, l, QK + 8 + j:QK + 9 + j], None,
                                               ALU.add), S_["dve_att"])

            def conv_taps(l, a):
                w = lambda k: cols[:, l, CWC + 2 * k + a:CWC + 2 * k + a + 1]
                step(dve.tensor_scalar(conv_acc[:, a], conv_in[:, a, 0:T], w(0), cols[:, l, CB + a:CB + a + 1],
                                       ALU.mult, ALU.add))
                for k in range(1, CK):
                    step(dve.scalar_tensor_tensor(conv_acc[:, a], conv_in[:, a, k:k + T], w(k), conv_acc[:, a],
                                                  ALU.mult, ALU.add), S_["dve_conv"] if k == CK - 1 else g["dve_order"])

            def ssm_out(l, half):
                dve.wait_ge(S_["pe_y"], l * PER["pe_y"] + half + 1)
                step(dve.scalar_tensor_tensor(ssm_z[:, half], uT[:, half], cols[:, l, SD + half:SD + half + 1],
                                              halves(4)[:, 0], ALU.mult, ALU.add), S_["dve_z"])

            for l in range(DEPTH):
                norm(2 * l, GM)
                for a in range(TT):
                    dve.wait_ge(S_["pe_proj"], l * PER["pe_proj"] + 5 + a)
                    step(dve.tensor_copy(v_sb[:, a], bank[a][:, :]), S_["dve_v"])
                dve.wait_ge(S_["pe_proj"], l * PER["pe_proj"] + 7)
                dve.wait_ge(g["side_in"], 16 * (6 + 4 * l))
                step(dve.tensor_scalar(fz[:, 0], bank[2][0:64, 0:T], bf[:, l:l + 1], None, ALU.add), S_["dve_fz"])
                step(dve.scalar_tensor_tensor(fz[:, 1], fz[:, 0], -1.0, fz[:, 0], ALU.mult, ALU.max), S_["dve_fz"])
                dve.wait_ge(S_["pe_proj"], l * PER["pe_proj"] + 8)
                for a in range(2):
                    step(dve.tensor_scalar(uT[:, a], halves(3)[:, a], cols[:, l, BI + a:BI + a + 1], None, ALU.add),
                         S_["dve_u"])
                dve.wait_ge(S_["act_f"], l * PER["act_f"] + 2)
                step(dve.scalar_tensor_tensor(fz[:, 0], fz[:, 0], 0.0, fz[:, 1], ALU.min, ALU.subtract))
                dve.wait_ge(g["pool_const"], 3)
                step(dve.tensor_tensor_scan(f_sum[:], ones_col[:].to_broadcast([64, T]), fz[:, 0], 0.0,
                                            ALU.mult, ALU.add))
                step(dve.tensor_scalar(f_left[0:64], f_sum[:], f_scale[:, H:H + 1], f_shift[:, H:H + 1],
                                       ALU.mult, ALU.add), S_["dve_f"])
                forget_right(l, 0)
                dve.wait_ge(S_["act_cg"], l * PER["act_cg"] + 2)
                dve.wait_ge(g["pool_const"], 4)
                for a in range(2):
                    step(dve.scalar_tensor_tensor(conv_in[:, a, PAD:PAD + T], halves(4)[:, a],
                                                  cols[:, l, BI + 2 + a:BI + 3 + a], conv_sig[:, a],
                                                  ALU.add, ALU.mult), S_["dve_cv"])
                rotate_scan(l, 0)
                softmax_max(l, 0)
                softmax_norm(l, 0)
                forget_right(l, 1)
                rotate_scan(l, 1)
                conv_taps(l, 0)
                attention_out(l, 0)
                ssm_out(l, 0)
                rotate_scan(l, 2)
                softmax_max(l, 1)
                softmax_norm(l, 1)
                rotate_scan(l, 3)
                conv_taps(l, 1)
                attention_out(l, 1)
                for a in range(2):
                    if a == 0:
                        dve.wait_ge(S_["pe_ln"], l * PER["pe_ln"] + 1)
                    step(dve.tensor_tensor(conv_acc[:, a], conv_acc[:, a], halves(6)[:, 0], ALU.subtract))
                step(dve.tensor_tensor(conv_sig[:], conv_acc[:], conv_acc[:], ALU.mult), S_["dve_ln"])
                dve.wait_ge(S_["pe_ln"], l * PER["pe_ln"] + 2)
                step(dve.tensor_scalar(ln_r[:], halves(7)[:, 0], EPS, None, ALU.add), S_["dve_ln"])
                step(dve.reciprocal(ln_r[:], ln_r[:]), S_["dve_ln"])
                dve.wait_ge(S_["act_ln"], l * PER["act_ln"] + 1)
                for a in range(2):
                    last = dve.tensor_tensor(conv_acc[:, a], conv_acc[:, a], ln_r[:], ALU.mult)
                    step(last, S_["dve_ln"] if a else g["dve_order"])
                ssm_out(l, 1)
                dve.wait_ge(S_["act_glu"], l * PER["act_glu"] + 1)
                step(dve.tensor_tensor(ssm_z[:], halves(4)[:, :], ssm_sig[:], ALU.mult), S_["dve_glu"])
                for i in range(4):
                    b0 = 3 * (i % 2)
                    gt = [gates[:, 8 * b + 2 * i:8 * b + 2 * i + 2] for b in range(3)]
                    m_ = merged[:, 2 * i:2 * i + 2]
                    dve.wait_ge(S_["act_gate"], l * PER["act_gate"] + 24)
                    dve.wait_ge(S_["pe_out"], l * PER["pe_out"] + 3 * i + 1)
                    step(dve.tensor_tensor(m_, halves(b0)[:, :], gt[0], ALU.mult))
                    dve.wait_ge(S_["pe_out"], l * PER["pe_out"] + 3 * i + 2)
                    step(dve.tensor_tensor(rot_tmp[:, 0], halves(b0 + 1)[:, :], gt[1], ALU.mult))
                    dve.wait_ge(S_["pe_out"], l * PER["pe_out"] + 3 * i + 3)
                    step(dve.tensor_tensor(rot_tmp[:, 1], halves(b0 + 2)[:, :], gt[2], ALU.mult))
                    step(dve.tensor_tensor(m_, m_, rot_tmp[:, 0], ALU.add))
                    step(dve.tensor_tensor(m_, m_, rot_tmp[:, 1], ALU.add), S_["dve_merge"])
                dve.wait_ge(S_["pe_wo"], l * PER["pe_wo"] + 2)
                for n, b in enumerate((6, 7, 0, 1)):
                    xs = x_sb[:, n // 2, (n % 2) * 512:(n % 2 + 1) * 512]
                    step(dve.tensor_tensor(xs, xs, bank[b][:, :], ALU.add), S_["dve_wo"])

                norm(2 * l + 1, GF)
                if l == 0:
                    for f in range(N_FF):
                        dve.wait_ge(g["ffn_act_silu"], f + 1)
                        if f >= 4:
                            dve.wait_ge(g["ffn_down_done"], f - 3)
                        dve.tensor_tensor(hidden[:, f % 4], silu_g[:, f % 2], halves(4 + f % 4)[:, 1],
                                          ALU.mult).then_inc(g["ffn_hidden"], 1)
                    dve.wait_ge(g["ffn_down_done"], N_FF)
                    for n in range(4):
                        xs = x_sb[:, n // 2, (n % 2) * 512:(n % 2 + 1) * 512]
                        step(dve.tensor_tensor(xs, xs, bank[n][:, :], ALU.add), g["acc_read"])
                else:
                    dve.wait_ge(g["pe_router"], 2)
                    for a in range(TT):
                        step(dve.tensor_copy(logits[:, a], bank[4 + a][:, 0:NE]), g["router_read"])
                        step(dve.max(top[:, a], logits[:, a]))
                        step(dve.max_index(top_at[:, a], top[:, a], logits[:, a]))
                    step(dve.tensor_copy(top_f[:], top_at[:]))
                    r_ = [rt[:, :, k:k + 1] for k in range(4)]
                    step(dve.tensor_tensor(r_[0], top[:, :, 1:2], top[:, :, 0:1], ALU.subtract), g["router_read"])
                    dve.wait_ge(g["act_top"], 1)
                    step(dve.tensor_scalar(r_[2], r_[1], 1.0, None, ALU.add))
                    step(dve.reciprocal(r_[2], r_[2]))
                    step(dve.tensor_tensor(r_[3], r_[1], r_[2], ALU.mult))
                    for a in range(TT):
                        step(dve.tensor_scalar(w_exp[:, a], e_iota[:], top_f[:, a, 0:1], rt[:, a, 2:3],
                                               ALU.is_equal, ALU.mult))
                        step(dve.tensor_scalar(w_tmp[:, a], e_iota[:], top_f[:, a, 1:2], rt[:, a, 3:4],
                                               ALU.is_equal, ALU.mult))
                    step(dve.tensor_tensor(w_exp[:], w_exp[:], w_tmp[:], ALU.add))
                    with dve.Fori(0, NE) as e:
                        for f in range(N_FE):
                            dve.wait_ge(g["ffn_act_silu"], e * N_FE + (N_FF + f + 1))
                            dve.wait_ge(g["ffn_down_done"], e * N_FE + (N_FF + f - 3))
                            dve.tensor_tensor(hidden[:, f % 4], silu_g[:, f % 2], halves(4 + f % 4)[:, 1],
                                              ALU.mult).then_inc(g["ffn_hidden"], 1)
                        dve.wait_ge(g["ffn_down_done"], e * N_FE + (N_FF + N_FE))
                        dve.wait_ge(g["acc_read"], e * 4 + 4)
                        for n in range(4):
                            a = n // 2
                            xs = x_sb[:, a, (n % 2) * 512:(n % 2 + 1) * 512]
                            dve.scalar_tensor_tensor(xs, bank[n][:, :], w_exp[:, a, bass.ds(e, 1)], xs,
                                                     ALU.mult, ALU.add).then_inc(g["acc_read"], 1)
            dve.wait_ge(g["acc_read"], 4 + 4 * NE)
            norm(4, None)
            dve.wait_ge(S_["act_hn"], 5)
            dve.wait_ge(g["gain_in"], 16)
            for a in range(TT):
                step(dve.tensor_tensor(hn[:, a], hn[:, a], g_final, ALU.mult), g["final_in"] if a else g["dve_order"])

        @block.tensor
        def _(pe):
            pe.wait_ge(g["pool_const"], 1)
            pe.wait_ge(g["rows_in"], 9 * 16 * DEPTH)
            for l in range(DEPTH):
                pe.transpose(bank[7 - l][:, 0:NROW], rows[0:NROW, l], ident[0:NROW, 0:NROW]).then_inc(g["pe_params"], 1)
            pe.wait_ge(g["states_in"], 48)
            pe.transpose(bank[5][:, 0:32], srow[:], ident[0:32, 0:32])
            pe.wait_ge(g["dve_const"], 5)
            pe.transpose(bank[5][:, 32:48], ldt_row[:], ident[0:16, 0:16]).then_inc(g["pe_params"], 1)

            def arrived(n):
                pe.wait_ge(slot_full[n % RING], full_at[n])

            def weights(n, k, w, first=0):
                return slot(n % RING, k, w, first)

            def product(o, lhs, rhs, n, first=True, last=True):
                for k in range(n):
                    ins = pe.matmul(o, lhs(k), rhs(k), start=(first and k == 0), stop=(last and k == n - 1))
                return ins

            def feature_tile(o, w, c):
                return product(o, lambda k: w[:, k, c:c + P], lambda k: hT[:, k], KT)

            def norm(m):
                pe.wait_ge(S_["dve_hn"], m * PER["dve_hn"] + 1)
                pe.wait_ge(S_["act_hn"], m * PER["act_hn"] + 1)
                for b in range(4):
                    for a in range(2):
                        for tt in range(TT):
                            k = 2 * b + a
                            ins = pe.transpose(halves(b)[:, a, tt * P:(tt + 1) * P], hn[:, tt, k * P:(k + 1) * P], ident[:])
                    ins.then_inc(S_["pe_tr"], 1)
                pe.wait_ge(S_["dve_ht"], m * PER["dve_ht"] + 4)
                pe.wait_ge(S_["act_ht"], m * PER["act_ht"] + 4)

            def gate_jobs(l, first, last):
                for n in range(first, last):
                    ld = mix_at[l] + 5 + n // 2
                    if n % 2 == 0:
                        arrived(ld)
                    if n < 2:
                        pe.wait_ge(S_["act_qk"], l * PER["act_qk"] + 12)
                    else:
                        pe.wait_ge(S_["act_gate"], l * PER["act_gate"] + 2 * n - 2)
                    w = weights(ld, KT, 512)
                    for a in range(2):
                        ins = feature_tile(halves(6 + n % 2)[:, a], w, (2 * n + a) % 4 * P)
                    ins.then_inc(S_["pe_gate"], 1)

            def mats(l, half):
                if half == 0:
                    pe.wait_ge(S_["dve_v"], l * PER["dve_v"] + 2)
                    pe.wait_ge(S_["dve_u"], l * PER["dve_u"] + 2)
                else:
                    pe.wait_ge(S_["dve_att"], l * PER["dve_att"] + 4)
                    pe.wait_ge(S_["act_pt"], l * PER["act_pt"] + 4)
                for n in range(4):
                    pe.wait_ge(S_["pool_mats"], l * PER["pool_mats"] + 4 * half + n + 1)
                    for j in range(HJ):
                        ins = pe.transpose(bank[n][:, j * P:(j + 1) * P], mat_src[:, n, j * P:(j + 1) * P], ident[:])
                    ins.then_inc(S_["pe_mats"], 1)

            def states_in(l, pair):
                half, q = pair // 2, pair % 2
                pe.wait_ge(S_["act_mats"], l * PER["act_mats"] + 4 * half + 2)
                if pair == 0:
                    pe.wait_ge(S_["dve_cv"], l * PER["dve_cv"] + 2)
                    pe.wait_ge(S_["act_cg"], l * PER["act_cg"] + 2)
                else:
                    pe.wait_ge(S_["dve_bu"], l * PER["dve_bu"] + pair)
                if pair == 2:
                    pe.wait_ge(S_["dve_z"], l * PER["dve_z"] + 1)
                for c in range(2):
                    for a in range(2):
                        ins = pe.matmul(halves(4 + c)[:, a], b_mat[:, c, 2 * q + a], uT[:, half], start=True, stop=True)
                ins.then_inc(S_["pe_bu"], 1)

            def states_out(l, half):
                pe.wait_ge(S_["pool_back"], l * PER["pool_back"] + 2 * half + 2)
                pe.wait_ge(S_["dve_bu"], l * PER["dve_bu"] + 2 * half + 2)
                pe.wait_ge(S_["act_mats"], l * PER["act_mats"] + 4 * half + 4)
                for c in range(2):
                    ins = product(halves(4)[:, 0], lambda j: c_mat[:, c, j], lambda j: state[:, c, j], HJ,
                                  first=(c == 0), last=(c == 1))
                ins.then_inc(S_["pe_y"], 1)

            def scores(l, grp):
                pe.wait_ge(S_["act_qk"], l * PER["act_qk"] + 12)
                pe.wait_ge(S_["dve_f"], l * PER["dve_f"] + 5 + 4 * grp)
                pe.wait_ge(S_["act_mats"], l * PER["act_mats"] + 4 * grp + 4)
                for h in range(4):
                    hd = 4 * grp + h
                    for q, at_, n in ((0, 0, P), (1, P, T)):
                        o = bank[h][:, at_:at_ + n]
                        pe.matmul(o, qT[:, hd // 2, q * P:(q + 1) * P], k_pad[:, hd, 0:n], start=True, stop=False)
                        pe.matmul(o, f_left[:, q * P:(q + 1) * P], f_right[:, h, 0:n], start=False, stop=False)
                        ins = pe.matmul(bank[h][:, at_ + n - P:at_ + n], ident[:], causal[:], start=False, stop=True)
                    ins.then_inc(S_["pe_s"], 1)

            def probs_transposed(l, grp):
                pe.wait_ge(S_["dve_p"], l * PER["dve_p"] + 2 * grp + 2)
                for h in range(4):
                    for n in range(3):
                        ins = pe.transpose(bank[h][:, n * P:(n + 1) * P], probs[:, h, n * P:(n + 1) * P], ident[:])
                    ins.then_inc(S_["pe_pt"], 1)

            def attention(l, grp):
                pe.wait_ge(S_["act_pt"], l * PER["act_pt"] + 4 * grp + 4)
                for q in range(2):
                    j = 2 * grp + q
                    for o in range(2):
                        h = 2 * q + o
                        pe.matmul(halves(q)[:, o], v_sb[:, 0, j * P:(j + 1) * P], probsT[:, h, 0:T], start=True, stop=False)
                        ins = pe.matmul(halves(q)[:, o, P:T], v_sb[:, 1, j * P:(j + 1) * P], probsT[:, h, T:384],
                                        start=False, stop=True)
                    ins.then_inc(S_["pe_att"], 1)

            for l in range(DEPTH):
                m0 = mix_at[l]
                norm(2 * l)
                if l == 0:
                    pe.wait_ge(g["dve_theta"], 1)
                for b in range(4):
                    if b % 2 == 0:
                        arrived(m0 + b // 2)
                    w = weights(m0 + b // 2, KT, 512)
                    for a in range(2):
                        ins = feature_tile(halves(4 + b)[:, a], w, (2 * (b % 2) + a) * P)
                    ins.then_inc(S_["pe_proj"], 1)
                arrived(m0 + 2)
                w = weights(m0 + 2, KT, AW)
                for a in range(TT):
                    ins = product(bank[a][:, :], lambda k: hT[:, k, a * P:(a + 1) * P], lambda k: w[:, k], KT)
                    ins.then_inc(S_["pe_proj"], 1)
                pe.wait_ge(g["side_in"], 16 * (6 + 4 * l))
                product(bank[2][0:64, 0:T], lambda k: wf[:, k], lambda k: hT[:, k], KT).then_inc(S_["pe_proj"], 1)
                arrived(m0 + 3)
                w = weights(m0 + 3, KT, 256)
                for a in range(2):
                    ins = feature_tile(halves(3)[:, a], w, a * P)
                ins.then_inc(S_["pe_proj"], 1)
                arrived(m0 + 4)
                pe.wait_ge(S_["act_qk"], l * PER["act_qk"] + 4)
                w = weights(m0 + 4, KT, 512)
                for b in range(2):
                    for a in range(2):
                        ins = feature_tile(halves(4 + b)[:, a], w, (2 * b + a) * P)
                    ins.then_inc(S_["pe_proj"], 1)
                mats(l, 0)
                states_in(l, 0)
                scores(l, 0)
                gate_jobs(l, 0, 2)
                states_in(l, 1)
                gate_jobs(l, 2, 4)
                probs_transposed(l, 0)
                gate_jobs(l, 4, 6)
                attention(l, 0)
                states_out(l, 0)
                mats(l, 1)
                states_in(l, 2)
                scores(l, 1)
                gate_jobs(l, 6, 8)
                states_in(l, 3)
                gate_jobs(l, 8, 10)
                probs_transposed(l, 1)
                gate_jobs(l, 10, 12)
                attention(l, 1)
                pe.wait_ge(S_["act_gate"], l * PER["act_gate"] + 24)
                pe.wait_ge(S_["dve_conv"], l * PER["dve_conv"] + 2)
                product(halves(6)[:, 0], lambda k: mean_mat[:], lambda k: conv_acc[:, k], 2).then_inc(S_["pe_ln"], 1)
                states_out(l, 1)
                pe.wait_ge(S_["dve_ln"], l * PER["dve_ln"] + 1)
                product(halves(7)[:, 0], lambda k: mean_mat[:], lambda k: conv_sig[:, k], 2).then_inc(S_["pe_ln"], 1)
                arrived(m0 + 11)
                pe.wait_ge(S_["act_gelu"], l * PER["act_gelu"] + 1)
                pe.wait_ge(S_["dve_z"], l * PER["dve_z"] + 2)
                w = weights(m0 + 11, 2, 512)
                for b in range(2):
                    for a in range(2):
                        ins = product(halves(4 + b)[:, a], lambda k: w[:, k, (2 * b + a) * P:(2 * b + a + 1) * P],
                                      lambda k: ssm_g[:, k], 2)
                    ins.then_inc(S_["pe_glu"], 1)
                arrived(m0 + 12)
                arrived(m0 + 13)
                wa, ws, wc = weights(m0 + 12, 4, D), weights(m0 + 13, 2, D), weights(m0 + 13, 2, D, 2 * D)
                pe.wait_ge(S_["dve_att"], l * PER["dve_att"] + 8)
                pe.wait_ge(S_["act_pt"], l * PER["act_pt"] + 8)
                for i in range(4):
                    b0 = 3 * (i % 2)
                    if i >= 2:
                        pe.wait_ge(S_["dve_merge"], l * PER["dve_merge"] + i - 1)
                    for b, (w, r, n) in enumerate(((wa, attT, 4), (ws, ssm_z, 2), (wc, conv_sig, 2))):
                        if i == 0 and b == 1:
                            pe.wait_ge(S_["dve_glu"], l * PER["dve_glu"] + 1)
                        if i == 0 and b == 2:
                            pe.wait_ge(S_["act_conv"], l * PER["act_conv"] + 2)
                        for a in range(2):
                            c = (2 * i + a) * P
                            ins = product(halves(b0 + b)[:, a], lambda k: w[:, k, c:c + P], lambda k: r[:, k], n)
                        ins.then_inc(S_["pe_out"], 1)
                arrived(m0 + 14)
                arrived(m0 + 15)
                pe.wait_ge(S_["dve_merge"], l * PER["dve_merge"] + 4)
                for kk in range(2):
                    w = weights(m0 + 14 + kk, 4, D)
                    for k in range(4):
                        for n, b in enumerate((6, 7, 0, 1)):
                            a, h = n // 2, n % 2
                            ins = pe.matmul(bank[b][:, :], merged[:, 4 * kk + k, a * P:(a + 1) * P],
                                            w[:, k, h * 512:(h + 1) * 512], start=(kk + k == 0), stop=(kk == 1 and k == 3))
                    ins.then_inc(S_["pe_wo"], 1)

                norm(2 * l + 1)

                def down(f, wd, kk, first, last):
                    for n in range(4):
                        a, h = n // 2, n % 2
                        ins = pe.matmul(bank[n][:, :], hidden[:, f % 4, a * P:(a + 1) * P],
                                        wd[:, kk, h * 512:(h + 1) * 512], start=first, stop=last)
                    ins.then_inc(g["ffn_down_done"], 1)
                    return ins

                if l == 0:
                    for f in range(N_FF + 1):
                        if f < N_FF:
                            c, kk = f // 4, f % 4
                            n0 = ffn_at + 3 * c
                            wid = FF_CH[c][1]
                            if kk == 0:
                                arrived(n0)
                                arrived(n0 + 1)
                            if f >= 4:
                                pe.wait_ge(g["ffn_hidden"], f - 3)
                            b = halves(4 + f % 4)
                            ig = feature_tile(b[:, 0], weights(n0, KT, wid), kk * P)
                            iu = feature_tile(b[:, 1], weights(n0 + 1, KT, wid), kk * P)
                            iu.then_inc(g["ffn_up_done"], 1)
                            if kk == wid // P - 1:
                                ig.then_inc(g["gate_used"], 1)
                        if f > 0:
                            p_ = f - 1
                            c, kk = p_ // 4, p_ % 4
                            if kk == 0:
                                arrived(ffn_at + 3 * c + 2)
                            pe.wait_ge(g["ffn_hidden"], p_ + 1)
                            wid = FF_CH[c][1]
                            ins = down(p_, weights(ffn_at + 3 * c + 2, wid // P, D), kk, p_ == 0, p_ == N_FF - 1)
                else:
                    pe.wait_ge(g["side_in"], 16 * 6)
                    for a in range(TT):
                        o = bank[4 + a][:, 0:NE]
                        pe.matmul(o, ones_row[:], b_router[:], start=True, stop=False)
                        product(o, lambda k: hT[:, k, a * P:(a + 1) * P], lambda k: w_router[:, k], KT,
                                first=False).then_inc(g["pe_router"], 1)
                    pe.wait_ge(g["router_read"], 2)
                    with pe.Fori(0, NE) as e:
                        def e_arrived(j):
                            pe.wait_ge(expert_full[j % EXPERT_RING], e * (16 * E_TURNS) + 16 * (j // EXPERT_RING + 1))

                        for f in range(N_FE + 1):
                            if f < N_FE:
                                c, kk = f // 4, f % 4
                                if kk == 0:
                                    e_arrived(3 * c)
                                    e_arrived(3 * c + 1)
                                pe.wait_ge(g["ffn_hidden"], e * N_FE + (N_FF + f - 3))
                                b = halves(4 + f % 4)
                                ig = feature_tile(b[:, 0], slot(3 * c % EXPERT_RING, KT, 512), kk * P)
                                iu = feature_tile(b[:, 1], slot((3 * c + 1) % EXPERT_RING, KT, 512), kk * P)
                                iu.then_inc(g["ffn_up_done"], 1)
                                if kk == 3:
                                    ig.then_inc(g["gate_used"], 1)
                            if f > 0:
                                p_ = f - 1
                                c, kk = p_ // 4, p_ % 4
                                if kk == 0:
                                    e_arrived(3 * c + 2)
                                if p_ == 0:
                                    pe.wait_ge(g["acc_read"], e * 4 + 4)
                                pe.wait_ge(g["ffn_hidden"], e * N_FE + (N_FF + f))
                                down(p_, slot((3 * c + 2) % EXPERT_RING, 4, D), kk, p_ == 0, p_ == N_FE - 1)


_INS = ["x", "g_mix", "w_in", "b_in", "ssm_a_re", "ssm_a_im", "ssm_log_dt", "ssm_b_re", "ssm_b_im", "ssm_c_re",
        "ssm_c_im", "ssm_d", "ssm_w_glu", "conv_w", "conv_b", "conv_ln_g", "conv_ln_b", "w_att_out", "w_ssm_out",
        "w_conv_out", "w_o", "g_ffn", "ffn_w_gate", "ffn_w_up", "ffn_w_down", "moe_w_router", "moe_b_router",
        "moe_w_gate", "moe_w_up", "moe_w_down", "g_final"]


def kernel(**inputs):
    import numpy as np
    import concourse.bacc as bacc
    from concourse.bass_utils import run_bass_kernel_spmd

    nc = bacc.Bacc("TRN2", target_bir_lowering=False, num_devices=1)
    arrays, t = {}, {}
    for name in _INS:
        a = np.ascontiguousarray(inputs[name])
        arrays[f"in_{name}"] = a
        t[name] = nc.dram_tensor(f"in_{name}", a.shape, mybir.dt.from_np(a.dtype), kind="ExternalInput").ap()
    shape = inputs["x"].shape
    out = nc.dram_tensor("out", shape, F32, kind="ExternalOutput").ap()
    hybrid_trunk(nc, t, out)
    return run_bass_kernel_spmd(nc, [arrays], core_ids=[0]).results[0]["out"]
```

```python
from contextlib import ExitStack

import concourse.bass as bass
from concourse import mybir

P = 128
F32 = mybir.dt.float32
U32 = mybir.dt.uint32
F32R = mybir.dt.float32r
ALU = mybir.AluOpType
ACT = mybir.ActivationFunctionType
AX_X = mybir.AxisListType.X

EPS = 1e-6
MASKED = -1e30
TWO_PI = 6.283185307179586
TWO_PI_A = 6.28125
TWO_PI_B = 0.0019340515136718750
TWO_PI_C = TWO_PI - TWO_PI_A - TWO_PI_B
ROUND_MAGIC = 12582912.0

RING = 4
SLOT = 4096
UNIT = 2048
UNIT_RING = 7
SPLIT_RING = 3
MIX_LOADS = 16


def hybrid_trunk(nc, t, out):
    DEPTH, D, N_IN = t["w_in"].shape
    T = t["x"].shape[1]
    KT, TT = D // P, T // P
    G, S, GH = t["ssm_b_re"].shape[1:]
    H = (N_IN - 3 * D - G * GH - 2 * t["conv_w"].shape[2]) // (3 * 64 + 1)
    DH = 64
    AW = H * DH
    V_AT, F_AT = 2 * AW, 3 * AW
    U_AT = F_AT + H
    C_AT = U_AT + G * GH
    CK, CW = t["conv_w"].shape[1:]
    G_AT = C_AT + 2 * CW
    DFF = t["ffn_w_gate"].shape[2]
    NE, _, DFE = t["moe_w_gate"].shape[1:]
    NJ = G * S // P
    HJ = NJ // 2
    PAD = CK - 1
    assert (D, T, AW, G * GH, CW, NJ) == (1024, 256, 512, 256, 256, 8) and DEPTH == 2

    ctx = ExitStack()
    with ctx:
        def sb(name, shape, dt=F32):
            handle = ctx.enter_context(nc.sbuf_tensor(name, shape, dt))
            size = 4
            for n in shape[1:]:
                size *= n
            address[name] = nc.sbuf_base - size
            return handle

        address = {}

        def over(name, shape, dt, where, at=0):
            return nc.alloc_sbuf_tensor_at(name, shape, dt, offset=address[where] + at)

        arena = sb("arena", [P, RING * SLOT + 48 * T])
        at = RING * SLOT
        gates = arena[:, at:at + 24 * T].rearrange("p (n t) -> p n t", t=T)
        at += 24 * T
        phase = arena[:, at:at + 2 * HJ * T].rearrange("p (c j t) -> p c j t", c=2, t=T)
        at += 2 * HJ * T
        state = arena[:, at:at + 2 * HJ * T].rearrange("p (c j t) -> p c j t", c=2, t=T)
        at += 2 * HJ * T
        rot_tmp = arena[:, at:at + 1024].rearrange("p (c j t) -> p c j t", c=2, t=T)
        at += 1024
        back_flat = arena[:, at:at + 1024]
        back_tmp = back_flat.rearrange("p (c j t) -> p c j t", c=2, t=T)
        at += 1024
        assert at == RING * SLOT + 48 * T

        def slot(s, k, n, first=0):
            return arena[:, s * SLOT + first:s * SLOT + first + k * n].rearrange("p (k n) -> p k n", n=n)

        x_sb = sb("x_sb", [P, TT, D])
        hn = sb("hn", [P, TT, D])
        merged = hn[:].rearrange("p a (b t) -> p (a b) t", t=T)
        mat_src = hn[:].rearrange("p a (b n) -> p (a b) n", n=512)
        hT = sb("hT", [P, KT, T])
        qT = sb("qT", [P, AW // P, T])
        k_pad = sb("k_pad", [P, H, T])
        v_sb = sb("v_sb", [P, TT, AW])
        f_left = sb("f_left", [P, T])
        f_right = sb("f_right", [P, 4, T])
        f_sum = sb("f_sum", [64, T])
        probs = sb("probs", [P, 4, 384])
        probsT = sb("probsT", [P, 4, 384])
        attT = sb("attT", [P, AW // P, T])
        uT = sb("uT", [P, 2, T])
        conv_in = sb("conv_in", [P, 2, PAD + T])
        conv_acc = sb("conv_acc", [P, 2, T])
        conv_sig = sb("conv_sig", [P, 2, T])
        ssm_z = uT
        ssm_g = sb("ssm_g", [P, 2, T])
        ssm_sig = ssm_g
        b_mat = sb("b_mat", [P, 2, HJ, P])
        c_mat = sb("c_mat", [P, 2, HJ, P])
        silu_g = probs[:].rearrange("p a b -> p (a b)")[:, 0:2 * T].rearrange("p (r t) -> p r t", t=T)
        hidden = probsT[:].rearrange("p a b -> p (a b)")[:, 0:4 * T].rearrange("p (r t) -> p r t", t=T)

        probs_f, probsT_f = (b[:].rearrange("p a b -> p (a b)") for b in (probs, probsT))
        e_silu = probs_f[:, 0:1024].rearrange("p (r n) -> p r n", n=512)
        spreadT = probs_f[:, 1024:1024 + T]
        e_hidden = probsT_f[:, 0:1024].rearrange("p (r n) -> p r n", n=512)
        pick = conv_in[:, :, 0:P]
        spread = probsT_f[:, 1024:1024 + TT * P].rearrange("p (a n) -> p a n", a=TT)
        picked = k_pad[:, 0:4].rearrange("p a (b n) -> p (a b) n", n=P)
        picked_hi = over("picked_hi", [P, KT, P], F32R, "attT")
        picked_lo = over("picked_lo", [P, KT, P], F32R, "arena", 4 * UNIT_RING * UNIT)
        turned_hi = over("turned_hi", [P, 2, 4, P], F32R, "v_sb")
        turned_lo = over("turned_lo", [P, 2, 4, P], F32R, "arena", 4 * UNIT_RING * UNIT + 4096)
        unit_raw = arena[:, 0:UNIT_RING * UNIT].rearrange("p (r n) -> p r n", n=UNIT)
        unit_hi = over("unit_hi", [P, SPLIT_RING, UNIT], F32R, "arena", 4 * RING * SLOT)
        unit_lo = over("unit_lo", [P, SPLIT_RING, UNIT], F32R, "arena", 4 * (RING * SLOT + SPLIT_RING * UNIT))
        e_out = k_pad[:, 4:8].rearrange("p a t -> p (a t)")
        acc_f = conv_acc[:].rearrange("p a t -> p (a t)")
        before, ones_mat, slot_iota = acc_f[:, 0:P], acc_f[:, P:2 * P], acc_f[:, 2 * P:3 * P]

        ident = sb("ident", [P, P])
        causal = sb("causal", [P, P])
        mean_mat = sb("mean_mat", [P, P])
        ones_row = sb("ones_row", [1, P])
        b_mask = sb("b_mask", [P, HJ * 8])
        c_mask = sb("c_mask", [P, 2, 8])
        f_scale = sb("f_scale", [64, H + 1])
        f_shift = sb("f_shift", [64, H + 1])

        NROW = 30 + 12 + 8 + 8 + 8 + CK * CW // P
        rows = back_flat[:, 512:512 + DEPTH * P].rearrange("p (l n) -> p l n", l=DEPTH)
        cols = sb("cols", [P, DEPTH, NROW])
        srow = sb("srow", [32, P])
        ldt_row = sb("ldt_row", [16, P])
        ones_col = sb("ones_col", [64, 1])
        ldt = sb("ldt", [16, 2])
        scol = sb("scol", [P, 48])
        b_raw = sb("b_raw", [P, 2, DEPTH, NJ, GH])
        b_bar = sb("b_bar", [P, 2, NJ, GH])
        b_tmp = back_flat[:, 0:2 * NJ * GH].rearrange("p (c j h) -> p c j h", c=2, j=NJ)
        c_raw = sb("c_raw", [P, 2, DEPTH, 2, S])
        wf = sb("wf", [P, KT, 64])
        bf = sb("bf", [64, DEPTH])
        w_router = sb("w_router", [P, KT, NE])
        b_router = sb("b_router", [1, NE])
        g_final = qT[:].rearrange("p a t -> p (a t)")
        fz = rot_tmp[0:64, 0]
        SC = DEPTH * NJ
        sm = sb("sm", [P, 14, SC])
        rot_pow = sb("rot_pow", [P, 2, 8, SC])
        st = sb("st", [P, 5, 3, TT])
        att_max = sb("att_max", [P, 2, 4])
        att_sum = sb("att_sum", [P, 2, 4])
        att_rs = sb("att_rs", [P, 2, 4])
        ln_r = rot_tmp[:, 0, 0]
        logits = sb("logits", [P, TT, NE])
        top = sb("top", [P, TT, 8])
        top_at = sb("top_at", [P, TT, 8], U32)
        top_f = sb("top_f", [P, TT, 8])
        rt = sb("rt", [P, TT, 4])
        e_iota = sb("e_iota", [P, NE])
        w_exp = sb("w_exp", [P, TT, NE + 1])
        chosen = sb("chosen", [P, TT, NE])
        place = sb("place", [P, TT, NE + 1])
        most = sb("most", [P, 1])
        crowded = sb("crowded", [P, 1], mybir.dt.int32)
        w_tmp = sb("w_tmp", [P, TT, NE])

        bank = [ctx.enter_context(nc.psum_tensor(f"bank{i}", [P, 512], F32)) for i in range(8)]

        def halves(b):
            return bank[b][:, :].rearrange("p (a t) -> p a t", a=2)

        BI = 0
        QK = 30
        GM, GF = 42, 50
        SD, CB, LG, LB = 58, 60, 62, 64
        CWC = 66

        def sems(names):
            return {n: ctx.enter_context(nc.semaphore(n)) for n in names.split()}

        slot_full = [ctx.enter_context(nc.semaphore(f"slot_full{i}")) for i in range(RING)]
        unit_full = [ctx.enter_context(nc.semaphore(f"unit_full{i}")) for i in range(UNIT_RING)]
        g = sems("x_in rows_in states_in mats_in side_in gain_in final_in out_done "
                 "gate_used pe_params act_params "
                 "pool_const pool_order dve_const dve_order act_order dve_theta act_trig dve_states "
                 "ffn_up_done ffn_act_silu ffn_hidden ffn_down_done acc_read "
                 "pe_router router_read act_top "
                 "dve_second pool_route dve_route pe_route dve_pick pe_picked dve_picked pe_spread dve_spread "
                 "pe_e_turned act_turned dve_turned act_picked dve_picked_lo "
                 "act_e_out pe_combined split_hi split_lo unit_used")
        PER = dict(pe_proj=10, act_qk=12, dve_v=2, dve_fz=2, act_f=2, dve_f=9, dve_u=2, act_cg=2, dve_cv=2,
                   pool_mats=8, pe_mats=8, act_mats=8, pool_phase=2, pe_bu=4, dve_bu=4, dve_scan=4, pool_back=4,
                   pe_y=2, dve_z=2, act_gelu=1, pe_glu=2, act_glu=1, dve_glu=1, pe_gate=12, act_gate=24,
                   pe_s=8, dve_max=2, act_exp=16, dve_p=4, pe_pt=8, act_pt=8, pe_att=4, dve_att=8,
                   dve_conv=2, pe_ln=2, dve_ln=4, act_ln=1, act_conv=2, pe_out=12, dve_merge=4, pe_wo=2, dve_wo=4,
                   act_ss=2, dve_rv=1, act_sd=1, dve_hn=1, act_hn=1, pe_tr=4, dve_ht=4, act_ht=4)
        S_ = sems(" ".join(PER))

        loads, used_at = [], []

        def k_tiles(w):
            return w.rearrange("(k p) n -> p k n", p=P)

        def load(used, *parts):
            s = len(loads) % RING
            loads.append([(slot(s, src.shape[1], src.shape[2], first), src) for src, first in parts])
            used_at.append(used)

        FF_CH = [(c, min(512, DFF - c)) for c in range(0, DFF, 512)]
        mix_at, ffn_at = [], None
        for l in range(DEPTH):
            mix_at.append(len(loads))
            w = t["w_in"][l]

            def used(name, v):
                return S_[name], l * PER[name] + v

            for n, (a, b) in enumerate(((0, AW), (AW, V_AT), (V_AT, F_AT), (U_AT, C_AT), (C_AT, G_AT))):
                load(used("pe_proj", (2, 4, 6, 8, 10)[n]), (k_tiles(w[:, a:b]), 0))
            for n, c in enumerate(range(G_AT, N_IN, 512)):
                load(used("pe_gate", 2 * n + 2), (k_tiles(w[:, c:c + 512]), 0))
            load(used("pe_glu", 2), (k_tiles(t["ssm_w_glu"][l]), 0))
            load(used("pe_out", 12), (k_tiles(t["w_att_out"][l]), 0))
            load(used("pe_out", 12), (k_tiles(t["w_ssm_out"][l]), 0), (k_tiles(t["w_conv_out"][l]), 2 * D))
            load(used("pe_wo", 1), (k_tiles(t["w_o"][l, 0:512]), 0))
            load(used("pe_wo", 2), (k_tiles(t["w_o"][l, 512:D]), 0))
            assert len(loads) == mix_at[l] + MIX_LOADS
            if l == 0:
                ffn_at = len(loads)
                for n, (c, w_) in enumerate(FF_CH):
                    tiles = (c + w_) // P
                    load((g["gate_used"], n + 1), (k_tiles(t["ffn_w_gate"][0][:, c:c + w_]), 0))
                    load((g["ffn_up_done"], tiles), (k_tiles(t["ffn_w_up"][0][:, c:c + w_]), 0))
                    load((g["ffn_down_done"], tiles), (k_tiles(t["ffn_w_down"][0][c:c + w_, :]), 0))
        N_LOADS = len(loads)
        full_at, count = [], [0] * RING
        for n, parts in enumerate(loads):
            count[n % RING] += 16 * len(parts)
            full_at.append(count[n % RING])
        last_in_slot = [max(n for n in range(N_LOADS) if n % RING == s) for s in range(RING)]

        E_CH = DFE // 512
        units = []
        for c in range(E_CH + 1):
            if c < E_CH:
                units += [("gate", c, 0), ("gate", c, 1), ("up", c, 0), ("up", c, 1)]
            if c:
                units += [("down", c - 1, 0), ("down", c - 1, 1)]
        NU = len(units)
        unit_at = {u: n for n, u in enumerate(units)}
        assert NU % UNIT_RING == 0 and NU % SPLIT_RING == 0 and DFE % 512 == 0
        N_FF = DFF // P

        block = ctx.enter_context(nc.Block())

        @block.sync
        def _(sp):
            sp.dma_start(x_sb[:], t["x"][0].rearrange("(a p) d -> p a d", p=P)).then_inc(g["x_in"], 16)
            for n, parts in enumerate(loads):
                if n >= RING:
                    sp.wait_ge(*used_at[n - RING])
                for dst, src in parts:
                    sp.dma_start(dst, src).then_inc(slot_full[n % RING], 16)
            def expert_loads(e, v):
                for n, (kind, c, h) in enumerate(units):
                    r = n % UNIT_RING
                    w = t["moe_w_" + kind][0, bass.ds(e, 1)]
                    if kind == "down":
                        w = w[:, c * 512 + h * 256:c * 512 + h * 256 + 256, :]
                        dst = unit_raw[:, r].rearrange("p (k n) -> p k n", n=D)
                    else:
                        w = w[:, h * 512:(h + 1) * 512, c * 512:(c + 1) * 512]
                        dst = unit_raw[:, r].rearrange("p (k n) -> p k n", n=512)
                    if n < UNIT_RING:
                        sp.wait_ge(*used_at[last_in_slot[r // 2]])
                    sp.wait_ge(g["split_lo"], v * NU + (n + 1))
                    sp.dma_start(dst, w.rearrange("o (k p) n -> p (o k) n", p=P)).then_inc(unit_full[r], 16)

            with sp.Fori(0, NE) as e:
                expert_loads(e, e)
            sp.wait_ge(g["dve_route"], 2)
            with sp.If(sp.value_load(crowded[0:1, 0:1], min_val=0, max_val=1) > 0):
                with sp.Fori(0, NE) as e:
                    expert_loads(e, e + NE)
            sp.wait_ge(g["final_in"], 1)
            sp.dma_start(out[0].rearrange("(a p) d -> p a d", p=P), hn[:]).then_inc(g["out_done"], 16)
            sp.wait_ge(g["out_done"], 16)

        @block.gpsimd
        def _(pool):
            done = [0]

            def link(ins):
                done[0] += 1
                ins.then_inc(g["pool_order"], 1)
                pool.wait_ge(g["pool_order"], done[0])

            def const(ins):
                ins.then_inc(g["pool_const"], 1)

            link(pool.memset(ident[:], 0.0))
            const(pool.affine_select(out=ident[:], in_=ident[:], compare_op=ALU.not_equal, fill=1.0, base=0,
                                     pattern=[[-1, P]], channel_multiplier=1))
            link(pool.memset(causal[:], 0.0))
            const(pool.affine_select(out=causal[:], in_=causal[:], compare_op=ALU.is_ge, fill=MASKED, base=0,
                                     pattern=[[-1, P]], channel_multiplier=1))
            link(pool.memset(c_mask[:, 0, :], 1.0))
            link(pool.affine_select(out=c_mask[:, 0, :], in_=c_mask[:, 0, :], compare_op=ALU.is_ge, fill=0.0, base=0,
                                    pattern=[[-GH, 8]], channel_multiplier=1))
            link(pool.affine_select(out=c_mask[:, 0, :], in_=c_mask[:, 0, :], compare_op=ALU.is_ge, fill=0.0,
                                    base=GH - 1, pattern=[[GH, 8]], channel_multiplier=-1))
            link(pool.tensor_scalar(c_mask[:, 1, :], c_mask[:, 0, :], -1.0, None, ALU.mult))
            link(pool.memset(b_mask[:], 0.0))
            link(pool.memset(b_mask[0:64, 0:3 * 10 + 1:10], 1.0))
            link(pool.memset(b_mask[64:P, 1:3 * 10 + 2:10], 1.0))
            link(pool.memset(f_scale[:], 0.0))
            link(pool.memset(f_shift[:], 0.0))
            link(pool.memset(f_scale[0:H, H:H + 1], 8.0))
            link(pool.memset(f_shift[32:32 + H, H:H + 1], 1.0))
            link(pool.affine_select(out=f_scale[:, 0:H], in_=f_scale[:, 0:H], compare_op=ALU.not_equal, fill=-8.0,
                                    base=-32, pattern=[[-1, H]], channel_multiplier=1))
            const(pool.affine_select(out=f_shift[:, 0:H], in_=f_shift[:, 0:H], compare_op=ALU.not_equal, fill=1.0,
                                     base=0, pattern=[[-1, H]], channel_multiplier=1))
            link(pool.memset(k_pad[:], 0.0))
            link(pool.memset(conv_in[:], 0.0))
            const(pool.iota(e_iota[:], [[1, NE]], base=0, channel_multiplier=0,
                            allow_small_or_imprecise_dtypes=True))

            pool.wait_ge(g["dve_const"], 2)
            def forget_weights(l):
                for at_ in (0, 32):
                    pool.dma_start(wf[:, :, at_:at_ + H], k_tiles(t["w_in"][l][:, F_AT:U_AT])).then_inc(g["side_in"], 16)
                    pool.dma_start(bf[at_:at_ + H, l:l + 1],
                                   t["b_in"][l, F_AT:U_AT].rearrange("(n o) -> n o", o=1)).then_inc(g["side_in"], 16)

            forget_weights(0)
            pool.dma_start(w_router[:], k_tiles(t["moe_w_router"][0])).then_inc(g["side_in"], 16)
            pool.dma_start(b_router[:], t["moe_b_router"][0:1]).then_inc(g["side_in"], 16)

            for l in range(DEPTH):
                if l:
                    pool.wait_ge(S_["pe_proj"], (l - 1) * PER["pe_proj"] + 7)
                    forget_weights(l)
                pool.wait_ge(g["dve_states"], 1)
                pool.wait_ge(g["mats_in"], 128)
                j0 = l * NJ
                f_re, f_im = (sm[:, k, j0:j0 + NJ].rearrange("p (j o) -> p j o", o=1).to_broadcast([P, NJ, GH])
                              for k in (10, 11))
                link(pool.tensor_tensor(b_bar[:, 0], b_raw[:, 0, l], f_re, ALU.mult))
                link(pool.tensor_tensor(b_tmp[:, 0], b_raw[:, 1, l], f_im, ALU.mult))
                link(pool.tensor_tensor(b_bar[:, 1], b_raw[:, 1, l], f_re, ALU.mult))
                link(pool.tensor_tensor(b_tmp[:, 1], b_raw[:, 0, l], f_im, ALU.mult))
                link(pool.tensor_tensor(b_bar[:, 0], b_bar[:, 0], b_tmp[:, 0], ALU.subtract))
                link(pool.tensor_tensor(b_bar[:, 1], b_bar[:, 1], b_tmp[:, 1], ALU.add))
                pool.wait_ge(S_["pe_tr"], 2 * l * PER["pe_tr"] + 4)
                for half in range(2):
                    if half:
                        pool.wait_ge(S_["pe_mats"], l * PER["pe_mats"] + 4)
                    for c in range(2):
                        o = mat_src[:, c].rearrange("p (j g h) -> p j g h", j=HJ, g=8)
                        src = b_bar[:, c, half * HJ:(half + 1) * HJ]
                        pool.tensor_tensor(
                            o, src.rearrange("p j (o h) -> p j o h", o=1).to_broadcast([P, HJ, 8, GH]),
                            b_mask[:].rearrange("p (j g o) -> p j g o", g=8, o=1).to_broadcast([P, HJ, 8, GH]),
                            ALU.mult).then_inc(S_["pool_mats"], 1)
                    for c in range(2):
                        o = mat_src[:, 2 + c].rearrange("p (g s) -> p g s", g=8)
                        pool.tensor_tensor(
                            o, c_raw[:, c, l, half:half + 1].to_broadcast([P, 8, S]),
                            c_mask[:, c].rearrange("p (g o) -> p g o", o=1).to_broadcast([P, 8, S]),
                            ALU.mult).then_inc(S_["pool_mats"], 1)
                    if l and half == 0:
                        pool.wait_ge(S_["dve_bu"], l * PER["dve_bu"])
                    if half:
                        pool.wait_ge(S_["dve_bu"], l * PER["dve_bu"] + 2)
                        pool.wait_ge(S_["pool_back"], l * PER["pool_back"] + 2)
                    cs, sn = phase[:, 0], phase[:, 1]
                    link(pool.memset(cs[:, :, 0:1], 1.0))
                    link(pool.memset(sn[:, :, 0:1], 0.0))
                    w, n = 1, 0
                    while w < T:
                        zj = j0 + half * HJ
                        z_re, z_im = (rot_pow[:, c, n, zj:zj + HJ].rearrange("p (j o) -> p j o", o=1)
                                      .to_broadcast([P, HJ, w]) for c in range(2))
                        tmp = [back_tmp.rearrange("p c j t -> p (c j t)")[:, a * HJ * w:(a + 1) * HJ * w]
                               .rearrange("p (j t) -> p j t", t=w) for a in range(2)]
                        link(pool.tensor_tensor(tmp[0], cs[:, :, 0:w], z_re, ALU.mult))
                        link(pool.tensor_tensor(tmp[1], sn[:, :, 0:w], z_im, ALU.mult))
                        link(pool.tensor_tensor(cs[:, :, w:2 * w], tmp[0], tmp[1], ALU.subtract))
                        link(pool.tensor_tensor(tmp[0], cs[:, :, 0:w], z_im, ALU.mult))
                        link(pool.tensor_tensor(tmp[1], sn[:, :, 0:w], z_re, ALU.mult))
                        last = pool.tensor_tensor(sn[:, :, w:2 * w], tmp[0], tmp[1], ALU.add)
                        w, n = 2 * w, n + 1
                        if w < T:
                            link(last)
                        else:
                            last.then_inc(S_["pool_phase"], 1)
                            pool.wait_ge(S_["pool_phase"], l * PER["pool_phase"] + half + 1)
                    for q in range(2):
                        pair = 2 * half + q
                        pool.wait_ge(S_["dve_scan"], l * PER["dve_scan"] + pair + 1)
                        y_re, y_im = (state[:, c, 2 * q:2 * q + 2] for c in range(2))
                        c_, s_ = (phase[:, c, 2 * q:2 * q + 2] for c in range(2))
                        ta, tb = back_tmp[:, 0], back_tmp[:, 1]
                        link(pool.tensor_tensor(ta, y_im, s_, ALU.mult))
                        link(pool.tensor_tensor(tb, y_re, s_, ALU.mult))
                        link(pool.tensor_tensor(y_re, y_re, c_, ALU.mult))
                        link(pool.tensor_tensor(y_im, y_im, c_, ALU.mult))
                        link(pool.tensor_tensor(y_re, y_re, ta, ALU.subtract))
                        pool.tensor_tensor(y_im, y_im, tb, ALU.add).then_inc(S_["pool_back"], 1)
                        pool.wait_ge(S_["pool_back"], l * PER["pool_back"] + pair + 1)
            pool.wait_ge(S_["dve_merge"], DEPTH * 4)
            link(pool.memset(acc_f[:, 0:2 * P], 1.0))
            pool.affine_select(out=before, in_=before, compare_op=ALU.is_ge, fill=0.0, base=-1,
                               pattern=[[1, P]], channel_multiplier=-1).then_inc(g["pool_route"], 1)
            pool.iota(slot_iota, [[1, P]], base=0, channel_multiplier=0,
                      allow_small_or_imprecise_dtypes=True).then_inc(g["pool_route"], 1)
            pool.dma_start(g_final, t["g_final"].rearrange("(o d) -> o d", o=1).to_broadcast([P, D])).then_inc(g["gain_in"], 16)

        @block.scalar
        def _(act):
            for l in range(DEPTH):
                def row_load(at, src):
                    act.dma_start(rows[at:at + src.shape[0], l, :], src).then_inc(g["rows_in"], 16)

                row_load(BI, t["b_in"][l, U_AT:N_IN].rearrange("(r n) -> r n", n=P))
                row_load(QK, t["b_in"][l, 0:F_AT].rearrange("(r n) -> r n", n=P))
                row_load(GM, t["g_mix"][l].rearrange("(r n) -> r n", n=P))
                row_load(GF, t["g_ffn"][l].rearrange("(r n) -> r n", n=P))
                row_load(SD, t["ssm_d"][l].rearrange("(r a) h -> r (a h)", r=2))
                row_load(CB, t["conv_b"][l].rearrange("(r n) -> r n", n=P))
                row_load(LG, t["conv_ln_g"][l].rearrange("(r n) -> r n", n=P))
                row_load(LB, t["conv_ln_b"][l].rearrange("(r n) -> r n", n=P))
                row_load(CWC, t["conv_w"][l].rearrange("k (r n) -> (k r) n", n=P))
            act.dma_start(srow[0:16, :], t["ssm_a_re"].rearrange("l (j a) s -> (l j) (a s)", a=2)).then_inc(g["states_in"], 16)
            act.dma_start(srow[16:32, :], t["ssm_a_im"].rearrange("l (j a) s -> (l j) (a s)", a=2)).then_inc(g["states_in"], 16)
            act.dma_start(ldt[:, :], t["ssm_log_dt"].rearrange("l (j a) -> (l j) a", a=2)).then_inc(g["states_in"], 16)
            for l in range(DEPTH):
                for c, (b, cc) in enumerate((("ssm_b_re", "ssm_c_re"), ("ssm_b_im", "ssm_c_im"))):
                    act.dma_start(b_raw[:, c, l], t[b][l].rearrange("(j a) s h -> (a s) j h", a=2)).then_inc(g["mats_in"], 16)
                    act.dma_start(c_raw[:, c, l], t[cc][l].rearrange("(i a) h s -> (a h) i s", i=2)).then_inc(g["mats_in"], 16)
            for l in range(DEPTH):
                act.wait_ge(g["pe_params"], l + 1)
                act.activation(cols[:, l], bank[7 - l][:, 0:NROW], ACT.Copy).then_inc(g["act_params"], 1)
            act.wait_ge(g["dve_theta"], 1)
            act.activation(sm[:, 0], sm[:, 0], ACT.Exp).then_inc(g["act_trig"], 1)
            act.wait_ge(g["dve_theta"], 2)
            act.activation(sm[:, 3], sm[:, 3], ACT.Exp).then_inc(g["act_trig"], 1)
            act.activation(sm[:, 4], sm[:, 4], ACT.Sin).then_inc(g["act_trig"], 1)
            act.activation(sm[:, 5], sm[:, 5], ACT.Sin).then_inc(g["act_trig"], 1)

            def norm(m, gain):
                if m == 0:
                    act.wait_ge(g["x_in"], 16)
                else:
                    act.wait_ge(g["acc_read"] if m % 2 == 0 else S_["dve_wo"], {1: 4, 2: 4, 3: 8, 4: 4 + 4 * NE}[m])
                for a in range(TT):
                    act.activation(hn[:, a], x_sb[:, a], ACT.Square, accum_out=st[:, m, 0, a:a + 1]).then_inc(S_["act_ss"], 1)
                act.wait_ge(S_["dve_rv"], m * PER["dve_rv"] + 1)
                act.activation(st[:, m, 2], st[:, m, 1], ACT.Sqrt).then_inc(S_["act_sd"], 1)
                act.wait_ge(S_["act_sd"], m * PER["act_sd"] + 1)
                act.activation(hn[:, 1], x_sb[:, 1], ACT.Copy, scale=st[:, m, 2, 1:2]).then_inc(S_["act_hn"], 1)
                if gain is None:
                    return
                act.wait_ge(g["act_params"], 2)
                for b in (2, 3):
                    act.wait_ge(S_["pe_tr"], m * PER["pe_tr"] + b + 1)
                    for a in range(2):
                        k = 2 * b + a
                        act.activation(hT[:, k], halves(b)[:, a], ACT.Copy,
                                       scale=cols[:, m // 2, gain + k:gain + k + 1]).then_inc(S_["act_ht"], 1)

            def gate_sigmoids(l, first, last):
                for n in range(first, last):
                    act.wait_ge(S_["pe_gate"], l * PER["pe_gate"] + n + 1)
                    for a in range(2):
                        i = 2 * n + a
                        act.activation(gates[:, i], halves(6 + n % 2)[:, a], ACT.Sigmoid,
                                       bias=cols[:, l, BI + 6 + i:BI + 7 + i]).then_inc(S_["act_gate"], 1)

            def mats(l, half):
                for n in range(4):
                    act.wait_ge(S_["pe_mats"], l * PER["pe_mats"] + 4 * half + n + 1)
                    if half and n < 2:
                        act.wait_ge(S_["pe_bu"], l * PER["pe_bu"] + 2)
                    if half and n >= 2:
                        act.wait_ge(S_["pe_y"], l * PER["pe_y"] + 1)
                    dst = (b_mat if n < 2 else c_mat)[:, n % 2].rearrange("p j n -> p (j n)")
                    act.activation(dst, bank[n][:, :], ACT.Copy).then_inc(S_["act_mats"], 1)

            def exps(l, grp):
                act.wait_ge(S_["dve_max"], l * PER["dve_max"] + grp + 1)
                if grp:
                    act.wait_ge(S_["pe_pt"], l * PER["pe_pt"] + 4)
                for h in range(4):
                    s = bank[h]
                    act.activation(probs[:, h, 0:P], s[:, 0:P], ACT.Exp, bias=att_max[:, 0, h:h + 1], scale=0.125,
                                   accum_out=att_sum[:, 0, h:h + 1]).then_inc(S_["act_exp"], 1)
                    act.activation(probs[:, h, P:384], s[:, P:384], ACT.Exp, bias=att_max[:, 1, h:h + 1], scale=0.125,
                                   accum_out=att_sum[:, 1, h:h + 1]).then_inc(S_["act_exp"], 1)

            def probs_out(l, grp):
                for h in range(4):
                    act.wait_ge(S_["pe_pt"], l * PER["pe_pt"] + 4 * grp + h + 1)
                    if grp:
                        act.wait_ge(S_["pe_att"], l * PER["pe_att"] + 2)
                    act.activation(probsT[:, h], bank[h][:, 0:384], ACT.Copy).then_inc(S_["act_pt"], 1)

            for l in range(DEPTH):
                norm(2 * l, GM)
                for b in range(4):
                    act.wait_ge(S_["pe_proj"], l * PER["pe_proj"] + b + 1)
                    for a in range(2):
                        j = 2 * (b % 2) + a
                        src = halves(4 + b)[:, a]
                        if b < 2:
                            act.activation(qT[:, j], src, ACT.Identity,
                                           bias=cols[:, l, QK + j:QK + j + 1]).then_inc(S_["act_qk"], 1)
                        else:
                            if b == 2 and a == 0:
                                act.wait_ge(g["pool_const"], 4)
                            for o in range(2):
                                r = slice(64 * o, 64 * o + 64)
                                act.activation(k_pad[r, 2 * j + o], src[r], ACT.Identity,
                                               bias=cols[r, l, QK + 4 + j:QK + 5 + j]).then_inc(S_["act_qk"], 1)
                act.wait_ge(S_["dve_fz"], l * PER["dve_fz"] + 2)
                act.activation(fz[:, 1], fz[:, 1], ACT.Exp, scale=-1.0).then_inc(S_["act_f"], 1)
                act.wait_ge(S_["act_f"], l * PER["act_f"] + 1)
                act.activation(fz[:, 1], fz[:, 1], ACT.Ln, bias=1.0).then_inc(S_["act_f"], 1)
                act.wait_ge(S_["pe_proj"], l * PER["pe_proj"] + 10)
                for a in range(2):
                    act.activation(conv_sig[:, a], halves(5)[:, a], ACT.Sigmoid,
                                   bias=cols[:, l, BI + 4 + a:BI + 5 + a]).then_inc(S_["act_cg"], 1)
                mats(l, 0)
                exps(l, 0)
                gate_sigmoids(l, 0, 4)
                probs_out(l, 0)
                gate_sigmoids(l, 4, 6)
                mats(l, 1)
                exps(l, 1)
                gate_sigmoids(l, 6, 10)
                probs_out(l, 1)
                gate_sigmoids(l, 10, 12)
                act.wait_ge(S_["dve_ln"], l * PER["dve_ln"] + 3)
                act.activation(ln_r[:], ln_r[:], ACT.Sqrt).then_inc(S_["act_ln"], 1)
                act.wait_ge(S_["dve_ln"], l * PER["dve_ln"] + 4)
                for a in range(2):
                    act.activation(conv_sig[:, a], conv_acc[:, a], ACT.Silu, scale=cols[:, l, LG + a:LG + a + 1],
                                   bias=cols[:, l, LB + a:LB + a + 1]).then_inc(S_["act_conv"], 1)
                act.wait_ge(S_["dve_z"], l * PER["dve_z"] + 2)
                act.activation(ssm_g[:], ssm_z[:], ACT.Gelu_apprx_tanh).then_inc(S_["act_gelu"], 1)
                act.wait_ge(S_["pe_glu"], l * PER["pe_glu"] + 2)
                act.activation(ssm_sig[:], halves(5)[:, :], ACT.Sigmoid).then_inc(S_["act_glu"], 1)

                norm(2 * l + 1, GF)
                if l == 0:
                    for f in range(N_FF):
                        act.wait_ge(g["ffn_up_done"], f + 1)
                        if f >= 2:
                            act.wait_ge(g["ffn_hidden"], f - 1)
                        act.activation(silu_g[:, f % 2], halves(4 + f % 4)[:, 0], ACT.Silu).then_inc(g["ffn_act_silu"], 1)
                else:
                    act.wait_ge(g["router_read"], 3)
                    act.activation(rt[:, :, 1:2], rt[:, :, 0:1], ACT.Exp).then_inc(g["act_top"], 1)
                    def picked_high(v):
                        for n in range(2):
                            act.wait_ge(g["dve_picked"], v * 2 + (n + 1))
                            act.activation(picked_hi[:, 4 * n:4 * n + 4], picked[:, 4 * n:4 * n + 4],
                                           ACT.Copy).then_inc(g["act_picked"], 1)

                    def expert(v, p_):
                        def high(n):
                            r, q = n % UNIT_RING, n % SPLIT_RING
                            act.wait_ge(unit_full[r], v * (16 * NU // UNIT_RING) + 16 * (n // UNIT_RING + 1))
                            act.wait_ge(g["unit_used"], v * NU + (n + 1))
                            act.activation(unit_hi[:, q], unit_raw[:, r], ACT.Copy).then_inc(g["split_hi"], 1)

                        def used(kind, c):
                            act.wait_ge(g["unit_used"], v * NU + (unit_at[kind, c, 1] + 1 + SPLIT_RING))

                        def turn_high(c):
                            act.wait_ge(g["pe_e_turned"], v * E_CH + (c + 1))
                            if c >= 2:
                                used("down", c - 2)
                            act.activation(turned_hi[:, c % 2], bank[4][:, :].rearrange("p (b n) -> p b n", n=P),
                                           ACT.Copy).then_inc(g["act_turned"], 1)

                        for n in range(SPLIT_RING):
                            high(n)
                        for n, (kind, c, h) in enumerate(units):
                            if kind == "gate" and h:
                                used("gate", c)
                                act.wait_ge(g["ffn_hidden"], v * E_CH + (N_FF + max(c - 1, 0)))
                                act.activation(e_silu[:, c % 2], bank[c % 2][:, :],
                                               ACT.Silu).then_inc(g["ffn_act_silu"], 1)
                                if c:
                                    turn_high(c - 1)
                            if n == unit_at["down", E_CH - 2, 1]:
                                turn_high(E_CH - 1)
                            if n + SPLIT_RING < NU:
                                high(n + SPLIT_RING)
                        used("down", E_CH - 1)
                        for h in range(2):
                            act.activation(e_out[:, h * 512:(h + 1) * 512], bank[5 + h][:, :],
                                           ACT.Copy).then_inc(g["act_e_out"], 1)
                        picked_high(v + (1 + p_))

                    picked_high(0)
                    with act.Fori(0, NE) as e:
                        expert(e, 0)
                    with act.If(act.value_load(crowded[0:1, 0:1], min_val=0, max_val=1) > 0):
                        picked_high(NE + 1)
                        with act.Fori(0, NE) as e:
                            expert(e + NE, 1)
                        act.wait_ge(g["acc_read"], 4 + 8 * NE)
            norm(4, None)

        @block.vector
        def _(dve):
            counts = {}

            def step(ins, sem=g["dve_order"]):
                counts[id(sem)] = counts.get(id(sem), 0) + 1
                ins.then_inc(sem, 1)
                dve.wait_ge(sem, counts[id(sem)])

            step(dve.memset(wf[:], 0.0), g["dve_const"])
            step(dve.memset(bf[:], 0.0), g["dve_const"])
            step(dve.memset(mean_mat[:], 1.0 / CW), g["dve_const"])
            step(dve.memset(ones_row[:], 1.0), g["dve_const"])
            step(dve.memset(ones_col[:], 1.0))
            step(dve.memset(f_left[:], 0.0))
            dve.memset(f_right[:], 0.0).then_inc(g["split_lo"], UNIT_RING)
            dve.wait_ge(g["split_lo"], UNIT_RING)

            dve.wait_ge(g["states_in"], 48)
            step(dve.tensor_copy(ldt_row[:].rearrange("r (a s) -> r a s", a=2),
                                 ldt[:].rearrange("r (a o) -> r a o", o=1).to_broadcast([16, 2, S])), g["dve_const"])
            dve.wait_ge(g["pe_params"], 3)
            step(dve.tensor_copy(scol[:], bank[5][:, 0:48]))
            a_re, a_im = scol[:, 0:SC], scol[:, SC:2 * SC]
            step(dve.tensor_copy(sm[:, 0], scol[:, 2 * SC:3 * SC]), g["dve_theta"])
            dve.wait_ge(g["act_trig"], 1)
            step(dve.tensor_tensor(sm[:, 3], a_re, sm[:, 0], ALU.mult))
            step(dve.tensor_tensor(sm[:, 1], a_im, sm[:, 0], ALU.mult))
            step(dve.tensor_scalar(sm[:, 2], sm[:, 1], 1.0 / TWO_PI, ROUND_MAGIC, ALU.mult, ALU.add))
            step(dve.tensor_scalar(sm[:, 2], sm[:, 2], ROUND_MAGIC, None, ALU.subtract))
            for part in (TWO_PI_A, TWO_PI_B, TWO_PI_C):
                step(dve.scalar_tensor_tensor(sm[:, 1], sm[:, 2], -part, sm[:, 1], ALU.mult, ALU.add))
            step(dve.tensor_scalar(sm[:, 4], sm[:, 1], 3.1415925, -3.1415925, ALU.min, ALU.max))
            step(dve.scalar_tensor_tensor(sm[:, 5], sm[:, 4], -1.0, sm[:, 4], ALU.mult, ALU.max))
            step(dve.tensor_scalar(sm[:, 5], sm[:, 5], -1.0, TWO_PI / 4, ALU.mult, ALU.add), g["dve_theta"])
            dve.wait_ge(g["act_trig"], 4)
            step(dve.tensor_copy(rot_pow[:, 0, 0], sm[:, 5]))
            step(dve.tensor_copy(rot_pow[:, 1, 0], sm[:, 4]))
            step(dve.tensor_tensor(sm[:, 5], sm[:, 5], sm[:, 3], ALU.mult))
            step(dve.tensor_scalar(sm[:, 5], sm[:, 5], 1.0, None, ALU.subtract))
            step(dve.tensor_tensor(sm[:, 6], sm[:, 4], sm[:, 3], ALU.mult))
            step(dve.tensor_tensor(sm[:, 7], a_re, a_re, ALU.mult))
            step(dve.tensor_tensor(sm[:, 8], a_im, a_im, ALU.mult))
            step(dve.tensor_tensor(sm[:, 7], sm[:, 7], sm[:, 8], ALU.add))
            step(dve.reciprocal(sm[:, 7], sm[:, 7]))
            step(dve.tensor_tensor(sm[:, 8], sm[:, 5], a_re, ALU.mult))
            step(dve.tensor_tensor(sm[:, 9], sm[:, 6], a_im, ALU.mult))
            step(dve.tensor_tensor(sm[:, 8], sm[:, 8], sm[:, 9], ALU.add))
            step(dve.tensor_tensor(sm[:, 10], sm[:, 8], sm[:, 7], ALU.mult))
            step(dve.tensor_tensor(sm[:, 8], sm[:, 6], a_re, ALU.mult))
            step(dve.tensor_tensor(sm[:, 9], sm[:, 5], a_im, ALU.mult))
            step(dve.tensor_tensor(sm[:, 8], sm[:, 8], sm[:, 9], ALU.subtract))
            step(dve.tensor_tensor(sm[:, 11], sm[:, 8], sm[:, 7], ALU.mult))
            for n in range(7):
                zr, zi = rot_pow[:, 0, n], rot_pow[:, 1, n]
                step(dve.tensor_tensor(sm[:, 12], zr, zr, ALU.mult))
                step(dve.tensor_tensor(sm[:, 13], zi, zi, ALU.mult))
                step(dve.tensor_tensor(rot_pow[:, 0, n + 1], sm[:, 12], sm[:, 13], ALU.subtract))
                step(dve.scalar_tensor_tensor(rot_pow[:, 1, n + 1], zr, 2.0, zi, ALU.mult, ALU.mult),
                     g["dve_states"] if n == 6 else g["dve_order"])

            def norm(m, gain):
                dve.wait_ge(S_["act_ss"], m * PER["act_ss"] + 2)
                step(dve.tensor_scalar(st[:, m, 1], st[:, m, 0], 1.0 / D, EPS, ALU.mult, ALU.add))
                step(dve.reciprocal(st[:, m, 1], st[:, m, 1]), S_["dve_rv"])
                dve.wait_ge(S_["act_sd"], m * PER["act_sd"] + 1)
                step(dve.tensor_scalar(hn[:, 0], x_sb[:, 0], st[:, m, 2, 0:1], None, ALU.mult), S_["dve_hn"])
                if gain is None:
                    return
                dve.wait_ge(g["act_params"], 2)
                for b in (0, 1):
                    dve.wait_ge(S_["pe_tr"], m * PER["pe_tr"] + b + 1)
                    for a in range(2):
                        k = 2 * b + a
                        step(dve.tensor_scalar(hT[:, k], halves(b)[:, a], cols[:, m // 2, gain + k:gain + k + 1],
                                               None, ALU.mult), S_["dve_ht"])

            def rotate_scan(l, pair):
                half, q = pair // 2, pair % 2
                dve.wait_ge(S_["pool_phase"], l * PER["pool_phase"] + half + 1)
                dve.wait_ge(S_["pe_bu"], l * PER["pe_bu"] + pair + 1)
                if pair == 2:
                    dve.wait_ge(S_["pe_y"], l * PER["pe_y"] + 1)
                re, im = halves(4)[:, :], halves(5)[:, :]
                c_, s_ = (phase[:, c, 2 * q:2 * q + 2] for c in range(2))
                y_re, y_im = (state[:, c, 2 * q:2 * q + 2] for c in range(2))
                step(dve.tensor_tensor(rot_tmp[:, 0], re, c_, ALU.mult))
                step(dve.tensor_tensor(rot_tmp[:, 1], im, s_, ALU.mult))
                step(dve.tensor_tensor(y_re, rot_tmp[:, 0], rot_tmp[:, 1], ALU.add))
                step(dve.tensor_tensor(rot_tmp[:, 0], im, c_, ALU.mult))
                step(dve.tensor_tensor(rot_tmp[:, 1], re, s_, ALU.mult))
                step(dve.tensor_tensor(y_im, rot_tmp[:, 0], rot_tmp[:, 1], ALU.subtract), S_["dve_bu"])
                for c in range(2):
                    for a in range(2):
                        j = l * NJ + 2 * pair + a
                        y = state[:, c, 2 * q + a]
                        step(dve.tensor_tensor_scan(y, sm[:, 3, j:j + 1].to_broadcast([P, T]), y, 0.0,
                                                    ALU.mult, ALU.add),
                             S_["dve_scan"] if c and a else g["dve_order"])

            def softmax_max(l, grp):
                dve.wait_ge(S_["pe_s"], l * PER["pe_s"] + 4 * grp + 4)
                if grp:
                    dve.wait_ge(S_["act_exp"], l * PER["act_exp"] + 8)
                for h in range(4):
                    step(dve.reduce_max(att_max[:, 0, h:h + 1], bank[h][:, 0:P], AX_X))
                    step(dve.reduce_max(att_max[:, 1, h:h + 1], bank[h][:, P:384], AX_X))
                step(dve.tensor_scalar(att_max[:], att_max[:], -0.125, None, ALU.mult), S_["dve_max"])

            def forget_right(l, grp):
                for h in range(4):
                    hd = 4 * grp + h
                    step(dve.tensor_scalar(f_right[0:64, h], f_sum[:], f_scale[:, hd:hd + 1], f_shift[:, hd:hd + 1],
                                           ALU.mult, ALU.add), S_["dve_f"])

            def softmax_norm(l, grp):
                dve.wait_ge(S_["act_exp"], l * PER["act_exp"] + 8 * grp + 8)
                step(dve.reciprocal(att_rs[:], att_sum[:]))
                for o, (a, b) in enumerate(((0, P), (P, 384))):
                    step(dve.tensor_tensor(probs[:, :, a:b], probs[:, :, a:b],
                                           att_rs[:, o].rearrange("p (h o) -> p h o", o=1).to_broadcast([P, 4, b - a]),
                                           ALU.mult), S_["dve_p"])

            def attention_out(l, grp):
                for q in range(2):
                    dve.wait_ge(S_["pe_att"], l * PER["pe_att"] + 2 * grp + q + 1)
                    for o in range(2):
                        r = slice(64 * o, 64 * o + 64)
                        j = 2 * grp + q
                        step(dve.tensor_scalar(attT[r, j], halves(q)[r, o], cols[r, l, QK + 8 + j:QK + 9 + j], None,
                                               ALU.add), S_["dve_att"])

            def conv_taps(l, a):
                w = lambda k: cols[:, l, CWC + 2 * k + a:CWC + 2 * k + a + 1]
                step(dve.tensor_scalar(conv_acc[:, a], conv_in[:, a, 0:T], w(0), cols[:, l, CB + a:CB + a + 1],
                                       ALU.mult, ALU.add))
                for k in range(1, CK):
                    step(dve.scalar_tensor_tensor(conv_acc[:, a], conv_in[:, a, k:k + T], w(k), conv_acc[:, a],
                                                  ALU.mult, ALU.add), S_["dve_conv"] if k == CK - 1 else g["dve_order"])

            def ssm_out(l, half):
                dve.wait_ge(S_["pe_y"], l * PER["pe_y"] + half + 1)
                step(dve.scalar_tensor_tensor(ssm_z[:, half], uT[:, half], cols[:, l, SD + half:SD + half + 1],
                                              halves(4)[:, 0], ALU.mult, ALU.add), S_["dve_z"])

            for l in range(DEPTH):
                norm(2 * l, GM)
                for a in range(TT):
                    dve.wait_ge(S_["pe_proj"], l * PER["pe_proj"] + 5 + a)
                    step(dve.tensor_copy(v_sb[:, a], bank[a][:, :]), S_["dve_v"])
                dve.wait_ge(S_["pe_proj"], l * PER["pe_proj"] + 7)
                dve.wait_ge(g["side_in"], 16 * (6 + 4 * l))
                step(dve.tensor_scalar(fz[:, 0], bank[2][0:64, 0:T], bf[:, l:l + 1], None, ALU.add), S_["dve_fz"])
                step(dve.scalar_tensor_tensor(fz[:, 1], fz[:, 0], -1.0, fz[:, 0], ALU.mult, ALU.max), S_["dve_fz"])
                dve.wait_ge(S_["pe_proj"], l * PER["pe_proj"] + 8)
                for a in range(2):
                    step(dve.tensor_scalar(uT[:, a], halves(3)[:, a], cols[:, l, BI + a:BI + a + 1], None, ALU.add),
                         S_["dve_u"])
                dve.wait_ge(S_["act_f"], l * PER["act_f"] + 2)
                step(dve.scalar_tensor_tensor(fz[:, 0], fz[:, 0], 0.0, fz[:, 1], ALU.min, ALU.subtract))
                dve.wait_ge(g["pool_const"], 3)
                step(dve.tensor_tensor_scan(f_sum[:], ones_col[:].to_broadcast([64, T]), fz[:, 0], 0.0,
                                            ALU.mult, ALU.add))
                step(dve.tensor_scalar(f_left[0:64], f_sum[:], f_scale[:, H:H + 1], f_shift[:, H:H + 1],
                                       ALU.mult, ALU.add), S_["dve_f"])
                forget_right(l, 0)
                dve.wait_ge(S_["act_cg"], l * PER["act_cg"] + 2)
                dve.wait_ge(g["pool_const"], 4)
                for a in range(2):
                    step(dve.scalar_tensor_tensor(conv_in[:, a, PAD:PAD + T], halves(4)[:, a],
                                                  cols[:, l, BI + 2 + a:BI + 3 + a], conv_sig[:, a],
                                                  ALU.add, ALU.mult), S_["dve_cv"])
                rotate_scan(l, 0)
                softmax_max(l, 0)
                softmax_norm(l, 0)
                forget_right(l, 1)
                rotate_scan(l, 1)
                conv_taps(l, 0)
                attention_out(l, 0)
                ssm_out(l, 0)
                rotate_scan(l, 2)
                softmax_max(l, 1)
                softmax_norm(l, 1)
                rotate_scan(l, 3)
                conv_taps(l, 1)
                attention_out(l, 1)
                for a in range(2):
                    if a == 0:
                        dve.wait_ge(S_["pe_ln"], l * PER["pe_ln"] + 1)
                    step(dve.tensor_tensor(conv_acc[:, a], conv_acc[:, a], halves(6)[:, 0], ALU.subtract))
                step(dve.tensor_tensor(conv_sig[:], conv_acc[:], conv_acc[:], ALU.mult), S_["dve_ln"])
                dve.wait_ge(S_["pe_ln"], l * PER["pe_ln"] + 2)
                step(dve.tensor_scalar(ln_r[:], halves(7)[:, 0], EPS, None, ALU.add), S_["dve_ln"])
                step(dve.reciprocal(ln_r[:], ln_r[:]), S_["dve_ln"])
                dve.wait_ge(S_["act_ln"], l * PER["act_ln"] + 1)
                for a in range(2):
                    last = dve.tensor_tensor(conv_acc[:, a], conv_acc[:, a], ln_r[:], ALU.mult)
                    step(last, S_["dve_ln"] if a else g["dve_order"])
                ssm_out(l, 1)
                dve.wait_ge(S_["act_glu"], l * PER["act_glu"] + 1)
                step(dve.tensor_tensor(ssm_z[:], halves(4)[:, :], ssm_sig[:], ALU.mult), S_["dve_glu"])
                for i in range(4):
                    b0 = 3 * (i % 2)
                    gt = [gates[:, 8 * b + 2 * i:8 * b + 2 * i + 2] for b in range(3)]
                    m_ = merged[:, 2 * i:2 * i + 2]
                    dve.wait_ge(S_["act_gate"], l * PER["act_gate"] + 24)
                    dve.wait_ge(S_["pe_out"], l * PER["pe_out"] + 3 * i + 1)
                    step(dve.tensor_tensor(m_, halves(b0)[:, :], gt[0], ALU.mult))
                    dve.wait_ge(S_["pe_out"], l * PER["pe_out"] + 3 * i + 2)
                    step(dve.tensor_tensor(rot_tmp[:, 0], halves(b0 + 1)[:, :], gt[1], ALU.mult))
                    dve.wait_ge(S_["pe_out"], l * PER["pe_out"] + 3 * i + 3)
                    step(dve.tensor_tensor(rot_tmp[:, 1], halves(b0 + 2)[:, :], gt[2], ALU.mult))
                    step(dve.tensor_tensor(m_, m_, rot_tmp[:, 0], ALU.add))
                    step(dve.tensor_tensor(m_, m_, rot_tmp[:, 1], ALU.add), S_["dve_merge"])
                dve.wait_ge(S_["pe_wo"], l * PER["pe_wo"] + 2)
                for n, b in enumerate((6, 7, 0, 1)):
                    xs = x_sb[:, n // 2, (n % 2) * 512:(n % 2 + 1) * 512]
                    step(dve.tensor_tensor(xs, xs, bank[b][:, :], ALU.add), S_["dve_wo"])

                norm(2 * l + 1, GF)
                if l == 0:
                    for f in range(N_FF):
                        dve.wait_ge(g["ffn_act_silu"], f + 1)
                        if f >= 4:
                            dve.wait_ge(g["ffn_down_done"], f - 3)
                        dve.tensor_tensor(hidden[:, f % 4], silu_g[:, f % 2], halves(4 + f % 4)[:, 1],
                                          ALU.mult).then_inc(g["ffn_hidden"], 1)
                    dve.wait_ge(g["ffn_down_done"], N_FF)
                    for n in range(4):
                        xs = x_sb[:, n // 2, (n % 2) * 512:(n % 2 + 1) * 512]
                        step(dve.tensor_tensor(xs, xs, bank[n][:, :], ALU.add), g["acc_read"])
                else:
                    dve.wait_ge(g["pe_router"], 2)
                    for a in range(TT):
                        step(dve.tensor_copy(logits[:, a], bank[4 + a][:, 0:NE]), g["router_read"])
                        step(dve.max(top[:, a], logits[:, a]))
                        step(dve.max_index(top_at[:, a], top[:, a], logits[:, a]))
                    step(dve.tensor_copy(top_f[:], top_at[:]))
                    r_ = [rt[:, :, k:k + 1] for k in range(4)]
                    step(dve.tensor_tensor(r_[0], top[:, :, 1:2], top[:, :, 0:1], ALU.subtract), g["router_read"])
                    dve.wait_ge(g["act_top"], 1)
                    step(dve.tensor_scalar(r_[2], r_[1], 1.0, None, ALU.add))
                    step(dve.reciprocal(r_[2], r_[2]))
                    step(dve.tensor_tensor(r_[3], r_[1], r_[2], ALU.mult))
                    step(dve.memset(w_exp[:], 0.0))
                    step(dve.memset(place[:], -1.0))
                    for a in range(TT):
                        step(dve.tensor_scalar(w_exp[:, a, 0:NE], e_iota[:], top_f[:, a, 0:1], rt[:, a, 2:3],
                                               ALU.is_equal, ALU.mult))
                        step(dve.tensor_scalar(w_tmp[:, a], e_iota[:], top_f[:, a, 1:2], rt[:, a, 3:4],
                                               ALU.is_equal, ALU.mult))
                    step(dve.tensor_tensor(w_exp[:, :, 0:NE], w_exp[:, :, 0:NE], w_tmp[:], ALU.add))
                    for a in range(TT):
                        step(dve.tensor_scalar(chosen[:, a], e_iota[:], top_f[:, a, 0:1], None, ALU.is_equal))
                        step(dve.scalar_tensor_tensor(chosen[:, a], e_iota[:], top_f[:, a, 1:2], chosen[:, a],
                                                      ALU.is_equal, ALU.add),
                             g["dve_route"] if a else g["dve_order"])
                    dve.wait_ge(g["pe_route"], 3)
                    for a in range(TT):
                        step(dve.scalar_tensor_tensor(place[:, a, 0:NE], bank[6 + a][:, 0:NE], 1.0, chosen[:, a],
                                                      ALU.add, ALU.mult))
                    step(dve.tensor_scalar(place[:, :, 0:NE], place[:, :, 0:NE], 1.0, None, ALU.subtract))
                    step(dve.reduce_max(most[:], bank[5][:, 0:NE], AX_X))
                    step(dve.tensor_scalar(crowded[:], most[:], P + 0.5, None, ALU.is_gt), g["dve_route"])
                    dve.wait_ge(g["pool_route"], 2)

                    def build_pick(e):
                        for a in range(TT):
                            at_ = place[:, a, e:e + 1] if isinstance(e, int) else place[:, a, bass.ds(e, 1)]
                            wt = w_exp[:, a, e:e + 1] if isinstance(e, int) else w_exp[:, a, bass.ds(e, 1)]
                            dve.tensor_scalar(pick[:, a], slot_iota, at_, None, ALU.is_equal)
                            last = dve.tensor_scalar(spread[:, a], slot_iota, at_, wt, ALU.is_equal, ALU.mult)
                        last.then_inc(g["dve_pick"], 1)

                    def read_picked(v):
                        for n, b in enumerate((7, 4)):
                            dve.wait_ge(g["pe_picked"], v * 2 + (n + 1))
                            gain = cols[:, 1, GF + 4 * n:GF + 4 * n + 4].rearrange("p (k o) -> p k o", o=1)
                            dve.tensor_tensor(picked[:, 4 * n:4 * n + 4],
                                              bank[b][:, :].rearrange("p (k n) -> p k n", n=P),
                                              gain.to_broadcast([P, 4, P]), ALU.mult).then_inc(g["dve_picked"], 1)

                    def picked_low(v):
                        for n in range(2):
                            dve.wait_ge(g["act_picked"], v * 2 + (n + 1))
                            k = slice(4 * n, 4 * n + 4)
                            dve.tensor_tensor(picked_lo[:, k], picked[:, k], picked_hi[:, k].bitcast(F32),
                                              ALU.subtract).then_inc(g["dve_picked_lo"], 1)

                    def expert(e, v, p_):
                        def low(n):
                            dve.wait_ge(g["split_hi"], v * NU + (n + 1))
                            r, q = n % UNIT_RING, n % SPLIT_RING
                            dve.tensor_tensor(unit_lo[:, q], unit_raw[:, r], unit_hi[:, q].bitcast(F32),
                                              ALU.subtract).then_inc(g["split_lo"], 1)

                        def turn_low(c):
                            dve.wait_ge(g["act_turned"], v * E_CH + (c + 1))
                            dve.tensor_tensor(turned_lo[:, c % 2], bank[4][:, :].rearrange("p (b n) -> p b n", n=P),
                                              turned_hi[:, c % 2].bitcast(F32),
                                              ALU.subtract).then_inc(g["dve_turned"], 1)

                        for n in range(SPLIT_RING):
                            low(n)
                        for n, (kind, c, h) in enumerate(units):
                            if kind == "gate" and h and c:
                                turn_low(c - 1)
                            if kind == "up" and h:
                                dve.wait_ge(g["ffn_act_silu"], v * E_CH + (N_FF + c + 1))
                                dve.wait_ge(g["unit_used"], v * NU + (n + 1 + SPLIT_RING))
                                dve.tensor_tensor(e_hidden[:, c % 2], e_silu[:, c % 2], bank[2 + c % 2][:, :],
                                                  ALU.mult).then_inc(g["ffn_hidden"], 1)
                            if n == unit_at["down", E_CH - 2, 1]:
                                turn_low(E_CH - 1)
                            if n + SPLIT_RING < NU:
                                low(n + SPLIT_RING)
                            if (kind, c, h) == ("down", 3, 1):
                                dve.wait_ge(g["pe_spread"], v + 1)
                                dve.tensor_copy(spreadT, bank[7][:, 0:T]).then_inc(g["dve_spread"], 1)
                                build_pick(e + 1)
                        read_picked(v + (1 + p_))
                        picked_low(v + (1 + p_))
                        dve.wait_ge(g["acc_read"], v * 4 + 4)
                        for n in range(4):
                            dve.wait_ge(g["pe_combined"], v * 4 + (n + 1))
                            xs = x_sb[:, n // 2, (n % 2) * 512:(n % 2 + 1) * 512]
                            dve.tensor_tensor(xs, xs, bank[n][:, :], ALU.add).then_inc(g["acc_read"], 1)

                    build_pick(0)
                    read_picked(0)
                    picked_low(0)
                    with dve.Fori(0, NE) as e:
                        expert(e, e, 0)
                    with dve.If(dve.value_load(crowded[0:1, 0:1], min_val=0, max_val=1) > 0):
                        dve.tensor_scalar(place[:], place[:], float(P), None, ALU.subtract).then_inc(g["dve_second"], 1)
                        dve.wait_ge(g["dve_second"], 1)
                        build_pick(0)
                        read_picked(NE + 1)
                        picked_low(NE + 1)
                        with dve.Fori(0, NE) as e:
                            expert(e, e + NE, 1)
                        dve.wait_ge(g["acc_read"], 4 + 8 * NE)
            dve.wait_ge(g["acc_read"], 4 + 4 * NE)
            norm(4, None)
            dve.wait_ge(S_["act_hn"], 5)
            dve.wait_ge(g["gain_in"], 16)
            for a in range(TT):
                step(dve.tensor_tensor(hn[:, a], hn[:, a], g_final, ALU.mult), g["final_in"] if a else g["dve_order"])

        @block.tensor
        def _(pe):
            pe.wait_ge(g["pool_const"], 1)
            pe.wait_ge(g["rows_in"], 9 * 16 * DEPTH)
            for l in range(DEPTH):
                pe.transpose(bank[7 - l][:, 0:NROW], rows[0:NROW, l], ident[0:NROW, 0:NROW]).then_inc(g["pe_params"], 1)
            pe.wait_ge(g["states_in"], 48)
            pe.transpose(bank[5][:, 0:32], srow[:], ident[0:32, 0:32])
            pe.wait_ge(g["dve_const"], 5)
            pe.transpose(bank[5][:, 32:48], ldt_row[:], ident[0:16, 0:16]).then_inc(g["pe_params"], 1)

            def arrived(n):
                pe.wait_ge(slot_full[n % RING], full_at[n])

            def weights(n, k, w, first=0):
                return slot(n % RING, k, w, first)

            def product(o, lhs, rhs, n, first=True, last=True):
                for k in range(n):
                    ins = pe.matmul(o, lhs(k), rhs(k), start=(first and k == 0), stop=(last and k == n - 1))
                return ins

            def feature_tile(o, w, c):
                return product(o, lambda k: w[:, k, c:c + P], lambda k: hT[:, k], KT)

            def norm(m):
                pe.wait_ge(S_["dve_hn"], m * PER["dve_hn"] + 1)
                pe.wait_ge(S_["act_hn"], m * PER["act_hn"] + 1)
                for b in range(4):
                    for a in range(2):
                        for tt in range(TT):
                            k = 2 * b + a
                            ins = pe.transpose(halves(b)[:, a, tt * P:(tt + 1) * P], hn[:, tt, k * P:(k + 1) * P], ident[:])
                    ins.then_inc(S_["pe_tr"], 1)
                pe.wait_ge(S_["dve_ht"], m * PER["dve_ht"] + 4)
                pe.wait_ge(S_["act_ht"], m * PER["act_ht"] + 4)

            def gate_jobs(l, first, last):
                for n in range(first, last):
                    ld = mix_at[l] + 5 + n // 2
                    if n % 2 == 0:
                        arrived(ld)
                    if n < 2:
                        pe.wait_ge(S_["act_qk"], l * PER["act_qk"] + 12)
                    else:
                        pe.wait_ge(S_["act_gate"], l * PER["act_gate"] + 2 * n - 2)
                    w = weights(ld, KT, 512)
                    for a in range(2):
                        ins = feature_tile(halves(6 + n % 2)[:, a], w, (2 * n + a) % 4 * P)
                    ins.then_inc(S_["pe_gate"], 1)

            def mats(l, half):
                if half == 0:
                    pe.wait_ge(S_["dve_v"], l * PER["dve_v"] + 2)
                    pe.wait_ge(S_["dve_u"], l * PER["dve_u"] + 2)
                else:
                    pe.wait_ge(S_["dve_att"], l * PER["dve_att"] + 4)
                    pe.wait_ge(S_["act_pt"], l * PER["act_pt"] + 4)
                for n in range(4):
                    pe.wait_ge(S_["pool_mats"], l * PER["pool_mats"] + 4 * half + n + 1)
                    for j in range(HJ):
                        ins = pe.transpose(bank[n][:, j * P:(j + 1) * P], mat_src[:, n, j * P:(j + 1) * P], ident[:])
                    ins.then_inc(S_["pe_mats"], 1)

            def states_in(l, pair):
                half, q = pair // 2, pair % 2
                pe.wait_ge(S_["act_mats"], l * PER["act_mats"] + 4 * half + 2)
                if pair == 0:
                    pe.wait_ge(S_["dve_cv"], l * PER["dve_cv"] + 2)
                    pe.wait_ge(S_["act_cg"], l * PER["act_cg"] + 2)
                else:
                    pe.wait_ge(S_["dve_bu"], l * PER["dve_bu"] + pair)
                if pair == 2:
                    pe.wait_ge(S_["dve_z"], l * PER["dve_z"] + 1)
                for c in range(2):
                    for a in range(2):
                        ins = pe.matmul(halves(4 + c)[:, a], b_mat[:, c, 2 * q + a], uT[:, half], start=True, stop=True)
                ins.then_inc(S_["pe_bu"], 1)

            def states_out(l, half):
                pe.wait_ge(S_["pool_back"], l * PER["pool_back"] + 2 * half + 2)
                pe.wait_ge(S_["dve_bu"], l * PER["dve_bu"] + 2 * half + 2)
                pe.wait_ge(S_["act_mats"], l * PER["act_mats"] + 4 * half + 4)
                for c in range(2):
                    ins = product(halves(4)[:, 0], lambda j: c_mat[:, c, j], lambda j: state[:, c, j], HJ,
                                  first=(c == 0), last=(c == 1))
                ins.then_inc(S_["pe_y"], 1)

            def scores(l, grp):
                pe.wait_ge(S_["act_qk"], l * PER["act_qk"] + 12)
                pe.wait_ge(S_["dve_f"], l * PER["dve_f"] + 5 + 4 * grp)
                pe.wait_ge(S_["act_mats"], l * PER["act_mats"] + 4 * grp + 4)
                for h in range(4):
                    hd = 4 * grp + h
                    for q, at_, n in ((0, 0, P), (1, P, T)):
                        o = bank[h][:, at_:at_ + n]
                        pe.matmul(o, qT[:, hd // 2, q * P:(q + 1) * P], k_pad[:, hd, 0:n], start=True, stop=False)
                        pe.matmul(o, f_left[:, q * P:(q + 1) * P], f_right[:, h, 0:n], start=False, stop=False)
                        ins = pe.matmul(bank[h][:, at_ + n - P:at_ + n], ident[:], causal[:], start=False, stop=True)
                    ins.then_inc(S_["pe_s"], 1)

            def probs_transposed(l, grp):
                pe.wait_ge(S_["dve_p"], l * PER["dve_p"] + 2 * grp + 2)
                for h in range(4):
                    for n in range(3):
                        ins = pe.transpose(bank[h][:, n * P:(n + 1) * P], probs[:, h, n * P:(n + 1) * P], ident[:])
                    ins.then_inc(S_["pe_pt"], 1)

            def attention(l, grp):
                pe.wait_ge(S_["act_pt"], l * PER["act_pt"] + 4 * grp + 4)
                for q in range(2):
                    j = 2 * grp + q
                    for o in range(2):
                        h = 2 * q + o
                        pe.matmul(halves(q)[:, o], v_sb[:, 0, j * P:(j + 1) * P], probsT[:, h, 0:T], start=True, stop=False)
                        ins = pe.matmul(halves(q)[:, o, P:T], v_sb[:, 1, j * P:(j + 1) * P], probsT[:, h, T:384],
                                        start=False, stop=True)
                    ins.then_inc(S_["pe_att"], 1)

            for l in range(DEPTH):
                m0 = mix_at[l]
                norm(2 * l)
                if l == 0:
                    pe.wait_ge(g["dve_theta"], 1)
                for b in range(4):
                    if b % 2 == 0:
                        arrived(m0 + b // 2)
                    w = weights(m0 + b // 2, KT, 512)
                    for a in range(2):
                        ins = feature_tile(halves(4 + b)[:, a], w, (2 * (b % 2) + a) * P)
                    ins.then_inc(S_["pe_proj"], 1)
                arrived(m0 + 2)
                w = weights(m0 + 2, KT, AW)
                for a in range(TT):
                    ins = product(bank[a][:, :], lambda k: hT[:, k, a * P:(a + 1) * P], lambda k: w[:, k], KT)
                    ins.then_inc(S_["pe_proj"], 1)
                pe.wait_ge(g["side_in"], 16 * (6 + 4 * l))
                product(bank[2][0:64, 0:T], lambda k: wf[:, k], lambda k: hT[:, k], KT).then_inc(S_["pe_proj"], 1)
                arrived(m0 + 3)
                w = weights(m0 + 3, KT, 256)
                for a in range(2):
                    ins = feature_tile(halves(3)[:, a], w, a * P)
                ins.then_inc(S_["pe_proj"], 1)
                arrived(m0 + 4)
                pe.wait_ge(S_["act_qk"], l * PER["act_qk"] + 4)
                w = weights(m0 + 4, KT, 512)
                for b in range(2):
                    for a in range(2):
                        ins = feature_tile(halves(4 + b)[:, a], w, (2 * b + a) * P)
                    ins.then_inc(S_["pe_proj"], 1)
                mats(l, 0)
                states_in(l, 0)
                scores(l, 0)
                gate_jobs(l, 0, 2)
                states_in(l, 1)
                gate_jobs(l, 2, 4)
                probs_transposed(l, 0)
                gate_jobs(l, 4, 6)
                attention(l, 0)
                states_out(l, 0)
                mats(l, 1)
                states_in(l, 2)
                scores(l, 1)
                gate_jobs(l, 6, 8)
                states_in(l, 3)
                gate_jobs(l, 8, 10)
                probs_transposed(l, 1)
                gate_jobs(l, 10, 12)
                attention(l, 1)
                pe.wait_ge(S_["act_gate"], l * PER["act_gate"] + 24)
                pe.wait_ge(S_["dve_conv"], l * PER["dve_conv"] + 2)
                product(halves(6)[:, 0], lambda k: mean_mat[:], lambda k: conv_acc[:, k], 2).then_inc(S_["pe_ln"], 1)
                states_out(l, 1)
                pe.wait_ge(S_["dve_ln"], l * PER["dve_ln"] + 1)
                product(halves(7)[:, 0], lambda k: mean_mat[:], lambda k: conv_sig[:, k], 2).then_inc(S_["pe_ln"], 1)
                arrived(m0 + 11)
                pe.wait_ge(S_["act_gelu"], l * PER["act_gelu"] + 1)
                pe.wait_ge(S_["dve_z"], l * PER["dve_z"] + 2)
                w = weights(m0 + 11, 2, 512)
                for b in range(2):
                    for a in range(2):
                        ins = product(halves(4 + b)[:, a], lambda k: w[:, k, (2 * b + a) * P:(2 * b + a + 1) * P],
                                      lambda k: ssm_g[:, k], 2)
                    ins.then_inc(S_["pe_glu"], 1)
                arrived(m0 + 12)
                arrived(m0 + 13)
                wa, ws, wc = weights(m0 + 12, 4, D), weights(m0 + 13, 2, D), weights(m0 + 13, 2, D, 2 * D)
                pe.wait_ge(S_["dve_att"], l * PER["dve_att"] + 8)
                pe.wait_ge(S_["act_pt"], l * PER["act_pt"] + 8)
                for i in range(4):
                    b0 = 3 * (i % 2)
                    if i >= 2:
                        pe.wait_ge(S_["dve_merge"], l * PER["dve_merge"] + i - 1)
                    for b, (w, r, n) in enumerate(((wa, attT, 4), (ws, ssm_z, 2), (wc, conv_sig, 2))):
                        if i == 0 and b == 1:
                            pe.wait_ge(S_["dve_glu"], l * PER["dve_glu"] + 1)
                        if i == 0 and b == 2:
                            pe.wait_ge(S_["act_conv"], l * PER["act_conv"] + 2)
                        for a in range(2):
                            c = (2 * i + a) * P
                            ins = product(halves(b0 + b)[:, a], lambda k: w[:, k, c:c + P], lambda k: r[:, k], n)
                        ins.then_inc(S_["pe_out"], 1)
                arrived(m0 + 14)
                arrived(m0 + 15)
                pe.wait_ge(S_["dve_merge"], l * PER["dve_merge"] + 4)
                for kk in range(2):
                    w = weights(m0 + 14 + kk, 4, D)
                    for k in range(4):
                        for n, b in enumerate((6, 7, 0, 1)):
                            a, h = n // 2, n % 2
                            ins = pe.matmul(bank[b][:, :], merged[:, 4 * kk + k, a * P:(a + 1) * P],
                                            w[:, k, h * 512:(h + 1) * 512], start=(kk + k == 0), stop=(kk == 1 and k == 3))
                    ins.then_inc(S_["pe_wo"], 1)

                norm(2 * l + 1)

                def down(f, wd, kk, first, last):
                    for n in range(4):
                        a, h = n // 2, n % 2
                        ins = pe.matmul(bank[n][:, :], hidden[:, f % 4, a * P:(a + 1) * P],
                                        wd[:, kk, h * 512:(h + 1) * 512], start=first, stop=last)
                    ins.then_inc(g["ffn_down_done"], 1)
                    return ins

                if l == 0:
                    for f in range(N_FF + 1):
                        if f < N_FF:
                            c, kk = f // 4, f % 4
                            n0 = ffn_at + 3 * c
                            wid = FF_CH[c][1]
                            if kk == 0:
                                arrived(n0)
                                arrived(n0 + 1)
                            if f >= 4:
                                pe.wait_ge(g["ffn_hidden"], f - 3)
                            b = halves(4 + f % 4)
                            ig = feature_tile(b[:, 0], weights(n0, KT, wid), kk * P)
                            iu = feature_tile(b[:, 1], weights(n0 + 1, KT, wid), kk * P)
                            iu.then_inc(g["ffn_up_done"], 1)
                            if kk == wid // P - 1:
                                ig.then_inc(g["gate_used"], 1)
                        if f > 0:
                            p_ = f - 1
                            c, kk = p_ // 4, p_ % 4
                            if kk == 0:
                                arrived(ffn_at + 3 * c + 2)
                            pe.wait_ge(g["ffn_hidden"], p_ + 1)
                            wid = FF_CH[c][1]
                            ins = down(p_, weights(ffn_at + 3 * c + 2, wid // P, D), kk, p_ == 0, p_ == N_FF - 1)
                else:
                    pe.wait_ge(g["side_in"], 16 * 6)
                    for a in range(TT):
                        o = bank[4 + a][:, 0:NE]
                        ins = pe.matmul(o, ones_row[:], b_router[:], start=True, stop=False)
                        if a == 0:
                            ins.then_inc(g["unit_used"], SPLIT_RING)
                        product(o, lambda k: hT[:, k, a * P:(a + 1) * P], lambda k: w_router[:, k], KT,
                                first=False).then_inc(g["pe_router"], 1)
                    pe.wait_ge(g["router_read"], 2)
                    pe.wait_ge(g["dve_route"], 1)
                    pe.wait_ge(g["pool_route"], 2)
                    pe.matmul(bank[6][:, 0:NE], before, chosen[:, 0], start=True, stop=True).then_inc(g["pe_route"], 1)
                    pe.matmul(bank[7][:, 0:NE], ones_mat, chosen[:, 0], start=True, stop=False)
                    pe.matmul(bank[7][:, 0:NE], before, chosen[:, 1], start=False, stop=True).then_inc(g["pe_route"], 1)
                    product(bank[5][:, 0:NE], lambda k: ones_mat, lambda k: chosen[:, k], 2).then_inc(g["pe_route"], 1)

                    def gather(v):
                        pe.wait_ge(g["dve_pick"], v + 1)
                        for n, b in enumerate((7, 4)):
                            for k in range(4):
                                f0 = (4 * n + k) * P
                                ins = product(bank[b][:, k * P:(k + 1) * P], lambda a: hn[:, a, f0:f0 + P],
                                              lambda a: pick[:, a], TT)
                            ins.then_inc(g["pe_picked"], 1)

                    def expert(e, v, p_):
                        def unit(n, k):
                            pe.wait_ge(g["split_lo"], v * NU + (n + 1 + UNIT_RING))
                            q = n % SPLIT_RING
                            return [u[:, q].rearrange("p (k n) -> p k n", k=k) for u in (unit_hi, unit_lo)]

                        def split_product(o, x_hi, x_lo, w_hi, w_lo, first, last):
                            pe.matmul(o, x_hi, w_hi, start=first, stop=False)
                            pe.matmul(o, x_hi, w_lo, start=False, stop=False)
                            return pe.matmul(o, x_lo, w_hi, start=False, stop=last)

                        def turn(c):
                            pe.wait_ge(g["ffn_hidden"], v * E_CH + (N_FF + c + 1))
                            if c:
                                pe.wait_ge(g["dve_turned"], v * E_CH + c)
                            for k in range(4):
                                ins = pe.transpose(bank[4][:, k * P:(k + 1) * P],
                                                   e_hidden[:, c % 2, k * P:(k + 1) * P], ident[:])
                            ins.then_inc(g["pe_e_turned"], 1)

                        pe.wait_ge(g["dve_picked_lo"], v * 2 + (2 + 2 * p_))
                        for n, (kind, c, h) in enumerate(units):
                            if kind == "down":
                                pe.wait_ge(g["dve_turned"], v * E_CH + (c + 1))
                                w_hi, w_lo = unit(n, 2)
                                for k in range(2):
                                    for b in range(2):
                                        cols_ = slice(b * 512, (b + 1) * 512)
                                        ins = split_product(bank[5 + b][:, :], turned_hi[:, c % 2, 2 * h + k],
                                                            turned_lo[:, c % 2, 2 * h + k], w_hi[:, k, cols_],
                                                            w_lo[:, k, cols_], c + h + k == 0,
                                                            c == E_CH - 1 and h + k == 2)
                            else:
                                b = c % 2 + (2 if kind == "up" else 0)
                                if h == 0 and c < 2:
                                    pe.wait_ge(g["acc_read"], v * 4 + (b + 1))
                                elif h == 0:
                                    pe.wait_ge(g["ffn_act_silu" if kind == "gate" else "ffn_hidden"],
                                               v * E_CH + (N_FF + c - 1))
                                w_hi, w_lo = unit(n, 4)
                                for k in range(4):
                                    ins = split_product(bank[b][:, :], picked_hi[:, 4 * h + k], picked_lo[:, 4 * h + k],
                                                        w_hi[:, k], w_lo[:, k], h + k == 0, h == 1 and k == 3)
                            ins.then_inc(g["unit_used"], 1)
                            if kind == "gate" and h and c:
                                turn(c - 1)
                            if kind == "up" and h and c == 3:
                                for a in range(TT):
                                    ins = pe.transpose(bank[7][:, a * P:(a + 1) * P], spread[:, a], ident[:])
                                ins.then_inc(g["pe_spread"], 1)
                            if n == unit_at["down", E_CH - 2, 1]:
                                turn(E_CH - 1)
                        pe.wait_ge(g["dve_spread"], v + 1)
                        gather(v + (1 + p_))
                        pe.wait_ge(g["act_e_out"], v * 2 + 2)
                        for n in range(4):
                            a, h = n // 2, n % 2
                            pe.matmul(bank[n][:, :], spreadT[:, a * P:(a + 1) * P], e_out[:, h * 512:(h + 1) * 512],
                                      start=True, stop=True).then_inc(g["pe_combined"], 1)

                    gather(0)
                    with pe.Fori(0, NE) as e:
                        expert(e, e, 0)
                    with pe.If(pe.value_load(crowded[0:1, 0:1], min_val=0, max_val=1) > 0):
                        gather(NE + 1)
                        with pe.Fori(0, NE) as e:
                            expert(e, e + NE, 1)
                        pe.wait_ge(g["acc_read"], 4 + 8 * NE)


_INS = ["x", "g_mix", "w_in", "b_in", "ssm_a_re", "ssm_a_im", "ssm_log_dt", "ssm_b_re", "ssm_b_im", "ssm_c_re",
        "ssm_c_im", "ssm_d", "ssm_w_glu", "conv_w", "conv_b", "conv_ln_g", "conv_ln_b", "w_att_out", "w_ssm_out",
        "w_conv_out", "w_o", "g_ffn", "ffn_w_gate", "ffn_w_up", "ffn_w_down", "moe_w_router", "moe_b_router",
        "moe_w_gate", "moe_w_up", "moe_w_down", "g_final"]


def kernel(**inputs):
    import numpy as np
    import concourse.bacc as bacc
    from concourse.bass_utils import run_bass_kernel_spmd

    nc = bacc.Bacc("TRN2", target_bir_lowering=False, num_devices=1)
    arrays, t = {}, {}
    for name in _INS:
        a = np.ascontiguousarray(inputs[name])
        arrays[f"in_{name}"] = a
        t[name] = nc.dram_tensor(f"in_{name}", a.shape, mybir.dt.from_np(a.dtype), kind="ExternalInput").ap()
    shape = inputs["x"].shape
    out = nc.dram_tensor("out", shape, F32, kind="ExternalOutput").ap()
    hybrid_trunk(nc, t, out)
    return run_bass_kernel_spmd(nc, [arrays], core_ids=[0]).results[0]["out"]
```

```python
from contextlib import ExitStack

import concourse.bass as bass
from concourse import mybir

P = 128
F32 = mybir.dt.float32
U32 = mybir.dt.uint32
F32R = mybir.dt.float32r
ALU = mybir.AluOpType
ACT = mybir.ActivationFunctionType
AX_X = mybir.AxisListType.X

EPS = 1e-6
MASKED = -1e30
TWO_PI = 6.283185307179586
TWO_PI_A = 6.28125
TWO_PI_B = 0.0019340515136718750
TWO_PI_C = TWO_PI - TWO_PI_A - TWO_PI_B
ROUND_MAGIC = 12582912.0

UNIT = 2048
TRUNK_RING = 4
TRUNK_SPLIT = 3
UNIT_RING = 7
SPLIT_RING = 3


def hybrid_trunk(nc, t, out):
    DEPTH, D, N_IN = t["w_in"].shape
    T = t["x"].shape[1]
    KT, TT = D // P, T // P
    G, S, GH = t["ssm_b_re"].shape[1:]
    H = (N_IN - 3 * D - G * GH - 2 * t["conv_w"].shape[2]) // (3 * 64 + 1)
    DH = 64
    AW = H * DH
    V_AT, F_AT = 2 * AW, 3 * AW
    U_AT = F_AT + H
    CK, CW = t["conv_w"].shape[1:]
    DFF = t["ffn_w_gate"].shape[2]
    NE, _, DFE = t["moe_w_gate"].shape[1:]
    NJ = G * S // P
    HJ = NJ // 2
    PAD = CK - 1
    assert (D, T, AW, G * GH, CW, NJ) == (1024, 256, 512, 256, 256, 8) and DEPTH == 2

    ctx = ExitStack()
    with ctx:
        def sb(name, shape, dt=F32):
            handle = ctx.enter_context(nc.sbuf_tensor(name, shape, dt))
            size = 4
            for n in shape[1:]:
                size *= n
            address[name] = nc.sbuf_base - size
            return handle

        address = {}

        def over(name, shape, dt, where, at=0):
            return nc.alloc_sbuf_tensor_at(name, shape, dt, offset=address[where] + at)

        WEIGHTS = (TRUNK_RING + TRUNK_SPLIT) * UNIT
        arena = sb("arena", [P, WEIGHTS + KT * T + 48 * T])
        raw = arena[:, 0:TRUNK_RING * UNIT].rearrange("p (r n) -> p r n", n=UNIT)
        raw_hi = over("raw_hi", [P, TRUNK_SPLIT, UNIT], F32R, "arena", 4 * TRUNK_RING * UNIT)
        raw_lo = over("raw_lo", [P, TRUNK_RING, UNIT], F32R, "arena")
        hT_hi = sb("hT_hi", [P, KT, T], F32R)
        hT_lo = over("hT_lo", [P, KT, T], F32R, "arena", 4 * WEIGHTS)
        assert UNIT_RING * UNIT == WEIGHTS
        at = WEIGHTS + KT * T
        MIX_ONLY = at
        gates = arena[:, at:at + 24 * T].rearrange("p (n t) -> p n t", t=T)
        at += 24 * T
        phase = arena[:, at:at + 2 * HJ * T].rearrange("p (c j t) -> p c j t", c=2, t=T)
        at += 2 * HJ * T
        state = arena[:, at:at + 2 * HJ * T].rearrange("p (c j t) -> p c j t", c=2, t=T)
        at += 2 * HJ * T
        rot_tmp = arena[:, at:at + 1024].rearrange("p (c j t) -> p c j t", c=2, t=T)
        at += 1024
        back_flat = arena[:, at:at + 1024]
        back_tmp = back_flat.rearrange("p (c j t) -> p c j t", c=2, t=T)
        at += 1024
        assert at == MIX_ONLY + 48 * T

        x_sb = sb("x_sb", [P, TT, D])
        hn = sb("hn", [P, TT, D])
        merged_hi, merged_lo = hT_hi, hT_lo
        merged = hn[:].rearrange("p a (b t) -> p (a b) t", t=T)
        mat_src = hn[:].rearrange("p a (b n) -> p (a b) n", n=512)
        qT = sb("qT", [P, AW // P, T])
        k_pad = sb("k_pad", [P, H, T])
        v_sb = sb("v_sb", [P, TT, AW])
        f_left = sb("f_left", [P, T])
        f_right = sb("f_right", [P, 4, T])
        f_sum = sb("f_sum", [64, T])
        probs = sb("probs", [P, 4, 384])
        probsT = sb("probsT", [P, 4, 384])
        attT = sb("attT", [P, AW // P, T])
        uT = sb("uT", [P, 2, T])
        conv_in = sb("conv_in", [P, 2, PAD + T])
        conv_acc = sb("conv_acc", [P, 2, T])
        conv_sig = sb("conv_sig", [P, 2, T])
        ssm_z = uT
        ssm_g = sb("ssm_g", [P, 2, T])
        ssm_sig = ssm_g
        b_mat = sb("b_mat", [P, 2, HJ, P])
        c_mat = sb("c_mat", [P, 2, HJ, P])
        silu_g = probs[:].rearrange("p a b -> p (a b)")[:, 0:4 * T].rearrange("p (r a t) -> p r a t", a=2, t=T)
        hidden = probsT[:].rearrange("p a b -> p (a b)")[:, 0:4 * T].rearrange("p (r a t) -> p r a t", a=2, t=T)
        small_hi = over("small_hi", [P, KT, 64], F32R, "probs")
        small_lo = over("small_lo", [P, KT, 64], F32R, "probsT")
        hidden_hi = over("hidden_hi", [P, 2, 2, T], F32R, "qT")
        hidden_lo = over("hidden_lo", [P, 2, 2, T], F32R, "attT")

        probs_f, probsT_f = (b[:].rearrange("p a b -> p (a b)") for b in (probs, probsT))
        e_silu = probs_f[:, 0:1024].rearrange("p (r n) -> p r n", n=512)
        spreadT = probs_f[:, 1024:1024 + T]
        e_hidden = probsT_f[:, 0:1024].rearrange("p (r n) -> p r n", n=512)
        pick = conv_in[:, :, 0:P]
        spread = probsT_f[:, 1024:1024 + TT * P].rearrange("p (a n) -> p a n", a=TT)
        picked = k_pad[:, 0:4].rearrange("p a (b n) -> p (a b) n", n=P)
        picked_hi = over("picked_hi", [P, KT, P], F32R, "attT")
        picked_lo = over("picked_lo", [P, KT, P], F32R, "arena", 4 * UNIT_RING * UNIT)
        turned_hi = over("turned_hi", [P, 2, 4, P], F32R, "v_sb")
        turned_lo = over("turned_lo", [P, 2, 4, P], F32R, "arena", 4 * UNIT_RING * UNIT + 4096)
        unit_raw = arena[:, 0:UNIT_RING * UNIT].rearrange("p (r n) -> p r n", n=UNIT)
        unit_hi = over("unit_hi", [P, SPLIT_RING, UNIT], F32R, "arena", 4 * MIX_ONLY)
        unit_lo = over("unit_lo", [P, SPLIT_RING, UNIT], F32R, "arena", 4 * (MIX_ONLY + SPLIT_RING * UNIT))
        e_out = k_pad[:, 4:8].rearrange("p a t -> p (a t)")
        acc_f = conv_acc[:].rearrange("p a t -> p (a t)")
        before, ones_mat, slot_iota = acc_f[:, 0:P], acc_f[:, P:2 * P], acc_f[:, 2 * P:3 * P]

        ident = sb("ident", [P, P])
        causal = sb("causal", [P, P])
        mean_mat = sb("mean_mat", [P, P])
        b_mask = sb("b_mask", [P, HJ * 8])
        c_mask = sb("c_mask", [P, 2, 8])
        f_scale = sb("f_scale", [64, H + 1])
        f_shift = sb("f_shift", [64, H + 1])

        NROW = 30 + 12 + 8 + 8 + 8 + CK * CW // P
        rows = back_flat[:, 512:512 + DEPTH * P].rearrange("p (l n) -> p l n", l=DEPTH)
        cols = sb("cols", [P, DEPTH, NROW])
        srow = sb("srow", [32, P])
        ldt_row = sb("ldt_row", [16, P])
        ones_col = sb("ones_col", [64, 1])
        ldt = sb("ldt", [16, 2])
        scol = sb("scol", [P, 48])
        b_raw = sb("b_raw", [P, 2, DEPTH, NJ, GH])
        b_bar = sb("b_bar", [P, 2, NJ, GH])
        b_tmp = back_flat[:, 0:2 * NJ * GH].rearrange("p (c j h) -> p c j h", c=2, j=NJ)
        c_raw = sb("c_raw", [P, 2, DEPTH, 2, S])
        wf = sb("wf", [P, KT, 64])
        bf = sb("bf", [64, DEPTH])
        w_router = sb("w_router", [P, KT, NE])
        b_router = sb("b_router", [NE, 1])
        g_final = qT[:].rearrange("p a t -> p (a t)")
        fz = rot_tmp[0:64, 0]
        SC = DEPTH * NJ
        sm = sb("sm", [P, 14, SC])
        rot_pow = sb("rot_pow", [P, 2, 8, SC])
        st = sb("st", [P, 5, 3, TT])
        att_max = sb("att_max", [P, 2, 4])
        att_sum = sb("att_sum", [P, 2, 4])
        att_rs = sb("att_rs", [P, 2, 4])
        ln_r = rot_tmp[:, 0, 0]
        logits_T = f_sum[0:NE]
        logits = sb("logits", [P, TT, NE])
        top = sb("top", [P, TT, 8])
        top_at = sb("top_at", [P, TT, 8], U32)
        top_f = sb("top_f", [P, TT, 8])
        rt = sb("rt", [P, TT, 4])
        e_iota = sb("e_iota", [P, NE])
        w_exp = sb("w_exp", [P, TT, NE])
        chosen = sb("chosen", [P, TT, NE])
        place = sb("place", [P, TT, NE])
        most = sb("most", [P, 1])
        crowded = sb("crowded", [P, 1], mybir.dt.int32)
        w_tmp = sb("w_tmp", [P, TT, NE])

        bank = [ctx.enter_context(nc.psum_tensor(f"bank{i}", [P, 512], F32)) for i in range(8)]

        def halves(b):
            return bank[b][:, :].rearrange("p (a t) -> p a t", a=2)

        BI = 0
        QK = 30
        GM, GF = 42, 50
        SD, CB, LG, LB = 58, 60, 62, 64
        CWC = 66

        def sems(names):
            return {n: ctx.enter_context(nc.semaphore(n)) for n in names.split()}

        raw_full = [ctx.enter_context(nc.semaphore(f"raw_full{i}")) for i in range(TRUNK_RING)]
        unit_full = [ctx.enter_context(nc.semaphore(f"unit_full{i}")) for i in range(UNIT_RING)]
        rows_in = [ctx.enter_context(nc.semaphore(f"rows_in{l}")) for l in range(DEPTH)]
        g = sems("x_in states_in mats_in side_in gain_in final_in out_done "
                 "trunk_hi trunk_lo trunk_used pe_params act_params "
                 "pool_const pool_order dve_const dve_order dve_theta act_trig dve_states "
                 "ffn_act_silu ffn_hidden ffn_act_hi ffn_lo acc_read "
                 "small_hi small_lo pe_router router_read act_top "
                 "dve_second pool_route dve_route pe_route dve_pick pe_picked dve_picked pe_spread dve_spread "
                 "pe_e_turned act_turned dve_turned act_picked dve_picked_lo "
                 "act_e_out pe_combined split_hi split_lo unit_used")
        PER = dict(pe_f=1, act_qk=12, dve_v=2, dve_fz=2, act_f=2, dve_f=9, dve_u=2, act_cg=2, dve_cv=2,
                   pool_mats=8, pe_mats=8, act_mats=8, pool_phase=2, pe_bu=4, dve_bu=4, dve_scan=4, pool_back=4,
                   pe_y=2, dve_z=2, act_gelu=1, pe_glu=2, act_glu=1, dve_glu=1, act_gate=24,
                   pe_s=8, dve_max=2, act_exp=16, dve_p=4, pe_pt=8, act_pt=8, pe_att=4, dve_att=8,
                   dve_conv=2, pe_ln=2, dve_ln=4, act_ln=1, act_conv=2, pe_out=12, dve_merge=4,
                   act_merged=4, dve_merged=4, dve_wo=4,
                   act_ss=2, dve_rv=1, act_sd=1, dve_hn=1, act_hn=1, pe_tr=4, dve_ht=8, act_ht=8)
        S_ = sems(" ".join(PER))

        loads, free_at, split_of, place_of = [], [], [], []

        def k_tiles(w):
            return w.rearrange("(k p) n -> p k n", p=P)

        def load(free, *parts):
            r, at, out_ = len(loads) % TRUNK_RING, 0, []
            for src in parts:
                k, n = src.shape[1:]
                out_.append((raw[:, r, at:at + k * n].rearrange("p (k n) -> p k n", n=n), src))
                at += k * n
            assert at <= UNIT
            loads.append(out_)
            if free is None:
                place_of.append(len(loads) - 1)
                free = (g["trunk_used"], len(place_of))
                split_of.append(len(place_of) - 1)
            else:
                split_of.append(None)
            free_at.append(free)

        U_V, U_U, U_C, U_G, U_O, U_MIX = 4, 6, 7, 9, 21, 25
        N_PAIR = DFF // (2 * P)
        dense = []
        for q in range(N_PAIR):
            dense += [("gate", q), ("up", q)] + ([("down", q - 1)] if q else [])
        dense += [("down", N_PAIR - 1)]
        split_at = {}
        plain_at = {}
        for l in range(DEPTH):
            split_at[l] = len(place_of)
            w = t["w_in"][l]
            for c in [*range(0, F_AT, 256), *range(U_AT, N_IN, 256)]:
                load(None, k_tiles(w[:, c:c + 256]))
            plain_at[l] = len(loads)
            load((S_["pe_glu"], l * PER["pe_glu"] + 2), k_tiles(t["ssm_w_glu"][l]))
            for i in range(4):
                c = slice(256 * i, 256 * i + 256)
                load((S_["pe_out"], l * PER["pe_out"] + 3 * i + 3), k_tiles(t["w_att_out"][l][:, c]),
                     k_tiles(t["w_ssm_out"][l][:, c]), k_tiles(t["w_conv_out"][l][:, c]))
            for i in range(4):
                load(None, k_tiles(t["w_o"][l, 256 * i:256 * i + 256]))
            if l == 0:
                split_at["dense"] = len(place_of)
                for kind, q in dense:
                    w = t["ffn_w_" + kind][0]
                    c = slice(256 * q, 256 * q + 256)
                    load(None, k_tiles(w[c, :] if kind == "down" else w[:, c]))
        assert split_at["dense"] == split_at[0] + U_MIX

        def ahead(m):
            for l in range(DEPTH):
                if split_at[l] <= m < split_at[l] + U_O:
                    return min(m + TRUNK_SPLIT, split_at[l] + U_O) - 1
            return m + TRUNK_SPLIT - 1

        full_at, count = [], [0] * TRUNK_RING
        for n, parts in enumerate(loads):
            count[n % TRUNK_RING] += 16 * len(parts)
            full_at.append(count[n % TRUNK_RING])
        last_in = [max(n for n in range(len(loads)) if n % TRUNK_RING == r) for r in range(TRUNK_RING)]

        E_CH = DFE // 512
        units = []
        for c in range(E_CH + 1):
            if c < E_CH:
                units += [("gate", c, 0), ("gate", c, 1), ("up", c, 0), ("up", c, 1)]
            if c:
                units += [("down", c - 1, 0), ("down", c - 1, 1)]
        NU = len(units)
        unit_at = {u: n for n, u in enumerate(units)}
        assert NU % UNIT_RING == 0 and NU % SPLIT_RING == 0 and DFE % 512 == 0
        block = ctx.enter_context(nc.Block())

        def parameter_rows(engine, l):
            for at, src in ((BI, t["b_in"][l, U_AT:N_IN].rearrange("(r n) -> r n", n=P)),
                            (QK, t["b_in"][l, 0:F_AT].rearrange("(r n) -> r n", n=P)),
                            (GM, t["g_mix"][l].rearrange("(r n) -> r n", n=P)),
                            (GF, t["g_ffn"][l].rearrange("(r n) -> r n", n=P)),
                            (SD, t["ssm_d"][l].rearrange("(r a) h -> r (a h)", r=2)),
                            (CB, t["conv_b"][l].rearrange("(r n) -> r n", n=P)),
                            (LG, t["conv_ln_g"][l].rearrange("(r n) -> r n", n=P)),
                            (LB, t["conv_ln_b"][l].rearrange("(r n) -> r n", n=P)),
                            (CWC, t["conv_w"][l].rearrange("k (r n) -> (k r) n", n=P))):
                engine.dma_start(rows[at:at + src.shape[0], l, :], src).then_inc(rows_in[l], 16)

        @block.sync
        def _(sp):
            sp.dma_start(x_sb[:], t["x"][0].rearrange("(a p) d -> p a d", p=P)).then_inc(g["x_in"], 16)
            for n, parts in enumerate(loads):
                if n == 1:
                    parameter_rows(sp, 1)
                if n == 2:
                    for l in range(DEPTH):
                        for c, (b, cc) in enumerate((("ssm_b_re", "ssm_c_re"), ("ssm_b_im", "ssm_c_im"))):
                            sp.dma_start(b_raw[:, c, l], t[b][l].rearrange("(j a) s h -> (a s) j h", a=2)).then_inc(g["mats_in"], 16)
                            sp.dma_start(c_raw[:, c, l], t[cc][l].rearrange("(i a) h s -> (a h) i s", i=2)).then_inc(g["mats_in"], 16)
                if n >= TRUNK_RING:
                    sp.wait_ge(*free_at[n - TRUNK_RING])
                for dst, src in parts:
                    sp.dma_start(dst, src).then_inc(raw_full[n % TRUNK_RING], 16)

            def expert_loads(e, v):
                for n, (kind, c, h) in enumerate(units):
                    r = n % UNIT_RING
                    w = t["moe_w_" + kind][0, bass.ds(e, 1)]
                    if kind == "down":
                        w = w[:, c * 512 + h * 256:c * 512 + h * 256 + 256, :]
                        dst = unit_raw[:, r].rearrange("p (k n) -> p k n", n=D)
                    else:
                        w = w[:, h * 512:(h + 1) * 512, c * 512:(c + 1) * 512]
                        dst = unit_raw[:, r].rearrange("p (k n) -> p k n", n=512)
                    if n < UNIT_RING:
                        sp.wait_ge(*(free_at[last_in[r]] if r < TRUNK_RING else (g["trunk_used"], len(place_of))))
                    sp.wait_ge(g["split_lo"], v * NU + (n + 1))
                    sp.dma_start(dst, w.rearrange("o (k p) n -> p (o k) n", p=P)).then_inc(unit_full[r], 16)

            with sp.Fori(0, NE) as e:
                expert_loads(e, e)
            sp.wait_ge(g["dve_route"], 2)
            with sp.If(sp.value_load(crowded[0:1, 0:1], min_val=0, max_val=1) > 0):
                with sp.Fori(0, NE) as e:
                    expert_loads(e, e + NE)
            sp.wait_ge(g["final_in"], 1)
            sp.dma_start(out[0].rearrange("(a p) d -> p a d", p=P), hn[:]).then_inc(g["out_done"], 16)
            sp.wait_ge(g["out_done"], 16)

        @block.gpsimd
        def _(pool):
            done = [0]

            def link(ins):
                done[0] += 1
                ins.then_inc(g["pool_order"], 1)
                pool.wait_ge(g["pool_order"], done[0])

            def const(ins):
                ins.then_inc(g["pool_const"], 1)

            link(pool.memset(ident[:], 0.0))
            const(pool.affine_select(out=ident[:], in_=ident[:], compare_op=ALU.not_equal, fill=1.0, base=0,
                                     pattern=[[-1, P]], channel_multiplier=1))
            link(pool.memset(causal[:], 0.0))
            const(pool.affine_select(out=causal[:], in_=causal[:], compare_op=ALU.is_ge, fill=MASKED, base=0,
                                     pattern=[[-1, P]], channel_multiplier=1))
            link(pool.memset(c_mask[:, 0, :], 1.0))
            link(pool.affine_select(out=c_mask[:, 0, :], in_=c_mask[:, 0, :], compare_op=ALU.is_ge, fill=0.0, base=0,
                                    pattern=[[-GH, 8]], channel_multiplier=1))
            link(pool.affine_select(out=c_mask[:, 0, :], in_=c_mask[:, 0, :], compare_op=ALU.is_ge, fill=0.0,
                                    base=GH - 1, pattern=[[GH, 8]], channel_multiplier=-1))
            link(pool.tensor_scalar(c_mask[:, 1, :], c_mask[:, 0, :], -1.0, None, ALU.mult))
            link(pool.memset(b_mask[:], 0.0))
            link(pool.memset(b_mask[0:64, 0:3 * 10 + 1:10], 1.0))
            link(pool.memset(b_mask[64:P, 1:3 * 10 + 2:10], 1.0))
            link(pool.memset(f_scale[:], 0.0))
            link(pool.memset(f_shift[:], 0.0))
            link(pool.memset(f_scale[0:H, H:H + 1], 8.0))
            link(pool.memset(f_shift[32:32 + H, H:H + 1], 1.0))
            link(pool.affine_select(out=f_scale[:, 0:H], in_=f_scale[:, 0:H], compare_op=ALU.not_equal, fill=-8.0,
                                    base=-32, pattern=[[-1, H]], channel_multiplier=1))
            const(pool.affine_select(out=f_shift[:, 0:H], in_=f_shift[:, 0:H], compare_op=ALU.not_equal, fill=1.0,
                                     base=0, pattern=[[-1, H]], channel_multiplier=1))
            link(pool.memset(k_pad[:], 0.0))
            link(pool.memset(conv_in[:], 0.0))
            const(pool.iota(e_iota[:], [[1, NE]], base=0, channel_multiplier=0,
                            allow_small_or_imprecise_dtypes=True))

            pool.wait_ge(g["dve_const"], 2)
            def forget_weights(l):
                for at_ in (0, 32):
                    pool.dma_start(wf[:, :, at_:at_ + H], k_tiles(t["w_in"][l][:, F_AT:U_AT])).then_inc(g["side_in"], 16)
                    pool.dma_start(bf[at_:at_ + H, l:l + 1],
                                   t["b_in"][l, F_AT:U_AT].rearrange("(n o) -> n o", o=1)).then_inc(g["side_in"], 16)

            forget_weights(0)
            pool.dma_start(w_router[:], k_tiles(t["moe_w_router"][0])).then_inc(g["side_in"], 16)
            pool.dma_start(b_router[:], t["moe_b_router"][0].rearrange("(n o) -> n o", o=1)).then_inc(g["side_in"], 16)

            for l in range(DEPTH):
                if l:
                    pool.wait_ge(S_["pe_f"], l)
                    forget_weights(l)
                pool.wait_ge(g["dve_states"], 1)
                pool.wait_ge(g["mats_in"], 128)
                pool.wait_ge(g["pe_params"], 3)
                j0 = l * NJ
                f_re, f_im = (sm[:, k, j0:j0 + NJ].rearrange("p (j o) -> p j o", o=1).to_broadcast([P, NJ, GH])
                              for k in (10, 11))
                link(pool.tensor_tensor(b_bar[:, 0], b_raw[:, 0, l], f_re, ALU.mult))
                link(pool.tensor_tensor(b_tmp[:, 0], b_raw[:, 1, l], f_im, ALU.mult))
                link(pool.tensor_tensor(b_bar[:, 1], b_raw[:, 1, l], f_re, ALU.mult))
                link(pool.tensor_tensor(b_tmp[:, 1], b_raw[:, 0, l], f_im, ALU.mult))
                link(pool.tensor_tensor(b_bar[:, 0], b_bar[:, 0], b_tmp[:, 0], ALU.subtract))
                link(pool.tensor_tensor(b_bar[:, 1], b_bar[:, 1], b_tmp[:, 1], ALU.add))
                pool.wait_ge(S_["pe_tr"], 2 * l * PER["pe_tr"] + 4)
                def spread_matrices(half):
                    if half:
                        pool.wait_ge(S_["pe_mats"], l * PER["pe_mats"] + 4)
                    for c in range(2):
                        o = mat_src[:, c].rearrange("p (j g h) -> p j g h", j=HJ, g=8)
                        src = b_bar[:, c, half * HJ:(half + 1) * HJ]
                        pool.tensor_tensor(
                            o, src.rearrange("p j (o h) -> p j o h", o=1).to_broadcast([P, HJ, 8, GH]),
                            b_mask[:].rearrange("p (j g o) -> p j g o", g=8, o=1).to_broadcast([P, HJ, 8, GH]),
                            ALU.mult).then_inc(S_["pool_mats"], 1)
                    for c in range(2):
                        o = mat_src[:, 2 + c].rearrange("p (g s) -> p g s", g=8)
                        pool.tensor_tensor(
                            o, c_raw[:, c, l, half:half + 1].to_broadcast([P, 8, S]),
                            c_mask[:, c].rearrange("p (g o) -> p g o", o=1).to_broadcast([P, 8, S]),
                            ALU.mult).then_inc(S_["pool_mats"], 1)

                spread_matrices(0)
                for half in range(2):
                    if l and half == 0:
                        pool.wait_ge(S_["dve_bu"], l * PER["dve_bu"])
                    if half:
                        pool.wait_ge(S_["dve_bu"], l * PER["dve_bu"] + 2)
                        pool.wait_ge(S_["pool_back"], l * PER["pool_back"] + 2)
                    cs, sn = phase[:, 0], phase[:, 1]
                    link(pool.memset(cs[:, :, 0:1], 1.0))
                    link(pool.memset(sn[:, :, 0:1], 0.0))
                    w, n = 1, 0
                    while w < T:
                        zj = j0 + half * HJ
                        z_re, z_im = (rot_pow[:, c, n, zj:zj + HJ].rearrange("p (j o) -> p j o", o=1)
                                      .to_broadcast([P, HJ, w]) for c in range(2))
                        tmp = [back_tmp.rearrange("p c j t -> p (c j t)")[:, a * HJ * w:(a + 1) * HJ * w]
                               .rearrange("p (j t) -> p j t", t=w) for a in range(2)]
                        link(pool.tensor_tensor(tmp[0], cs[:, :, 0:w], z_re, ALU.mult))
                        link(pool.tensor_tensor(tmp[1], sn[:, :, 0:w], z_im, ALU.mult))
                        link(pool.tensor_tensor(cs[:, :, w:2 * w], tmp[0], tmp[1], ALU.subtract))
                        link(pool.tensor_tensor(tmp[0], cs[:, :, 0:w], z_im, ALU.mult))
                        link(pool.tensor_tensor(tmp[1], sn[:, :, 0:w], z_re, ALU.mult))
                        last = pool.tensor_tensor(sn[:, :, w:2 * w], tmp[0], tmp[1], ALU.add)
                        w, n = 2 * w, n + 1
                        if w < T:
                            link(last)
                        else:
                            last.then_inc(S_["pool_phase"], 1)
                            pool.wait_ge(S_["pool_phase"], l * PER["pool_phase"] + half + 1)
                    if half == 0:
                        spread_matrices(1)
                    for q in range(2):
                        pair = 2 * half + q
                        pool.wait_ge(S_["dve_scan"], l * PER["dve_scan"] + pair + 1)
                        y_re, y_im = (state[:, c, 2 * q:2 * q + 2] for c in range(2))
                        c_, s_ = (phase[:, c, 2 * q:2 * q + 2] for c in range(2))
                        ta, tb = back_tmp[:, 0], back_tmp[:, 1]
                        link(pool.tensor_tensor(ta, y_im, s_, ALU.mult))
                        link(pool.tensor_tensor(tb, y_re, s_, ALU.mult))
                        link(pool.tensor_tensor(y_re, y_re, c_, ALU.mult))
                        link(pool.tensor_tensor(y_im, y_im, c_, ALU.mult))
                        link(pool.tensor_tensor(y_re, y_re, ta, ALU.subtract))
                        pool.tensor_tensor(y_im, y_im, tb, ALU.add).then_inc(S_["pool_back"], 1)
                        pool.wait_ge(S_["pool_back"], l * PER["pool_back"] + pair + 1)
            pool.wait_ge(S_["dve_merge"], DEPTH * 4)
            link(pool.memset(acc_f[:, 0:2 * P], 1.0))
            pool.affine_select(out=before, in_=before, compare_op=ALU.is_ge, fill=0.0, base=-1,
                               pattern=[[1, P]], channel_multiplier=-1).then_inc(g["pool_route"], 1)
            pool.iota(slot_iota, [[1, P]], base=0, channel_multiplier=0,
                      allow_small_or_imprecise_dtypes=True).then_inc(g["pool_route"], 1)
            pool.dma_start(g_final, t["g_final"].rearrange("(o d) -> o d", o=1).to_broadcast([P, D])).then_inc(g["gain_in"], 16)

        @block.scalar
        def _(act):
            parameter_rows(act, 0)
            for dst, src in ((srow[0:16, :], t["ssm_a_re"]), (srow[16:32, :], t["ssm_a_im"])):
                act.dma_start(dst, src.rearrange("l (j a) s -> (l j) (a s)", a=2)).then_inc(g["states_in"], 16)
            act.dma_start(ldt[:, :], t["ssm_log_dt"].rearrange("l (j a) -> (l j) a", a=2)).then_inc(g["states_in"], 16)

            def layer_params(l):
                act.wait_ge(g["pe_params"], (1, 3)[l])
                act.activation(cols[:, l], bank[7 - l][:, 0:NROW], ACT.Copy).then_inc(g["act_params"], 1)

            def state_functions():
                act.wait_ge(g["dve_theta"], 1)
                act.activation(sm[:, 0], sm[:, 0], ACT.Exp).then_inc(g["act_trig"], 1)
                act.wait_ge(g["dve_theta"], 2)
                act.activation(sm[:, 3], sm[:, 3], ACT.Exp).then_inc(g["act_trig"], 1)
                act.activation(sm[:, 4], sm[:, 4], ACT.Sin).then_inc(g["act_trig"], 1)
                act.activation(sm[:, 5], sm[:, 5], ACT.Sin).then_inc(g["act_trig"], 1)

            highs = [0]

            def high_until(last):
                while highs[0] <= min(last, len(place_of) - 1):
                    m = highs[0]
                    n = place_of[m]
                    act.wait_ge(raw_full[n % TRUNK_RING], full_at[n])
                    if m >= TRUNK_SPLIT:
                        act.wait_ge(g["trunk_used"], m - TRUNK_SPLIT + 1)
                    act.activation(raw_hi[:, m % TRUNK_SPLIT], raw[:, n % TRUNK_RING], ACT.Copy).then_inc(g["trunk_hi"], 1)
                    highs[0] += 1

            def used(m):
                high_until(ahead(m))
                act.wait_ge(g["trunk_used"], m + 1)

            def norm(m, gain):
                if m == 0:
                    act.wait_ge(g["x_in"], 16)
                for a in range(TT):
                    if m:
                        act.wait_ge(g["acc_read"] if m % 2 == 0 else S_["dve_wo"],
                                    {1: 4, 2: 4, 3: 8, 4: 4 + 4 * NE}[m] - 2 * (TT - 1 - a))
                    act.activation(hn[:, a], x_sb[:, a], ACT.Square, accum_out=st[:, m, 0, a:a + 1]).then_inc(S_["act_ss"], 1)
                act.wait_ge(S_["dve_rv"], m * PER["dve_rv"] + 1)
                act.activation(st[:, m, 2], st[:, m, 1], ACT.Sqrt).then_inc(S_["act_sd"], 1)
                act.wait_ge(S_["act_sd"], m * PER["act_sd"] + 1)
                act.activation(hn[:, 1], x_sb[:, 1], ACT.Copy, scale=st[:, m, 2, 1:2]).then_inc(S_["act_hn"], 1)
                if gain is None:
                    return
                if m == 0:
                    layer_params(0)
                act.wait_ge(g["act_params"], m // 2 + 1)
                if m < 3:
                    high_until((0, split_at["dense"], split_at[1])[m] + 1)
                for b in range(4):
                    act.wait_ge(S_["pe_tr"], m * PER["pe_tr"] + b + 1)
                    for a in range(2):
                        k = 2 * b + a
                        act.activation(hT_hi[:, k], halves(b)[:, a], ACT.Copy,
                                       scale=cols[:, m // 2, gain + k:gain + k + 1]).then_inc(S_["act_ht"], 1)

            def gate_sigmoids(l, first, last):
                for n in range(first, last):
                    used(split_at[l] + U_G + n)
                    for a in range(2):
                        i = 2 * n + a
                        act.activation(gates[:, i], halves(6 + n % 2)[:, a], ACT.Sigmoid,
                                       bias=cols[:, l, BI + 6 + i:BI + 7 + i]).then_inc(S_["act_gate"], 1)

            def mats(l, half):
                for n in range(4):
                    act.wait_ge(S_["pe_mats"], l * PER["pe_mats"] + 4 * half + n + 1)
                    if half and n < 2:
                        act.wait_ge(S_["pe_bu"], l * PER["pe_bu"] + 2)
                    if half and n >= 2:
                        act.wait_ge(S_["pe_y"], l * PER["pe_y"] + 1)
                    dst = (b_mat if n < 2 else c_mat)[:, n % 2].rearrange("p j n -> p (j n)")
                    act.activation(dst, bank[n][:, :], ACT.Copy).then_inc(S_["act_mats"], 1)

            def exps(l, grp):
                act.wait_ge(S_["dve_max"], l * PER["dve_max"] + grp + 1)
                if grp:
                    act.wait_ge(S_["pe_pt"], l * PER["pe_pt"] + 4)
                for h in range(4):
                    s = bank[h]
                    act.activation(probs[:, h, 0:P], s[:, 0:P], ACT.Exp, bias=att_max[:, 0, h:h + 1], scale=0.125,
                                   accum_out=att_sum[:, 0, h:h + 1]).then_inc(S_["act_exp"], 1)
                    act.activation(probs[:, h, P:384], s[:, P:384], ACT.Exp, bias=att_max[:, 1, h:h + 1], scale=0.125,
                                   accum_out=att_sum[:, 1, h:h + 1]).then_inc(S_["act_exp"], 1)

            def probs_out(l, grp):
                for h in range(4):
                    act.wait_ge(S_["pe_pt"], l * PER["pe_pt"] + 4 * grp + h + 1)
                    if grp:
                        act.wait_ge(S_["pe_att"], l * PER["pe_att"] + 2)
                    act.activation(probsT[:, h], bank[h][:, 0:384], ACT.Copy).then_inc(S_["act_pt"], 1)

            for l in range(DEPTH):
                norm(2 * l, GM)
                if l == 0:
                    state_functions()
                for b in range(4):
                    used(split_at[l] + b)
                    if b == 1:
                        if l == 0:
                            layer_params(1)
                        act.wait_ge(g["side_in"], 16 * (6 + 4 * l))
                        act.activation(small_hi[:], wf[:], ACT.Copy).then_inc(g["small_hi"], 1)
                    for a in range(2):
                        j = 2 * (b % 2) + a
                        src = halves(4 + b)[:, a]
                        if b < 2:
                            act.activation(qT[:, j], src, ACT.Identity,
                                           bias=cols[:, l, QK + j:QK + j + 1]).then_inc(S_["act_qk"], 1)
                        else:
                            if b == 2 and a == 0:
                                act.wait_ge(g["pool_const"], 4)
                            for o in range(2):
                                r = slice(64 * o, 64 * o + 64)
                                act.activation(k_pad[r, 2 * j + o], src[r], ACT.Identity,
                                               bias=cols[r, l, QK + 4 + j:QK + 5 + j]).then_inc(S_["act_qk"], 1)
                high_until(split_at[l] + U_U + 1)
                act.wait_ge(S_["dve_fz"], l * PER["dve_fz"] + 2)
                act.activation(fz[:, 1], fz[:, 1], ACT.Exp, scale=-1.0).then_inc(S_["act_f"], 1)
                act.wait_ge(S_["act_f"], l * PER["act_f"] + 1)
                act.activation(fz[:, 1], fz[:, 1], ACT.Ln, bias=1.0).then_inc(S_["act_f"], 1)
                used(split_at[l] + U_C + 1)
                for a in range(2):
                    act.activation(conv_sig[:, a], halves(5)[:, a], ACT.Sigmoid,
                                   bias=cols[:, l, BI + 4 + a:BI + 5 + a]).then_inc(S_["act_cg"], 1)
                mats(l, 0)
                high_until(split_at[l] + U_G + 2)
                exps(l, 0)
                gate_sigmoids(l, 0, 4)
                probs_out(l, 0)
                gate_sigmoids(l, 4, 6)
                mats(l, 1)
                high_until(split_at[l] + U_G + 8)
                exps(l, 1)
                gate_sigmoids(l, 6, 10)
                probs_out(l, 1)
                gate_sigmoids(l, 10, 12)
                act.wait_ge(S_["dve_z"], l * PER["dve_z"] + 2)
                act.activation(ssm_g[:], ssm_z[:], ACT.Gelu_apprx_tanh).then_inc(S_["act_gelu"], 1)
                act.wait_ge(S_["dve_ln"], l * PER["dve_ln"] + 3)
                act.activation(ln_r[:], ln_r[:], ACT.Sqrt).then_inc(S_["act_ln"], 1)
                act.wait_ge(S_["pe_glu"], l * PER["pe_glu"] + 2)
                act.activation(ssm_sig[:], halves(5)[:, :], ACT.Sigmoid).then_inc(S_["act_glu"], 1)
                act.wait_ge(S_["dve_ln"], l * PER["dve_ln"] + 4)
                for a in range(2):
                    act.activation(conv_sig[:, a], conv_acc[:, a], ACT.Silu, scale=cols[:, l, LG + a:LG + a + 1],
                                   bias=cols[:, l, LB + a:LB + a + 1]).then_inc(S_["act_conv"], 1)
                for i in range(4):
                    act.wait_ge(S_["dve_merge"], l * PER["dve_merge"] + i + 1)
                    act.activation(merged_hi[:, 2 * i:2 * i + 2], merged[:, 2 * i:2 * i + 2],
                                   ACT.Copy).then_inc(S_["act_merged"], 1)
                    high_until(split_at[l] + U_O + i)
                if l:
                    act.wait_ge(S_["pe_att"], DEPTH * PER["pe_att"])
                    act.activation(small_hi[:, :, 0:NE], w_router[:], ACT.Copy).then_inc(g["small_hi"], 1)

                norm(2 * l + 1, GF)
                if l == 0:
                    for n, (kind, q) in enumerate(dense):
                        if kind == "gate":
                            used(split_at["dense"] + n)
                            if q >= 2:
                                act.wait_ge(g["ffn_hidden"], q - 1)
                            act.activation(silu_g[:, q % 2], halves(4 + q % 2)[:, :], ACT.Silu).then_inc(g["ffn_act_silu"], 1)
                        elif kind == "up":
                            high_until(split_at["dense"] + n + TRUNK_SPLIT - 1)
                            act.wait_ge(g["ffn_hidden"], q + 1)
                            if q >= 2:
                                act.wait_ge(g["trunk_used"], split_at["dense"] + dense.index(("down", q - 2)) + 1)
                            act.activation(hidden_hi[:, q % 2], hidden[:, q % 2], ACT.Copy).then_inc(g["ffn_act_hi"], 1)
                    high_until(split_at[1] - 1)
                else:
                    def picked_high(v):
                        for n in range(2):
                            act.wait_ge(g["dve_picked"], v * 2 + (n + 1))
                            act.activation(picked_hi[:, 4 * n:4 * n + 4], picked[:, 4 * n:4 * n + 4],
                                           ACT.Copy).then_inc(g["act_picked"], 1)

                    def high(v, n):
                        r, q = n % UNIT_RING, n % SPLIT_RING
                        act.wait_ge(unit_full[r], v * (16 * NU // UNIT_RING) + 16 * (n // UNIT_RING + 1))
                        act.wait_ge(g["unit_used"], v * NU + (n + 1))
                        act.activation(unit_hi[:, q], unit_raw[:, r], ACT.Copy).then_inc(g["split_hi"], 1)

                    def expert(v, last=False):

                        def used(kind, c):
                            act.wait_ge(g["unit_used"], v * NU + (unit_at[kind, c, 1] + 1 + SPLIT_RING))

                        def turn_high(c):
                            act.wait_ge(g["pe_e_turned"], v * E_CH + (c + 1))
                            if c >= 2:
                                used("down", c - 2)
                            act.activation(turned_hi[:, c % 2], bank[4][:, :].rearrange("p (b n) -> p b n", n=P),
                                           ACT.Copy).then_inc(g["act_turned"], 1)

                        for n, (kind, c, h) in enumerate(units):
                            if kind == "gate" and h:
                                used("gate", c)
                                act.wait_ge(g["ffn_hidden"], v * E_CH + (N_PAIR + max(c - 1, 0)))
                                act.activation(e_silu[:, c % 2], bank[c % 2][:, :],
                                               ACT.Silu).then_inc(g["ffn_act_silu"], 1)
                                if c:
                                    turn_high(c - 1)
                            if n == unit_at["down", E_CH - 2, 1]:
                                turn_high(E_CH - 1)
                            if n + SPLIT_RING < NU or (n < NU - 1 and not last):
                                high(v, n + SPLIT_RING)
                        if not last:
                            picked_high(v + 1)
                        used("down", E_CH - 1)
                        for h in range(2):
                            act.activation(e_out[:, h * 512:(h + 1) * 512], bank[5 + h][:, :],
                                           ACT.Copy).then_inc(g["act_e_out"], 1)
                        if not last:
                            high(v, NU - 1 + SPLIT_RING)

                    for n in range(SPLIT_RING - 1):
                        high(0, n)
                    act.wait_ge(g["router_read"], 3)
                    act.activation(rt[:, :, 1:2], rt[:, :, 0:1], ACT.Exp).then_inc(g["act_top"], 1)
                    high(0, SPLIT_RING - 1)
                    picked_high(0)
                    with act.Fori(0, NE - 1) as e:
                        expert(e)
                    expert(NE - 1, last=True)
                    with act.If(act.value_load(crowded[0:1, 0:1], min_val=0, max_val=1) > 0):
                        for n in range(SPLIT_RING):
                            high(NE, n)
                        picked_high(NE)
                        with act.Fori(0, NE - 1) as e:
                            expert(e + NE)
                        expert(2 * NE - 1, last=True)
                        act.wait_ge(g["acc_read"], 4 + 8 * NE)
            norm(4, None)

        @block.vector
        def _(dve):
            counts = {}

            def step(ins, sem=g["dve_order"]):
                counts[id(sem)] = counts.get(id(sem), 0) + 1
                ins.then_inc(sem, 1)
                dve.wait_ge(sem, counts[id(sem)])

            step(dve.memset(wf[:], 0.0), g["dve_const"])
            step(dve.memset(bf[:], 0.0), g["dve_const"])
            step(dve.memset(mean_mat[:], 1.0 / CW), g["dve_const"])
            step(dve.memset(ones_col[:], 1.0))
            step(dve.memset(f_left[:], 0.0))
            dve.memset(f_right[:], 0.0).then_inc(g["split_lo"], UNIT_RING)
            dve.wait_ge(g["split_lo"], UNIT_RING)

            lows = [0]

            def low_until(last):
                while lows[0] <= min(last, len(place_of) - 1):
                    m = lows[0]
                    dve.wait_ge(g["trunk_hi"], m + 1)
                    r = place_of[m] % TRUNK_RING
                    dve.tensor_tensor(raw_lo[:, r], raw[:, r],
                                      raw_hi[:, m % TRUNK_SPLIT].bitcast(F32), ALU.subtract).then_inc(g["trunk_lo"], 1)
                    lows[0] += 1

            def used(m):
                low_until(ahead(m))
                dve.wait_ge(g["trunk_used"], m + 1)

            def norm(m, gain):
                dve.wait_ge(S_["act_ss"], m * PER["act_ss"] + 2)
                step(dve.tensor_scalar(st[:, m, 1], st[:, m, 0], 1.0 / D, EPS, ALU.mult, ALU.add))
                step(dve.reciprocal(st[:, m, 1], st[:, m, 1]), S_["dve_rv"])
                dve.wait_ge(S_["act_sd"], m * PER["act_sd"] + 1)
                step(dve.tensor_scalar(hn[:, 0], x_sb[:, 0], st[:, m, 2, 0:1], None, ALU.mult), S_["dve_hn"])
                if gain is None:
                    return
                if m == 0:
                    dve.wait_ge(g["states_in"], 48)
                    step(dve.tensor_copy(ldt_row[:].rearrange("r (a s) -> r a s", a=2),
                                         ldt[:].rearrange("r (a o) -> r a o", o=1).to_broadcast([16, 2, S])), g["dve_const"])
                dve.wait_ge(g["act_params"], m // 2 + 1)
                if m < 3:
                    low_until((0, split_at["dense"], split_at[1])[m])
                for k in range(KT):
                    dve.wait_ge(S_["act_ht"], m * PER["act_ht"] + 2 * (k // 2) + 2)
                    step(dve.scalar_tensor_tensor(hT_lo[:, k], halves(k // 2)[:, k % 2],
                                                  cols[:, m // 2, gain + k:gain + k + 1], hT_hi[:, k].bitcast(F32),
                                                  ALU.mult, ALU.subtract), S_["dve_ht"])

            def discretise():
                dve.wait_ge(g["pe_params"], 2)
                step(dve.tensor_copy(scol[:], bank[5][:, 0:48]))
                a_re, a_im = scol[:, 0:SC], scol[:, SC:2 * SC]
                step(dve.tensor_copy(sm[:, 0], scol[:, 2 * SC:3 * SC]), g["dve_theta"])
                dve.wait_ge(g["act_trig"], 1)
                step(dve.tensor_tensor(sm[:, 3], a_re, sm[:, 0], ALU.mult))
                step(dve.tensor_tensor(sm[:, 1], a_im, sm[:, 0], ALU.mult))
                step(dve.tensor_scalar(sm[:, 2], sm[:, 1], 1.0 / TWO_PI, ROUND_MAGIC, ALU.mult, ALU.add))
                step(dve.tensor_scalar(sm[:, 2], sm[:, 2], ROUND_MAGIC, None, ALU.subtract))
                for part in (TWO_PI_A, TWO_PI_B, TWO_PI_C):
                    step(dve.scalar_tensor_tensor(sm[:, 1], sm[:, 2], -part, sm[:, 1], ALU.mult, ALU.add))
                step(dve.tensor_scalar(sm[:, 4], sm[:, 1], 3.1415925, -3.1415925, ALU.min, ALU.max))
                step(dve.scalar_tensor_tensor(sm[:, 5], sm[:, 4], -1.0, sm[:, 4], ALU.mult, ALU.max))
                step(dve.tensor_scalar(sm[:, 5], sm[:, 5], -1.0, TWO_PI / 4, ALU.mult, ALU.add), g["dve_theta"])
                low_until(1)
                dve.wait_ge(g["act_trig"], 4)
                step(dve.tensor_copy(rot_pow[:, 0, 0], sm[:, 5]))
                step(dve.tensor_copy(rot_pow[:, 1, 0], sm[:, 4]))
                step(dve.tensor_tensor(sm[:, 5], sm[:, 5], sm[:, 3], ALU.mult))
                step(dve.tensor_scalar(sm[:, 5], sm[:, 5], 1.0, None, ALU.subtract))
                step(dve.tensor_tensor(sm[:, 6], sm[:, 4], sm[:, 3], ALU.mult))
                step(dve.tensor_tensor(sm[:, 7], a_re, a_re, ALU.mult))
                step(dve.tensor_tensor(sm[:, 8], a_im, a_im, ALU.mult))
                step(dve.tensor_tensor(sm[:, 7], sm[:, 7], sm[:, 8], ALU.add))
                step(dve.reciprocal(sm[:, 7], sm[:, 7]))
                step(dve.tensor_tensor(sm[:, 8], sm[:, 5], a_re, ALU.mult))
                step(dve.tensor_tensor(sm[:, 9], sm[:, 6], a_im, ALU.mult))
                step(dve.tensor_tensor(sm[:, 8], sm[:, 8], sm[:, 9], ALU.add))
                step(dve.tensor_tensor(sm[:, 10], sm[:, 8], sm[:, 7], ALU.mult))
                step(dve.tensor_tensor(sm[:, 8], sm[:, 6], a_re, ALU.mult))
                step(dve.tensor_tensor(sm[:, 9], sm[:, 5], a_im, ALU.mult))
                step(dve.tensor_tensor(sm[:, 8], sm[:, 8], sm[:, 9], ALU.subtract))
                step(dve.tensor_tensor(sm[:, 11], sm[:, 8], sm[:, 7], ALU.mult))
                low_until(2)
                for n in range(7):
                    if n == 4:
                        low_until(3)
                    zr, zi = rot_pow[:, 0, n], rot_pow[:, 1, n]
                    step(dve.tensor_tensor(sm[:, 12], zr, zr, ALU.mult))
                    step(dve.tensor_tensor(sm[:, 13], zi, zi, ALU.mult))
                    step(dve.tensor_tensor(rot_pow[:, 0, n + 1], sm[:, 12], sm[:, 13], ALU.subtract))
                    step(dve.scalar_tensor_tensor(rot_pow[:, 1, n + 1], zr, 2.0, zi, ALU.mult, ALU.mult),
                         g["dve_states"] if n == 6 else g["dve_order"])

            def rotate_scan(l, pair):
                half, q = pair // 2, pair % 2
                next_gate = split_at[l] + U_G + (3 if pair == 1 else 9)
                if q:
                    low_until(next_gate)
                dve.wait_ge(S_["pool_phase"], l * PER["pool_phase"] + half + 1)
                dve.wait_ge(S_["pe_bu"], l * PER["pe_bu"] + pair + 1)
                if pair == 2:
                    dve.wait_ge(S_["pe_y"], l * PER["pe_y"] + 1)
                re, im = halves(4)[:, :], halves(5)[:, :]
                c_, s_ = (phase[:, c, 2 * q:2 * q + 2] for c in range(2))
                y_re, y_im = (state[:, c, 2 * q:2 * q + 2] for c in range(2))
                step(dve.tensor_tensor(rot_tmp[:, 0], re, c_, ALU.mult))
                step(dve.tensor_tensor(rot_tmp[:, 1], im, s_, ALU.mult))
                step(dve.tensor_tensor(y_re, rot_tmp[:, 0], rot_tmp[:, 1], ALU.add))
                step(dve.tensor_tensor(rot_tmp[:, 0], im, c_, ALU.mult))
                step(dve.tensor_tensor(rot_tmp[:, 1], re, s_, ALU.mult))
                step(dve.tensor_tensor(y_im, rot_tmp[:, 0], rot_tmp[:, 1], ALU.subtract), S_["dve_bu"])
                if q:
                    low_until(next_gate + 1)
                for c in range(2):
                    for a in range(2):
                        j = l * NJ + 2 * pair + a
                        y = state[:, c, 2 * q + a]
                        step(dve.tensor_tensor_scan(y, sm[:, 3, j:j + 1].to_broadcast([P, T]), y, 0.0,
                                                    ALU.mult, ALU.add),
                             S_["dve_scan"] if c and a else g["dve_order"])

            def softmax_max(l, grp):
                dve.wait_ge(S_["pe_s"], l * PER["pe_s"] + 4 * grp + 4)
                if grp:
                    dve.wait_ge(S_["act_exp"], l * PER["act_exp"] + 8)
                for h in range(4):
                    step(dve.reduce_max(att_max[:, 0, h:h + 1], bank[h][:, 0:P], AX_X))
                    step(dve.reduce_max(att_max[:, 1, h:h + 1], bank[h][:, P:384], AX_X))
                step(dve.tensor_scalar(att_max[:], att_max[:], -0.125, None, ALU.mult), S_["dve_max"])

            def forget_right(l, grp):
                for h in range(4):
                    hd = 4 * grp + h
                    step(dve.tensor_scalar(f_right[0:64, h], f_sum[:], f_scale[:, hd:hd + 1], f_shift[:, hd:hd + 1],
                                           ALU.mult, ALU.add), S_["dve_f"])

            def softmax_norm(l, grp):
                dve.wait_ge(S_["act_exp"], l * PER["act_exp"] + 8 * grp + 8)
                step(dve.reciprocal(att_rs[:], att_sum[:]))
                for o, (a, b) in enumerate(((0, P), (P, 384))):
                    step(dve.tensor_tensor(probs[:, :, a:b], probs[:, :, a:b],
                                           att_rs[:, o].rearrange("p (h o) -> p h o", o=1).to_broadcast([P, 4, b - a]),
                                           ALU.mult), S_["dve_p"])

            def attention_out(l, grp):
                for q in range(2):
                    dve.wait_ge(S_["pe_att"], l * PER["pe_att"] + 2 * grp + q + 1)
                    for o in range(2):
                        r = slice(64 * o, 64 * o + 64)
                        j = 2 * grp + q
                        step(dve.tensor_scalar(attT[r, j], halves(q)[r, o], cols[r, l, QK + 8 + j:QK + 9 + j], None,
                                               ALU.add), S_["dve_att"])

            def conv_taps(l, a):
                w = lambda k: cols[:, l, CWC + 2 * k + a:CWC + 2 * k + a + 1]
                step(dve.tensor_scalar(conv_acc[:, a], conv_in[:, a, 0:T], w(0), cols[:, l, CB + a:CB + a + 1],
                                       ALU.mult, ALU.add))
                first_low = split_at[l] + U_G + (3, 9)[a]
                for k in range(1, CK):
                    if k % 7 == 0:
                        low_until(min(first_low + k // 7, split_at[l] + U_O - 1))
                    step(dve.scalar_tensor_tensor(conv_acc[:, a], conv_in[:, a, k:k + T], w(k), conv_acc[:, a],
                                                  ALU.mult, ALU.add), S_["dve_conv"] if k == CK - 1 else g["dve_order"])

            def ssm_out(l, half):
                dve.wait_ge(S_["pe_y"], l * PER["pe_y"] + half + 1)
                step(dve.scalar_tensor_tensor(ssm_z[:, half], uT[:, half], cols[:, l, SD + half:SD + half + 1],
                                              halves(4)[:, 0], ALU.mult, ALU.add), S_["dve_z"])

            for l in range(DEPTH):
                norm(2 * l, GM)
                if l == 0:
                    discretise()
                low_until(split_at[l] + 3)
                dve.wait_ge(g["small_hi"], l + 1)
                step(dve.tensor_tensor(small_lo[:], wf[:], small_hi[:].bitcast(F32), ALU.subtract), g["small_lo"])
                used(split_at[l] + U_V + 1)
                for a in range(TT):
                    step(dve.tensor_copy(v_sb[:, a], bank[a][:, :]), S_["dve_v"])
                dve.wait_ge(S_["pe_f"], l + 1)
                dve.wait_ge(g["side_in"], 16 * (6 + 4 * l))
                step(dve.tensor_scalar(fz[:, 0], bank[2][0:64, 0:T], bf[:, l:l + 1], None, ALU.add), S_["dve_fz"])
                step(dve.scalar_tensor_tensor(fz[:, 1], fz[:, 0], -1.0, fz[:, 0], ALU.mult, ALU.max), S_["dve_fz"])
                used(split_at[l] + U_U)
                for a in range(2):
                    step(dve.tensor_scalar(uT[:, a], halves(3)[:, a], cols[:, l, BI + a:BI + a + 1], None, ALU.add),
                         S_["dve_u"])
                dve.wait_ge(S_["act_f"], l * PER["act_f"] + 2)
                step(dve.scalar_tensor_tensor(fz[:, 0], fz[:, 0], 0.0, fz[:, 1], ALU.min, ALU.subtract))
                dve.wait_ge(g["pool_const"], 3)
                step(dve.tensor_tensor_scan(f_sum[:], ones_col[:].to_broadcast([64, T]), fz[:, 0], 0.0,
                                            ALU.mult, ALU.add))
                step(dve.tensor_scalar(f_left[0:64], f_sum[:], f_scale[:, H:H + 1], f_shift[:, H:H + 1],
                                       ALU.mult, ALU.add), S_["dve_f"])
                forget_right(l, 0)
                low_until(split_at[l] + U_G + 1)
                dve.wait_ge(S_["act_cg"], l * PER["act_cg"] + 2)
                dve.wait_ge(g["pool_const"], 4)
                for a in range(2):
                    step(dve.scalar_tensor_tensor(conv_in[:, a, PAD:PAD + T], halves(4)[:, a],
                                                  cols[:, l, BI + 2 + a:BI + 3 + a], conv_sig[:, a],
                                                  ALU.add, ALU.mult), S_["dve_cv"])
                rotate_scan(l, 0)
                softmax_max(l, 0)
                low_until(split_at[l] + U_G + 2)
                softmax_norm(l, 0)
                forget_right(l, 1)
                rotate_scan(l, 1)
                conv_taps(l, 0)
                attention_out(l, 0)
                ssm_out(l, 0)
                rotate_scan(l, 2)
                low_until(split_at[l] + U_G + 7)
                softmax_max(l, 1)
                low_until(split_at[l] + U_G + 8)
                softmax_norm(l, 1)
                rotate_scan(l, 3)
                conv_taps(l, 1)
                attention_out(l, 1)
                for a in range(2):
                    if a == 0:
                        dve.wait_ge(S_["pe_ln"], l * PER["pe_ln"] + 1)
                    step(dve.tensor_tensor(conv_acc[:, a], conv_acc[:, a], halves(6)[:, 0], ALU.subtract))
                step(dve.tensor_tensor(conv_sig[:], conv_acc[:], conv_acc[:], ALU.mult), S_["dve_ln"])
                ssm_out(l, 1)
                dve.wait_ge(S_["pe_ln"], l * PER["pe_ln"] + 2)
                step(dve.tensor_scalar(ln_r[:], halves(7)[:, 0], EPS, None, ALU.add), S_["dve_ln"])
                step(dve.reciprocal(ln_r[:], ln_r[:]), S_["dve_ln"])
                dve.wait_ge(S_["act_ln"], l * PER["act_ln"] + 1)
                for a in range(2):
                    last = dve.tensor_tensor(conv_acc[:, a], conv_acc[:, a], ln_r[:], ALU.mult)
                    step(last, S_["dve_ln"] if a else g["dve_order"])
                dve.wait_ge(S_["act_glu"], l * PER["act_glu"] + 1)
                step(dve.tensor_tensor(ssm_z[:], halves(4)[:, :], ssm_sig[:], ALU.mult), S_["dve_glu"])
                for i in range(4):
                    b0 = 3 * (i % 2)
                    gt = [gates[:, 8 * b + 2 * i:8 * b + 2 * i + 2] for b in range(3)]
                    m_ = merged[:, 2 * i:2 * i + 2]
                    dve.wait_ge(S_["act_gate"], l * PER["act_gate"] + 24)
                    dve.wait_ge(S_["pe_out"], l * PER["pe_out"] + 3 * i + 1)
                    step(dve.tensor_tensor(m_, halves(b0)[:, :], gt[0], ALU.mult))
                    dve.wait_ge(S_["pe_out"], l * PER["pe_out"] + 3 * i + 2)
                    step(dve.tensor_tensor(rot_tmp[:, 0], halves(b0 + 1)[:, :], gt[1], ALU.mult))
                    dve.wait_ge(S_["pe_out"], l * PER["pe_out"] + 3 * i + 3)
                    step(dve.tensor_tensor(rot_tmp[:, 1], halves(b0 + 2)[:, :], gt[2], ALU.mult))
                    step(dve.tensor_tensor(m_, m_, rot_tmp[:, 0], ALU.add))
                    step(dve.tensor_tensor(m_, m_, rot_tmp[:, 1], ALU.add), S_["dve_merge"])
                    dve.wait_ge(S_["act_merged"], l * PER["act_merged"] + i + 1)
                    step(dve.tensor_tensor(merged_lo[:, 2 * i:2 * i + 2], m_, merged_hi[:, 2 * i:2 * i + 2].bitcast(F32),
                                           ALU.subtract), S_["dve_merged"])
                    if i:
                        low_until(split_at[l] + U_O + i - 1)
                low_until(split_at[l] + U_O + 3)
                if l:
                    dve.wait_ge(g["small_hi"], DEPTH + 1)
                    step(dve.tensor_tensor(small_lo[:, :, 0:NE], w_router[:], small_hi[:, :, 0:NE].bitcast(F32),
                                           ALU.subtract), g["small_lo"])
                dve.wait_ge(g["trunk_used"], split_at[l] + U_MIX)
                for n, b in enumerate((6, 7, 0, 1)):
                    xs = x_sb[:, n // 2, (n % 2) * 512:(n % 2 + 1) * 512]
                    step(dve.tensor_tensor(xs, xs, bank[b][:, :], ALU.add), S_["dve_wo"])

                norm(2 * l + 1, GF)
                if l == 0:
                    for n, (kind, q) in enumerate(dense):
                        if kind == "up":
                            used(split_at["dense"] + n)
                            dve.wait_ge(g["ffn_act_silu"], q + 1)
                            step(dve.tensor_tensor(hidden[:, q % 2], silu_g[:, q % 2], halves(6 + q % 2)[:, :], ALU.mult),
                                 g["ffn_hidden"])
                            dve.wait_ge(g["ffn_act_hi"], q + 1)
                            dve.tensor_tensor(hidden_lo[:, q % 2], hidden[:, q % 2], hidden_hi[:, q % 2].bitcast(F32),
                                              ALU.subtract).then_inc(g["ffn_lo"], 1)
                    dve.wait_ge(g["trunk_used"], split_at[1])
                    for n in range(4):
                        xs = x_sb[:, n // 2, (n % 2) * 512:(n % 2 + 1) * 512]
                        step(dve.tensor_tensor(xs, xs, bank[n][:, :], ALU.add), g["acc_read"])
                else:
                    def low(v, n):
                        dve.wait_ge(g["split_hi"], v * NU + (n + 1))
                        r, q = n % UNIT_RING, n % SPLIT_RING
                        dve.tensor_tensor(unit_lo[:, q], unit_raw[:, r], unit_hi[:, q].bitcast(F32),
                                          ALU.subtract).then_inc(g["split_lo"], 1)

                    dve.wait_ge(g["pe_router"], 1)
                    step(dve.tensor_scalar(logits_T, bank[4][0:NE, 0:T], b_router[:], None, ALU.add), g["router_read"])
                    dve.wait_ge(g["pe_router"], 2)
                    step(dve.tensor_copy(logits[:].rearrange("p a n -> p (a n)"), bank[5][:, 0:TT * NE]), g["router_read"])
                    for a in range(TT):
                        step(dve.max(top[:, a], logits[:, a]))
                        step(dve.max_index(top_at[:, a], top[:, a], logits[:, a]))
                    step(dve.tensor_copy(top_f[:], top_at[:]))
                    r_ = [rt[:, :, k:k + 1] for k in range(4)]
                    step(dve.tensor_tensor(r_[0], top[:, :, 1:2], top[:, :, 0:1], ALU.subtract), g["router_read"])
                    dve.wait_ge(g["act_top"], 1)
                    step(dve.tensor_scalar(r_[2], r_[1], 1.0, None, ALU.add))
                    step(dve.reciprocal(r_[2], r_[2]))
                    step(dve.tensor_tensor(r_[3], r_[1], r_[2], ALU.mult))
                    step(dve.memset(w_exp[:], 0.0))
                    step(dve.memset(place[:], -1.0))
                    for a in range(TT):
                        step(dve.tensor_scalar(w_exp[:, a, 0:NE], e_iota[:], top_f[:, a, 0:1], rt[:, a, 2:3],
                                               ALU.is_equal, ALU.mult))
                        step(dve.tensor_scalar(w_tmp[:, a], e_iota[:], top_f[:, a, 1:2], rt[:, a, 3:4],
                                               ALU.is_equal, ALU.mult))
                    step(dve.tensor_tensor(w_exp[:, :, 0:NE], w_exp[:, :, 0:NE], w_tmp[:], ALU.add))
                    for a in range(TT):
                        step(dve.tensor_scalar(chosen[:, a], e_iota[:], top_f[:, a, 0:1], None, ALU.is_equal))
                        step(dve.scalar_tensor_tensor(chosen[:, a], e_iota[:], top_f[:, a, 1:2], chosen[:, a],
                                                      ALU.is_equal, ALU.add),
                             g["dve_route"] if a else g["dve_order"])
                    low(0, 0)
                    dve.wait_ge(g["pe_route"], 3)
                    for a in range(TT):
                        step(dve.scalar_tensor_tensor(place[:, a, 0:NE], bank[6 + a][:, 0:NE], 1.0, chosen[:, a],
                                                      ALU.add, ALU.mult))
                    step(dve.tensor_scalar(place[:, :, 0:NE], place[:, :, 0:NE], 1.0, None, ALU.subtract))
                    step(dve.reduce_max(most[:], bank[5][:, 0:NE], AX_X))
                    step(dve.tensor_scalar(crowded[:], most[:], P + 0.5, None, ALU.is_gt), g["dve_route"])
                    dve.wait_ge(g["pool_route"], 2)

                    def build_pick(e):
                        for a in range(TT):
                            at_ = place[:, a, e:e + 1] if isinstance(e, int) else place[:, a, bass.ds(e, 1)]
                            wt = w_exp[:, a, e:e + 1] if isinstance(e, int) else w_exp[:, a, bass.ds(e, 1)]
                            dve.tensor_scalar(pick[:, a], slot_iota, at_, None, ALU.is_equal)
                            last = dve.tensor_scalar(spread[:, a], slot_iota, at_, wt, ALU.is_equal, ALU.mult)
                        last.then_inc(g["dve_pick"], 1)

                    def read_picked(v):
                        for n, b in enumerate((7, 4)):
                            dve.wait_ge(g["pe_picked"], v * 2 + (n + 1))
                            gain = cols[:, 1, GF + 4 * n:GF + 4 * n + 4].rearrange("p (k o) -> p k o", o=1)
                            dve.tensor_tensor(picked[:, 4 * n:4 * n + 4],
                                              bank[b][:, :].rearrange("p (k n) -> p k n", n=P),
                                              gain.to_broadcast([P, 4, P]), ALU.mult).then_inc(g["dve_picked"], 1)

                    def picked_low(v):
                        for n in range(2):
                            dve.wait_ge(g["act_picked"], v * 2 + (n + 1))
                            k = slice(4 * n, 4 * n + 4)
                            dve.tensor_tensor(picked_lo[:, k], picked[:, k], picked_hi[:, k].bitcast(F32),
                                              ALU.subtract).then_inc(g["dve_picked_lo"], 1)

                    def expert(e, v, last=False):
                        def turn_low(c):
                            dve.wait_ge(g["act_turned"], v * E_CH + (c + 1))
                            dve.tensor_tensor(turned_lo[:, c % 2], bank[4][:, :].rearrange("p (b n) -> p b n", n=P),
                                              turned_hi[:, c % 2].bitcast(F32),
                                              ALU.subtract).then_inc(g["dve_turned"], 1)

                        for n, (kind, c, h) in enumerate(units):
                            if kind == "gate" and h and c:
                                turn_low(c - 1)
                            if kind == "up" and h:
                                dve.wait_ge(g["ffn_act_silu"], v * E_CH + (N_PAIR + c + 1))
                                dve.wait_ge(g["unit_used"], v * NU + (n + 1 + SPLIT_RING))
                                dve.tensor_tensor(e_hidden[:, c % 2], e_silu[:, c % 2], bank[2 + c % 2][:, :],
                                                  ALU.mult).then_inc(g["ffn_hidden"], 1)
                            if n == unit_at["down", E_CH - 2, 1]:
                                turn_low(E_CH - 1)
                            if n + SPLIT_RING < NU or (n < NU - 1 and not last):
                                low(v, n + SPLIT_RING)
                            if (kind, c, h) == ("down", 3, 1):
                                dve.wait_ge(g["pe_spread"], v + 1)
                                dve.tensor_copy(spreadT, bank[7][:, 0:T]).then_inc(g["dve_spread"], 1)
                                if not last:
                                    build_pick(e + 1)
                        if not last:
                            read_picked(v + 1)
                            picked_low(v + 1)
                        dve.wait_ge(g["acc_read"], v * 4 + 4)
                        for n in range(4):
                            if n == 1 and not last:
                                low(v, NU - 1 + SPLIT_RING)
                            dve.wait_ge(g["pe_combined"], v * 4 + (n + 1))
                            xs = x_sb[:, n // 2, (n % 2) * 512:(n % 2 + 1) * 512]
                            dve.tensor_tensor(xs, xs, bank[n][:, :], ALU.add).then_inc(g["acc_read"], 1)

                    build_pick(0)
                    low(0, 1)
                    read_picked(0)
                    picked_low(0)
                    low(0, 2)
                    with dve.Fori(0, NE - 1) as e:
                        expert(e, e)
                    expert(NE - 1, NE - 1, last=True)
                    with dve.If(dve.value_load(crowded[0:1, 0:1], min_val=0, max_val=1) > 0):
                        dve.tensor_scalar(place[:], place[:], float(P), None, ALU.subtract).then_inc(g["dve_second"], 1)
                        dve.wait_ge(g["dve_second"], 1)
                        build_pick(0)
                        for n in range(SPLIT_RING):
                            low(NE, n)
                        read_picked(NE)
                        picked_low(NE)
                        with dve.Fori(0, NE - 1) as e:
                            expert(e, e + NE)
                        expert(NE - 1, 2 * NE - 1, last=True)
                        dve.wait_ge(g["acc_read"], 4 + 8 * NE)
            dve.wait_ge(g["acc_read"], 4 + 4 * NE)
            norm(4, None)
            dve.wait_ge(S_["act_hn"], 5)
            dve.wait_ge(g["gain_in"], 16)
            for a in range(TT):
                step(dve.tensor_tensor(hn[:, a], hn[:, a], g_final, ALU.mult), g["final_in"] if a else g["dve_order"])

        @block.tensor
        def _(pe):
            pe.wait_ge(g["pool_const"], 1)

            def layer_params(l):
                pe.wait_ge(rows_in[l], 9 * 16)
                pe.transpose(bank[7 - l][:, 0:NROW], rows[0:NROW, l], ident[0:NROW, 0:NROW]).then_inc(g["pe_params"], 1)

            layer_params(0)

            def unit_at_once(n, sizes):
                pe.wait_ge(raw_full[n % TRUNK_RING], full_at[n])
                out_, at = [], 0
                for k, w in sizes:
                    out_.append(raw[:, n % TRUNK_RING, at:at + k * w].rearrange("p (k n) -> p k n", n=w))
                    at += k * w
                return out_

            def split_unit(m, k):
                pe.wait_ge(g["trunk_lo"], m + 1)
                return [u.rearrange("p (k n) -> p k n", k=k)
                        for u in (raw_hi[:, m % TRUNK_SPLIT], raw_lo[:, place_of[m] % TRUNK_RING])]

            def product(o, lhs, rhs, n, first=True, last=True):
                for k in range(n):
                    ins = pe.matmul(o, lhs(k), rhs(k), start=(first and k == 0), stop=(last and k == n - 1))
                return ins

            def split_product(o, lhs_hi, lhs_lo, rhs_hi, rhs_lo, first, last):
                pe.matmul(o, lhs_hi, rhs_hi, start=first, stop=False)
                pe.matmul(o, lhs_hi, rhs_lo, start=False, stop=False)
                return pe.matmul(o, lhs_lo, rhs_hi, start=False, stop=last)

            def feature_tiles(b, m, h_of=None):
                w_hi, w_lo = split_unit(m, KT)
                for a in range(2):
                    c = slice(a * P, (a + 1) * P)
                    for k in range(KT):
                        if a == 0 and h_of is not None:
                            pe.wait_ge(S_["dve_ht"], h_of * PER["dve_ht"] + k + 1)
                        ins = split_product(halves(b)[:, a], w_hi[:, k, c], w_lo[:, k, c], hT_hi[:, k], hT_lo[:, k],
                                            k == 0, k == KT - 1)
                ins.then_inc(g["trunk_used"], 1)

            def norm(m):
                pe.wait_ge(S_["dve_hn"], m * PER["dve_hn"] + 1)
                pe.wait_ge(S_["act_hn"], m * PER["act_hn"] + 1)
                for b in range(4):
                    for a in range(2):
                        for tt in range(TT):
                            k = 2 * b + a
                            ins = pe.transpose(halves(b)[:, a, tt * P:(tt + 1) * P], hn[:, tt, k * P:(k + 1) * P], ident[:])
                    ins.then_inc(S_["pe_tr"], 1)

            def gate_jobs(l, first, last):
                for n in range(first, last):
                    if n < 2:
                        pe.wait_ge(S_["act_qk"], l * PER["act_qk"] + 12)
                    else:
                        pe.wait_ge(S_["act_gate"], l * PER["act_gate"] + 2 * n - 2)
                    feature_tiles(6 + n % 2, split_at[l] + U_G + n)

            def mats(l, half):
                if half == 0:
                    pe.wait_ge(S_["dve_v"], l * PER["dve_v"] + 2)
                    pe.wait_ge(S_["dve_u"], l * PER["dve_u"] + 2)
                else:
                    pe.wait_ge(S_["dve_att"], l * PER["dve_att"] + 4)
                    pe.wait_ge(S_["act_pt"], l * PER["act_pt"] + 4)
                for n in range(4):
                    pe.wait_ge(S_["pool_mats"], l * PER["pool_mats"] + 4 * half + n + 1)
                    for j in range(HJ):
                        ins = pe.transpose(bank[n][:, j * P:(j + 1) * P], mat_src[:, n, j * P:(j + 1) * P], ident[:])
                    ins.then_inc(S_["pe_mats"], 1)

            def states_in(l, pair):
                half, q = pair // 2, pair % 2
                pe.wait_ge(S_["act_mats"], l * PER["act_mats"] + 4 * half + 2)
                if pair == 0:
                    pe.wait_ge(S_["dve_cv"], l * PER["dve_cv"] + 2)
                    pe.wait_ge(S_["act_cg"], l * PER["act_cg"] + 2)
                else:
                    pe.wait_ge(S_["dve_bu"], l * PER["dve_bu"] + pair)
                if pair == 2:
                    pe.wait_ge(S_["dve_z"], l * PER["dve_z"] + 1)
                for c in range(2):
                    for a in range(2):
                        ins = pe.matmul(halves(4 + c)[:, a], b_mat[:, c, 2 * q + a], uT[:, half], start=True, stop=True)
                ins.then_inc(S_["pe_bu"], 1)

            def states_out(l, half):
                pe.wait_ge(S_["pool_back"], l * PER["pool_back"] + 2 * half + 2)
                pe.wait_ge(S_["dve_bu"], l * PER["dve_bu"] + 2 * half + 2)
                pe.wait_ge(S_["act_mats"], l * PER["act_mats"] + 4 * half + 4)
                for c in range(2):
                    ins = product(halves(4)[:, 0], lambda j: c_mat[:, c, j], lambda j: state[:, c, j], HJ,
                                  first=(c == 0), last=(c == 1))
                ins.then_inc(S_["pe_y"], 1)

            def scores(l, grp):
                pe.wait_ge(S_["act_qk"], l * PER["act_qk"] + 12)
                pe.wait_ge(S_["dve_f"], l * PER["dve_f"] + 5 + 4 * grp)
                pe.wait_ge(S_["act_mats"], l * PER["act_mats"] + 4 * grp + 4)
                for h in range(4):
                    hd = 4 * grp + h
                    for q, at_, n in ((0, 0, P), (1, P, T)):
                        o = bank[h][:, at_:at_ + n]
                        pe.matmul(o, qT[:, hd // 2, q * P:(q + 1) * P], k_pad[:, hd, 0:n], start=True, stop=False)
                        pe.matmul(o, f_left[:, q * P:(q + 1) * P], f_right[:, h, 0:n], start=False, stop=False)
                        ins = pe.matmul(bank[h][:, at_ + n - P:at_ + n], ident[:], causal[:], start=False, stop=True)
                    ins.then_inc(S_["pe_s"], 1)

            def probs_transposed(l, grp):
                pe.wait_ge(S_["dve_p"], l * PER["dve_p"] + 2 * grp + 2)
                for h in range(4):
                    for n in range(3):
                        ins = pe.transpose(bank[h][:, n * P:(n + 1) * P], probs[:, h, n * P:(n + 1) * P], ident[:])
                    ins.then_inc(S_["pe_pt"], 1)

            def attention(l, grp):
                pe.wait_ge(S_["act_pt"], l * PER["act_pt"] + 4 * grp + 4)
                for q in range(2):
                    j = 2 * grp + q
                    for o in range(2):
                        h = 2 * q + o
                        pe.matmul(halves(q)[:, o], v_sb[:, 0, j * P:(j + 1) * P], probsT[:, h, 0:T], start=True, stop=False)
                        ins = pe.matmul(halves(q)[:, o, P:T], v_sb[:, 1, j * P:(j + 1) * P], probsT[:, h, T:384],
                                        start=False, stop=True)
                    ins.then_inc(S_["pe_att"], 1)

            for l in range(DEPTH):
                m0, n0 = split_at[l], plain_at[l]
                norm(2 * l)
                if l == 0:
                    pe.wait_ge(g["states_in"], 48)
                    pe.transpose(bank[5][:, 0:32], srow[:], ident[0:32, 0:32])
                    pe.wait_ge(g["dve_const"], 4)
                    pe.transpose(bank[5][:, 32:48], ldt_row[:], ident[0:16, 0:16]).then_inc(g["pe_params"], 1)
                for b in range(4):
                    if l == 0 and b == 1:
                        pe.wait_ge(g["dve_theta"], 1)
                        layer_params(1)
                    if l == 0 and b == 2:
                        pe.wait_ge(g["act_params"], 2)
                    feature_tiles(4 + b, m0 + b, None if b else 2 * l)
                for h in range(2):
                    w_hi, w_lo = split_unit(m0 + U_V + h, KT)
                    for a in range(TT):
                        c = slice(a * P, (a + 1) * P)
                        for k in range(KT):
                            ins = split_product(halves(a)[:, h], hT_hi[:, k, c], hT_lo[:, k, c], w_hi[:, k], w_lo[:, k],
                                                k == 0, k == KT - 1)
                    ins.then_inc(g["trunk_used"], 1)
                pe.wait_ge(g["small_lo"], l + 1)
                for k in range(KT):
                    ins = split_product(bank[2][0:64, 0:T], small_hi[:, k], small_lo[:, k], hT_hi[:, k], hT_lo[:, k],
                                        k == 0, k == KT - 1)
                ins.then_inc(S_["pe_f"], 1)
                feature_tiles(3, m0 + U_U)
                pe.wait_ge(S_["act_qk"], l * PER["act_qk"] + 4)
                for b in range(2):
                    feature_tiles(4 + b, m0 + U_C + b)
                mats(l, 0)
                states_in(l, 0)
                scores(l, 0)
                gate_jobs(l, 0, 2)
                states_in(l, 1)
                gate_jobs(l, 2, 4)
                probs_transposed(l, 0)
                gate_jobs(l, 4, 6)
                attention(l, 0)
                states_out(l, 0)
                mats(l, 1)
                states_in(l, 2)
                scores(l, 1)
                gate_jobs(l, 6, 8)
                states_in(l, 3)
                gate_jobs(l, 8, 10)
                probs_transposed(l, 1)
                gate_jobs(l, 10, 12)
                attention(l, 1)
                pe.wait_ge(S_["act_gate"], l * PER["act_gate"] + 24)
                pe.wait_ge(S_["dve_conv"], l * PER["dve_conv"] + 2)
                product(halves(6)[:, 0], lambda k: mean_mat[:], lambda k: conv_acc[:, k], 2).then_inc(S_["pe_ln"], 1)
                states_out(l, 1)
                pe.wait_ge(S_["dve_ln"], l * PER["dve_ln"] + 1)
                product(halves(7)[:, 0], lambda k: mean_mat[:], lambda k: conv_sig[:, k], 2).then_inc(S_["pe_ln"], 1)
                pe.wait_ge(S_["act_gelu"], l * PER["act_gelu"] + 1)
                pe.wait_ge(S_["dve_z"], l * PER["dve_z"] + 2)
                w, = unit_at_once(n0, [(2, 512)])
                for b in range(2):
                    for a in range(2):
                        ins = product(halves(4 + b)[:, a], lambda k: w[:, k, (2 * b + a) * P:(2 * b + a + 1) * P],
                                      lambda k: ssm_g[:, k], 2)
                    ins.then_inc(S_["pe_glu"], 1)
                pe.wait_ge(S_["dve_att"], l * PER["dve_att"] + 8)
                pe.wait_ge(S_["act_pt"], l * PER["act_pt"] + 8)
                for i in range(4):
                    b0 = 3 * (i % 2)
                    wa, ws, wc = unit_at_once(n0 + 1 + i, [(4, 256), (2, 256), (2, 256)])
                    if i >= 2:
                        pe.wait_ge(S_["dve_merge"], l * PER["dve_merge"] + i - 1)
                    for b, (w, r, n) in enumerate(((wa, attT, 4), (ws, ssm_z, 2), (wc, conv_sig, 2))):
                        if i == 0 and b == 1:
                            pe.wait_ge(S_["dve_glu"], l * PER["dve_glu"] + 1)
                        if i == 0 and b == 2:
                            pe.wait_ge(S_["act_conv"], l * PER["act_conv"] + 2)
                        for a in range(2):
                            c = a * P
                            ins = product(halves(b0 + b)[:, a], lambda k: w[:, k, c:c + P], lambda k: r[:, k], n)
                        ins.then_inc(S_["pe_out"], 1)
                pe.wait_ge(S_["dve_merge"], l * PER["dve_merge"] + 3)
                for i in range(4):
                    w_hi, w_lo = split_unit(m0 + U_O + i, 2)
                    pe.wait_ge(S_["dve_merged"], l * PER["dve_merged"] + i + 1)
                    for k in range(2):
                        for n, b in enumerate((6, 7, 0, 1)):
                            a, h = n // 2, n % 2
                            tokens, c = slice(a * P, (a + 1) * P), slice(h * 512, (h + 1) * 512)
                            ins = split_product(bank[b][:, :], merged_hi[:, 2 * i + k, tokens],
                                                merged_lo[:, 2 * i + k, tokens], w_hi[:, k, c], w_lo[:, k, c],
                                                i + k == 0, i == 3 and k == 1)
                    ins.then_inc(g["trunk_used"], 1)

                norm(2 * l + 1)

                if l == 0:
                    for n, (kind, q) in enumerate(dense):
                        m = split_at["dense"] + n
                        if kind != "down":
                            if q >= 2:
                                pe.wait_ge(g["ffn_act_silu" if kind == "gate" else "ffn_hidden"], q - 1)
                            feature_tiles((4 if kind == "gate" else 6) + q % 2, m, None if n else 1)
                            continue
                        pe.wait_ge(g["ffn_lo"], q + 1)
                        w_hi, w_lo = split_unit(m, 2)
                        for k in range(2):
                            for b in range(4):
                                c, h = slice(b // 2 * P, b // 2 * P + P), slice(b % 2 * 512, b % 2 * 512 + 512)
                                ins = split_product(bank[b][:, :], hidden_hi[:, q % 2, k, c], hidden_lo[:, q % 2, k, c],
                                                    w_hi[:, k, h], w_lo[:, k, h], q + k == 0,
                                                    q == N_PAIR - 1 and k == 1)
                        ins.then_inc(g["trunk_used"], 1)
                else:
                    pe.wait_ge(g["small_lo"], DEPTH + 1)
                    for k in range(KT):
                        pe.wait_ge(S_["dve_ht"], 3 * PER["dve_ht"] + k + 1)
                        ins = pe.matmul(bank[4][0:NE, 0:T], small_hi[:, k, 0:NE], hT_hi[:, k], start=(k == 0), stop=False)
                        if k == 0:
                            ins.then_inc(g["unit_used"], SPLIT_RING)
                        pe.matmul(bank[4][0:NE, 0:T], small_hi[:, k, 0:NE], hT_lo[:, k], start=False, stop=False)
                        ins = pe.matmul(bank[4][0:NE, 0:T], small_lo[:, k, 0:NE], hT_hi[:, k], start=False, stop=(k == KT - 1))
                    ins.then_inc(g["pe_router"], 1)
                    pe.wait_ge(g["router_read"], 1)
                    for a in range(TT):
                        ins = pe.transpose(bank[5][:, a * NE:(a + 1) * NE], logits_T[:, a * P:(a + 1) * P], ident[0:NE, 0:NE])
                    ins.then_inc(g["pe_router"], 1)
                    pe.wait_ge(g["router_read"], 2)
                    pe.wait_ge(g["dve_route"], 1)
                    pe.wait_ge(g["pool_route"], 2)
                    pe.matmul(bank[6][:, 0:NE], before, chosen[:, 0], start=True, stop=True).then_inc(g["pe_route"], 1)
                    pe.matmul(bank[7][:, 0:NE], ones_mat, chosen[:, 0], start=True, stop=False)
                    pe.matmul(bank[7][:, 0:NE], before, chosen[:, 1], start=False, stop=True).then_inc(g["pe_route"], 1)
                    product(bank[5][:, 0:NE], lambda k: ones_mat, lambda k: chosen[:, k], 2).then_inc(g["pe_route"], 1)

                    def gather(v):
                        pe.wait_ge(g["dve_pick"], v + 1)
                        for n, b in enumerate((7, 4)):
                            for k in range(4):
                                f0 = (4 * n + k) * P
                                ins = product(bank[b][:, k * P:(k + 1) * P], lambda a: hn[:, a, f0:f0 + P],
                                              lambda a: pick[:, a], TT)
                            ins.then_inc(g["pe_picked"], 1)

                    def expert(e, v, last=False):
                        def unit(n, k):
                            pe.wait_ge(g["split_lo"], v * NU + (n + 1 + UNIT_RING))
                            q = n % SPLIT_RING
                            return [u[:, q].rearrange("p (k n) -> p k n", k=k) for u in (unit_hi, unit_lo)]

                        def turn(c):
                            pe.wait_ge(g["ffn_hidden"], v * E_CH + (N_PAIR + c + 1))
                            if c:
                                pe.wait_ge(g["dve_turned"], v * E_CH + c)
                            for k in range(4):
                                ins = pe.transpose(bank[4][:, k * P:(k + 1) * P],
                                                   e_hidden[:, c % 2, k * P:(k + 1) * P], ident[:])
                            ins.then_inc(g["pe_e_turned"], 1)

                        pe.wait_ge(g["dve_picked_lo"], v * 2 + 2)
                        for n, (kind, c, h) in enumerate(units):
                            if kind == "down":
                                pe.wait_ge(g["dve_turned"], v * E_CH + (c + 1))
                                w_hi, w_lo = unit(n, 2)
                                for k in range(2):
                                    for b in range(2):
                                        cols_ = slice(b * 512, (b + 1) * 512)
                                        ins = split_product(bank[5 + b][:, :], turned_hi[:, c % 2, 2 * h + k],
                                                            turned_lo[:, c % 2, 2 * h + k], w_hi[:, k, cols_],
                                                            w_lo[:, k, cols_], c + h + k == 0,
                                                            c == E_CH - 1 and h + k == 2)
                            else:
                                b = c % 2 + (2 if kind == "up" else 0)
                                if h == 0 and c < 2:
                                    pe.wait_ge(g["acc_read"], v * 4 + (b + 1))
                                elif h == 0:
                                    pe.wait_ge(g["ffn_act_silu" if kind == "gate" else "ffn_hidden"],
                                               v * E_CH + (N_PAIR + c - 1))
                                w_hi, w_lo = unit(n, 4)
                                for k in range(4):
                                    ins = split_product(bank[b][:, :], picked_hi[:, 4 * h + k], picked_lo[:, 4 * h + k],
                                                        w_hi[:, k], w_lo[:, k], h + k == 0, h == 1 and k == 3)
                            ins.then_inc(g["unit_used"], 1)
                            if kind == "gate" and h and c:
                                turn(c - 1)
                            if kind == "up" and h and c == 3:
                                for a in range(TT):
                                    ins = pe.transpose(bank[7][:, a * P:(a + 1) * P], spread[:, a], ident[:])
                                ins.then_inc(g["pe_spread"], 1)
                            if n == unit_at["down", E_CH - 2, 1]:
                                turn(E_CH - 1)
                            if n == NU - 2:
                                pe.wait_ge(g["dve_spread"], v + 1)
                                if not last:
                                    gather(v + 1)
                        pe.wait_ge(g["act_e_out"], v * 2 + 2)
                        for n in range(4):
                            a, h = n // 2, n % 2
                            pe.matmul(bank[n][:, :], spreadT[:, a * P:(a + 1) * P], e_out[:, h * 512:(h + 1) * 512],
                                      start=True, stop=True).then_inc(g["pe_combined"], 1)

                    gather(0)
                    with pe.Fori(0, NE - 1) as e:
                        expert(e, e)
                    expert(NE - 1, NE - 1, last=True)
                    with pe.If(pe.value_load(crowded[0:1, 0:1], min_val=0, max_val=1) > 0):
                        gather(NE)
                        with pe.Fori(0, NE - 1) as e:
                            expert(e, e + NE)
                        expert(NE - 1, 2 * NE - 1, last=True)
                        pe.wait_ge(g["acc_read"], 4 + 8 * NE)


_INS = ["x", "g_mix", "w_in", "b_in", "ssm_a_re", "ssm_a_im", "ssm_log_dt", "ssm_b_re", "ssm_b_im", "ssm_c_re",
        "ssm_c_im", "ssm_d", "ssm_w_glu", "conv_w", "conv_b", "conv_ln_g", "conv_ln_b", "w_att_out", "w_ssm_out",
        "w_conv_out", "w_o", "g_ffn", "ffn_w_gate", "ffn_w_up", "ffn_w_down", "moe_w_router", "moe_b_router",
        "moe_w_gate", "moe_w_up", "moe_w_down", "g_final"]


def kernel(**inputs):
    import numpy as np
    import concourse.bacc as bacc
    from concourse.bass_utils import run_bass_kernel_spmd

    nc = bacc.Bacc("TRN2", target_bir_lowering=False, num_devices=1)
    arrays, t = {}, {}
    for name in _INS:
        a = np.ascontiguousarray(inputs[name])
        arrays[f"in_{name}"] = a
        t[name] = nc.dram_tensor(f"in_{name}", a.shape, mybir.dt.from_np(a.dtype), kind="ExternalInput").ap()
    shape = inputs["x"].shape
    out = nc.dram_tensor("out", shape, F32, kind="ExternalOutput").ap()
    hybrid_trunk(nc, t, out)
    return run_bass_kernel_spmd(nc, [arrays], core_ids=[0]).results[0]["out"]
```
